# Optimizing a Trainium2 kernel written in Bass

```python
import math
import jax, jax.numpy as jnp
from jax import lax
import numpy as np
import functools
import jax
import jax.numpy as jnp

D_MODEL = 2048
BATCH = 1
SEQ = 256
DEPTH = 2

CHUNK = 64
Q_BLOCK = 128
ROPE_THETA = 500000.0
NORM_EPS = 1e-6
NEG_INF = -1e30
PLE_DIM = 256
HEAD_DIM = 128

A_HEADS = 6
A_Q_RANK = 384
A_KV_RANK = 256
A_NOPE = 128
A_ROPE = 64
A_V = 128
A_WIDTH = A_HEADS * A_V
B_HEADS = 5
B_WIDTH = B_HEADS * HEAD_DIM
IDX_HEADS = 8
IDX_DIM = 64
TOPK_MAX = 256
C_HEADS = 5
C_QK = 64
C_V = 128
C_WIDTH = C_HEADS * C_V
D_MIX = A_WIDTH + B_WIDTH + C_WIDTH

IN_SPLITS = (A_Q_RANK, A_KV_RANK, A_ROPE, A_WIDTH,
             B_WIDTH, B_WIDTH, B_WIDTH, IDX_HEADS * IDX_DIM, IDX_DIM, IDX_HEADS, B_WIDTH,
             C_HEADS * 2 * C_QK, C_HEADS * 2 * C_QK, C_WIDTH, C_WIDTH)
D_IN = sum(IN_SPLITS)


def rms_norm(x, g):
    xf = x.astype(jnp.float32)
    y = xf * lax.rsqrt(jnp.mean(xf * xf, axis=-1, keepdims=True) + NORM_EPS)
    return (y * g.astype(jnp.float32)).astype(x.dtype)

def rope(x, pos, n_rot):
    half = n_rot // 2
    inv_freq = 1.0 / (ROPE_THETA ** (jnp.arange(half, dtype=jnp.float32) * (2.0 / n_rot)))
    ang = pos.astype(jnp.float32)[:, :, None] * inv_freq
    cos = jnp.cos(ang)[:, :, None, :]
    sin = jnp.sin(ang)[:, :, None, :]
    x1 = x[..., :half].astype(jnp.float32)
    x2 = x[..., half:n_rot].astype(jnp.float32)
    rot = jnp.concatenate([x1 * cos - x2 * sin, x2 * cos + x1 * sin], axis=-1).astype(x.dtype)
    return jnp.concatenate([rot, x[..., n_rot:]], axis=-1)

def split_cols(z, sizes):
    out, o = [], 0
    for sz in sizes:
        out.append(z[..., o:o + sz])
        o += sz
    return out

def to_blocks(a):
    b, s = a.shape[:2]
    return jnp.swapaxes(a.reshape(b, s // Q_BLOCK, Q_BLOCK, *a.shape[2:]), 0, 1)

def from_blocks(a):
    nb, b, qb = a.shape[:3]
    return jnp.swapaxes(a, 0, 1).reshape(b, nb * qb, *a.shape[3:])

def chunk_mask(blk, seq):
    q_pos = blk * Q_BLOCK + jnp.arange(Q_BLOCK)
    k_pos = jnp.arange(seq)
    return (k_pos // CHUNK)[None, :] <= (q_pos // CHUNK)[:, None]

def masked_softmax(scores, mask):
    return jax.nn.softmax(jnp.where(mask, scores.astype(jnp.float32), NEG_INF), axis=-1)

def mla_mixer(c_q, c_kv, k_rope, pos, q_norm_g, kv_norm_g, w_uq, w_ukv):
    b, s, _ = c_q.shape
    q = (rms_norm(c_q, q_norm_g) @ w_uq).reshape(b, s, A_HEADS, A_NOPE + A_ROPE)
    q = jnp.concatenate([q[..., :A_NOPE], rope(q[..., A_NOPE:], pos, A_ROPE)], axis=-1)
    kv = (rms_norm(c_kv, kv_norm_g) @ w_ukv).reshape(b, s, A_HEADS, A_NOPE + A_V)
    k_pe = rope(k_rope[:, :, None, :], pos, A_ROPE)
    k = jnp.concatenate([kv[..., :A_NOPE], jnp.broadcast_to(k_pe, (b, s, A_HEADS, A_ROPE))], axis=-1)
    v = kv[..., A_NOPE:]
    scale = (A_NOPE + A_ROPE) ** -0.5

    def block(args):
        blk, qb = args
        sc = jnp.einsum('bqhd,bkhd->bhqk', qb, k) * scale
        pr = masked_softmax(sc, chunk_mask(blk, s)).astype(v.dtype)
        return jnp.einsum('bhqk,bkhd->bqhd', pr, v)

    o = from_blocks(lax.map(block, (jnp.arange(s // Q_BLOCK), to_blocks(q))))
    return o.reshape(b, s, A_WIDTH)

def dsa_mixer(q, k, v, q_idx, k_idx, w_idx, pos):
    b, s, _ = q.shape
    q = rope(q.reshape(b, s, B_HEADS, HEAD_DIM), pos, HEAD_DIM // 4)
    k = rope(k.reshape(b, s, B_HEADS, HEAD_DIM), pos, HEAD_DIM // 4)
    v = v.reshape(b, s, B_HEADS, HEAD_DIM)
    qi = rope(q_idx.reshape(b, s, IDX_HEADS, IDX_DIM), pos, IDX_DIM // 4)
    ki = rope(k_idx[:, :, None, :], pos, IDX_DIM // 4)[:, :, 0, :]
    n_sel = min(TOPK_MAX, s // 4)
    scale = HEAD_DIM ** -0.5

    def block(args):
        blk, qb, qib, wb = args
        mask = chunk_mask(blk, s)
        rel = jax.nn.relu(jnp.einsum('bqhd,bkd->bqhk', qib, ki).astype(jnp.float32))
        score = jnp.einsum('bqhk,bqh->bqk', rel, wb.astype(jnp.float32))
        score = jnp.where(mask[None], score, NEG_INF)
        top_val, top_idx = lax.top_k(score, n_sel)
        valid = top_val > 0.5 * NEG_INF
        kg = jax.vmap(lambda kk, ii: kk[ii])(k, top_idx)
        vg = jax.vmap(lambda vv, ii: vv[ii])(v, top_idx)
        sc = jnp.einsum('bqhd,bqkhd->bhqk', qb, kg) * scale
        pr = masked_softmax(sc, valid[:, None]).astype(v.dtype)
        return jnp.einsum('bhqk,bqkhd->bqhd', pr, vg)

    o = from_blocks(lax.map(block, (jnp.arange(s // Q_BLOCK), to_blocks(q), to_blocks(qi), to_blocks(w_idx))))
    return o.reshape(b, s, B_WIDTH)

def diff_mixer(q, k, v, pos, lam, lam_init, subln_g):
    b, s, _ = q.shape
    q = rope(q.reshape(b, s, C_HEADS * 2, C_QK), pos, C_QK // 4).reshape(b, s, C_HEADS, 2, C_QK)
    k = rope(k.reshape(b, s, C_HEADS * 2, C_QK), pos, C_QK // 4).reshape(b, s, C_HEADS, 2, C_QK)
    v = v.reshape(b, s, C_HEADS, C_V)
    k1, k2 = k[..., 0, :], k[..., 1, :]
    scale = C_QK ** -0.5

    def block(args):
        blk, qb = args
        mask = chunk_mask(blk, s)
        a1 = masked_softmax(jnp.einsum('bqhd,bkhd->bhqk', qb[..., 0, :], k1) * scale, mask)
        a2 = masked_softmax(jnp.einsum('bqhd,bkhd->bhqk', qb[..., 1, :], k2) * scale, mask)
        pr = (a1 - lam * a2).astype(v.dtype)
        return jnp.einsum('bhqk,bkhd->bqhd', pr, v)

    o = from_blocks(lax.map(block, (jnp.arange(s // Q_BLOCK), to_blocks(q))))
    o = rms_norm(o, subln_g) * (1.0 - lam_init)
    return o.reshape(b, s, C_WIDTH)

def first_inputs(seed: int = 0) -> dict:
    key = jax.random.key(seed)
    ks = jax.random.split(key, 20)
    f32 = jnp.float32
    nrm = lambda k, shape, sc: jax.random.normal(k, shape, f32) * sc
    x = nrm(ks[0], (BATCH, SEQ, D_MODEL), 1.0)
    p = nrm(ks[1], (DEPTH, BATCH, SEQ, PLE_DIM), 1.0)
    start = jax.random.randint(ks[2], (BATCH, 1), 0, 64, dtype=jnp.int32) * CHUNK
    positions = (start + jnp.arange(SEQ, dtype=jnp.int32)[None, :]).astype(jnp.int32)
    return {
        "x": x,
        "p": p,
        "positions": positions,
        "w_in": nrm(ks[3], (DEPTH, D_MODEL, D_IN), D_MODEL ** -0.5),
        "w_uq": nrm(ks[4], (DEPTH, A_Q_RANK, A_HEADS * (A_NOPE + A_ROPE)), A_Q_RANK ** -0.5),
        "w_ukv": nrm(ks[5], (DEPTH, A_KV_RANK, A_HEADS * (A_NOPE + A_V)), A_KV_RANK ** -0.5),
        "w_o": nrm(ks[6], (DEPTH, D_MIX, D_MODEL), D_MIX ** -0.5),
        "norm_g": 1.0 + nrm(ks[7], (DEPTH, D_MODEL), 0.02),
        "q_norm_g": 1.0 + nrm(ks[8], (DEPTH, A_Q_RANK), 0.02),
        "kv_norm_g": 1.0 + nrm(ks[9], (DEPTH, A_KV_RANK), 0.02),
        "lam_q1": nrm(ks[10], (DEPTH, C_QK), 0.1),
        "lam_k1": nrm(ks[11], (DEPTH, C_QK), 0.1),
        "lam_q2": nrm(ks[12], (DEPTH, C_QK), 0.1),
        "lam_k2": nrm(ks[13], (DEPTH, C_QK), 0.1),
        "subln_g": 1.0 + nrm(ks[14], (DEPTH, C_V), 0.02),
        "w_ple": nrm(ks[15], (DEPTH, PLE_DIM, D_MODEL), PLE_DIM ** -0.5),
        "w_pg": nrm(ks[16], (DEPTH, D_MODEL, D_MODEL), D_MODEL ** -0.5),
        "final_g": 1.0 + nrm(ks[17], (D_MODEL,), 0.02),
    }

def first_block(x, p, positions, w_in, w_uq, w_ukv, w_o, norm_g, q_norm_g, kv_norm_g,
              lam_q1, lam_k1, lam_q2, lam_k2, subln_g, w_ple, w_pg, final_g):
    h = x
    f32 = jnp.float32
    for i in range(DEPTH):
        u = rms_norm(h, norm_g[i])
        z = u @ w_in[i]
        (c_q, c_kv, k_rope, g_a,
         q_b, k_b, v_b, q_idx, k_idx, w_idx, g_b,
         q_c, k_c, v_c, g_c) = split_cols(z, IN_SPLITS)
        o_a = mla_mixer(c_q, c_kv, k_rope, positions, q_norm_g[i], kv_norm_g[i], w_uq[i], w_ukv[i])
        o_b = dsa_mixer(q_b, k_b, v_b, q_idx, k_idx, w_idx, positions)
        lam_init = 0.8 - 0.6 * math.exp(-0.3 * i)
        lam = (jnp.exp(jnp.sum(lam_q1[i].astype(f32) * lam_k1[i].astype(f32)))
               - jnp.exp(jnp.sum(lam_q2[i].astype(f32) * lam_k2[i].astype(f32))) + lam_init)
        o_c = diff_mixer(q_c, k_c, v_c, positions, lam, lam_init, subln_g[i])
        mixed = jnp.concatenate([o_a * jax.nn.silu(g_a),
                                 o_b * jax.nn.silu(g_b),
                                 o_c * jax.nn.silu(g_c)], axis=-1)
        h = h + mixed @ w_o[i]
        h = h + (p[i] @ w_ple[i]) * jax.nn.sigmoid(h @ w_pg[i])
    return rms_norm(h, final_g)


DEPTH_2 = 1

CTX_LEN = 256
GRID_W = 64
CHUNK_2 = 128
EPS = 1e-6
ADA_CHUNKS = 6

R_HEADS = 8
R_DK = 64
R_DV = 128
R_QK = R_HEADS * R_DK
R_WIDTH = R_HEADS * R_DV
ROPE_BASE = 10000.0

M_HEADS = 4
M_DK = 128
M_DV = 256
M_QK = M_HEADS * M_DK
M_WIDTH = M_HEADS * M_DV
M_CONV = 3
M_N_GATES = 2 * 2 * M_HEADS

P_HEADS = 8
P_NKEYS = 128
P_EXPERTS = P_NKEYS * P_NKEYS
P_DQ = 256
P_TOPK = 16
P_BLOCK = 128

IN_SPLITS_2 = (R_QK, R_QK, R_WIDTH, R_WIDTH, M_QK, M_QK, M_WIDTH, M_WIDTH, M_N_GATES, D_MODEL, D_MODEL)
IN_COLS = 2 * R_QK + 2 * R_WIDTH + 2 * M_QK + 2 * M_WIDTH + M_N_GATES + 2 * D_MODEL


def _split_in(p):
    out, off = [], 0
    for size in IN_SPLITS_2:
        out.append(p[..., off:off + size])
        off += size
    return out

def _rmsnorm(x, g):
    xf = x.astype(jnp.float32)
    y = xf * lax.rsqrt(jnp.mean(xf * xf, axis=-1, keepdims=True) + EPS)
    return (y * g.astype(jnp.float32)).astype(x.dtype)

def _modulate(x, g, shift, scale):
    return _rmsnorm(x, g) * (1.0 + scale) + shift

def _head_norm(y):
    yc = y - jnp.mean(y, axis=-1, keepdims=True)
    return yc * lax.rsqrt(jnp.mean(yc * yc, axis=-1, keepdims=True) + EPS)

def _rotary_2d(t, row, col):
    half = t.shape[-1] // 2
    n_ax = half // 2
    freq = ROPE_BASE ** (-jnp.arange(n_ax, dtype=jnp.float32) / n_ax)
    ang = jnp.concatenate([row[:, None] * freq, col[:, None] * freq], axis=-1)
    cos = jnp.cos(ang)[None, :, None, :]
    sin = jnp.sin(ang)[None, :, None, :]
    t1, t2 = t[..., :half], t[..., half:]
    return jnp.concatenate([t1 * cos - t2 * sin, t2 * cos + t1 * sin], axis=-1)

def _to_chunks(t):
    bsz, length = t.shape[:2]
    t = t.reshape((bsz, length // CHUNK_2, CHUNK_2) + t.shape[2:])
    return jnp.swapaxes(jnp.moveaxis(t, 1, 0), 2, 3)

def _from_chunks(t):
    t = jnp.moveaxis(jnp.swapaxes(t, 2, 3), 0, 1)
    return t.reshape((t.shape[0], t.shape[1] * t.shape[2]) + t.shape[3:])

def _flip(ts):
    return tuple(jnp.flip(t, axis=1) for t in ts)

def _bidirectional(scan_f, scan_b, lat_f, lat_b, ctx_f, ctx_b, init, need_ctx):
    st_f, yc_f = scan_f(ctx_f, init, need_ctx)
    st_b, yc_b = scan_b(_flip(ctx_b), init, need_ctx)
    _, yl_f = scan_f(lat_f, st_f, True)
    _, yl_b = scan_b(_flip(lat_b), st_b, True)
    y_lat = yl_f + jnp.flip(yl_b, axis=1)
    y_ctx = yc_f + jnp.flip(yc_b, axis=1) if need_ctx else None
    return y_lat, y_ctx

def _retention_scan(seqs, s0, with_out, log_gamma):
    q, k, v = (_to_chunks(t) for t in seqs)
    pos = jnp.arange(CHUNK_2, dtype=jnp.float32)
    lg = log_gamma[:, None]
    rel = pos[:, None] - pos[None, :]
    intra = jnp.where(rel >= 0, jnp.exp(lg[:, :, None] * jnp.maximum(rel, 0.0)), 0.0)
    q_dec = jnp.exp(lg * (pos + 1.0))[None, :, :, None]
    k_dec = jnp.exp(lg * (CHUNK_2 - 1.0 - pos))[None, :, :, None]
    c_dec = jnp.exp(lg * CHUNK_2)[None, :, :, None]

    def step(s, inp):
        qc, kc, vc = inp
        s_new = c_dec * s + jnp.einsum('bhcd,bhce->bhde', kc * k_dec, vc)
        if not with_out:
            return s_new, None
        att = jnp.einsum('bhcd,bhsd->bhcs', qc, kc) * intra
        y = jnp.einsum('bhcs,bhse->bhce', att, vc) + jnp.einsum('bhcd,bhde->bhce', qc * q_dec, s)
        return s_new, y

    s_fin, ys = lax.scan(step, s0, (q, k, v))
    return s_fin, (_from_chunks(ys) if with_out else None)

def _mlstm_scan(seqs, state0, with_out):
    q, k, v, ig, lf = (_to_chunks(t) for t in seqs)
    tri = jnp.tril(jnp.ones((CHUNK_2, CHUNK_2), dtype=bool))

    def step(carry, inp):
        c_prev, n_prev, m_prev = carry
        qc, kc, vc, ic, fc = inp
        b = jnp.cumsum(fc, axis=-1)
        b_end = b[..., -1]
        w_log = b_end[..., None] - b + ic
        a_end = b_end + m_prev
        m_new = jnp.maximum(a_end, jnp.max(w_log, axis=-1))
        p = jnp.exp(a_end - m_new)
        kw = kc * jnp.exp(w_log - m_new[..., None])[..., None]
        c_new = p[..., None, None] * c_prev + jnp.einsum('bhcd,bhce->bhde', kw, vc)
        n_new = p[..., None] * n_prev + jnp.sum(kw, axis=2)
        new = (c_new, n_new, m_new)
        if not with_out:
            return new, None
        a = b + m_prev[..., None]
        d_log = jnp.where(tri, b[..., :, None] - b[..., None, :] + ic[..., None, :], -jnp.inf)
        m_t = jnp.maximum(a, jnp.max(d_log, axis=-1))
        att = jnp.einsum('bhcd,bhsd->bhcs', qc, kc) * jnp.exp(d_log - m_t[..., None])
        inter = jnp.exp(a - m_t)[..., None]
        num = jnp.einsum('bhcs,bhse->bhce', att, vc) + inter * jnp.einsum('bhcd,bhde->bhce', qc, c_prev)
        den = jnp.sum(att, axis=-1, keepdims=True) + inter * jnp.einsum('bhcd,bhd->bhc', qc, n_prev)[..., None]
        h = num / jnp.maximum(jnp.abs(den), jnp.exp(-m_t)[..., None])
        return new, h

    st, hs = lax.scan(step, state0, (q, k, v, ig, lf))
    return st, (_from_chunks(hs) if with_out else None)

def _retention_inputs(q, k, v, row, col):
    bsz, length = q.shape[:2]
    qh = q.reshape(bsz, length, R_HEADS, R_DK).astype(jnp.float32)
    kh = k.reshape(bsz, length, R_HEADS, R_DK).astype(jnp.float32)
    if row is not None:
        qh = _rotary_2d(qh, row, col)
        kh = _rotary_2d(kh, row, col)
    vh = v.reshape(bsz, length, R_HEADS, R_DV).astype(jnp.float32)
    return (qh, kh * (R_DK ** -0.5), vh)

def _dwconv_centred(x, w):
    ksz, ch = w.shape
    return lax.conv_general_dilated(x, w[:, None, :].astype(x.dtype), window_strides=(1,),
                                    padding=[(ksz // 2, ksz - 1 - ksz // 2)],
                                    dimension_numbers=('NWC', 'WIO', 'NWC'), feature_group_count=ch)

def _mlstm_inputs(q, k, v, gates, conv_w, gate_bias):
    bsz, length = q.shape[:2]
    qk = jax.nn.silu(_dwconv_centred(jnp.concatenate([q, k], axis=-1), conv_w))
    qh = qk[..., :M_QK].reshape(bsz, length, M_HEADS, M_DK).astype(jnp.float32)
    kh = qk[..., M_QK:].reshape(bsz, length, M_HEADS, M_DK).astype(jnp.float32) * (M_DK ** -0.5)
    vh = v.reshape(bsz, length, M_HEADS, M_DV).astype(jnp.float32)
    g = gates.astype(jnp.float32).reshape(bsz, length, 2, 2, M_HEADS) + gate_bias.astype(jnp.float32)
    fwd = (qh, kh, vh, g[:, :, 0, 0], jax.nn.log_sigmoid(g[:, :, 0, 1]))
    bwd = (qh, kh, vh, g[:, :, 1, 0], jax.nn.log_sigmoid(g[:, :, 1, 1]))
    return fwd, bwd

def _retention_out(y, gate):
    bsz, length = y.shape[:2]
    return _head_norm(y).reshape(bsz, length, R_WIDTH).astype(gate.dtype) * jax.nn.silu(gate)

def _mlstm_out(h, o):
    bsz, length = h.shape[:2]
    return _head_norm(h).reshape(bsz, length, M_WIDTH).astype(o.dtype) * jax.nn.sigmoid(o)

def _merge(yr, ym, g_r, g_m, w_ret_out, w_mlstm_out, w_out):
    merged = jax.nn.sigmoid(g_r) * (yr @ w_ret_out) + jax.nn.sigmoid(g_m) * (ym @ w_mlstm_out)
    return merged @ w_out

def _peer(h, w_query, sub_keys, expert_down, expert_up):
    bsz, length, dm = h.shape
    tokens = h.reshape(-1, P_BLOCK, dm)

    def block(tb):
        qh = (tb @ w_query).reshape(P_BLOCK, P_HEADS, 2, P_DQ // 2)
        s = jnp.einsum('thpd,hpkd->thpk', qh, sub_keys).astype(jnp.float32)
        sv, si = lax.top_k(s, P_TOPK)
        cand_s = (sv[:, :, 0, :, None] + sv[:, :, 1, None, :]).reshape(P_BLOCK, P_HEADS, P_TOPK * P_TOPK)
        cand_i = (si[:, :, 0, :, None] * P_NKEYS + si[:, :, 1, None, :]).reshape(P_BLOCK, P_HEADS, P_TOPK * P_TOPK)
        best_s, best_j = lax.top_k(cand_s, P_TOPK)
        eid = jnp.take_along_axis(cand_i, best_j, axis=-1)
        g = jax.nn.softmax(best_s, axis=-1)
        act = jax.nn.gelu(jnp.einsum('thkd,td->thk', expert_down[eid], tb).astype(jnp.float32), approximate=False)
        return jnp.einsum('thk,thkd->td', (g * act).astype(tb.dtype), expert_up[eid])

    return lax.map(block, tokens).reshape(bsz, length, dm)

def _layer(x, ctx, c, c_ctx, row, col, w_ada, b_ada, norm1_g, w_in, ret_decay, m_conv, m_gate_bias,
           w_ret_out, w_mlstm_out, w_out, norm2_g, peer_query, peer_keys, peer_down, peer_up, update_ctx):
    f32 = jnp.float32
    bsz = x.shape[0]
    sh1, sc1, gt1, sh2, sc2, gt2 = jnp.split((jax.nn.silu(c) @ w_ada + b_ada)[:, None, :], ADA_CHUNKS, axis=-1)
    csh1, csc1, cgt1, csh2, csc2, cgt2 = jnp.split(jax.nn.silu(c_ctx) @ w_ada + b_ada, ADA_CHUNKS, axis=-1)
    rq, rk, rv, rg, mq, mk, mv, mo, mg, gr, gm = _split_in(_modulate(x, norm1_g, sh1, sc1) @ w_in)
    crq, crk, crv, crg, cmq, cmk, cmv, cmo, cmg, cgr, cgm = _split_in(_modulate(ctx, norm1_g, csh1, csc1) @ w_in)

    log_gamma = jax.nn.log_sigmoid(ret_decay.astype(f32))
    r_lat = _retention_inputs(rq, rk, rv, row, col)
    r_ctx = _retention_inputs(crq, crk, crv, None, None)
    s0 = jnp.zeros((bsz, R_HEADS, R_DK, R_DV), f32)
    yr, yr_c = _bidirectional(functools.partial(_retention_scan, log_gamma=log_gamma[0]),
                              functools.partial(_retention_scan, log_gamma=log_gamma[1]),
                              r_lat, r_lat, r_ctx, r_ctx, s0, update_ctx)

    m_lat_f, m_lat_b = _mlstm_inputs(mq, mk, mv, mg, m_conv, m_gate_bias)
    m_ctx_f, m_ctx_b = _mlstm_inputs(cmq, cmk, cmv, cmg, m_conv, m_gate_bias)
    m0 = (jnp.zeros((bsz, M_HEADS, M_DK, M_DV), f32), jnp.zeros((bsz, M_HEADS, M_DK), f32),
          jnp.zeros((bsz, M_HEADS), f32))
    ym, ym_c = _bidirectional(_mlstm_scan, _mlstm_scan, m_lat_f, m_lat_b, m_ctx_f, m_ctx_b, m0, update_ctx)

    x = x + gt1 * _merge(_retention_out(yr, rg), _mlstm_out(ym, mo), gr, gm, w_ret_out, w_mlstm_out, w_out)
    x = x + gt2 * _peer(_modulate(x, norm2_g, sh2, sc2), peer_query, peer_keys, peer_down, peer_up)
    if update_ctx:
        ctx = ctx + cgt1 * _merge(_retention_out(yr_c, crg), _mlstm_out(ym_c, cmo), cgr, cgm,
                                  w_ret_out, w_mlstm_out, w_out)
        ctx = ctx + cgt2 * _peer(_modulate(ctx, norm2_g, csh2, csc2), peer_query, peer_keys, peer_down, peer_up)
    return x, ctx

def second_inputs(seed: int = 0) -> dict:
    key = jax.random.key(seed)
    ks = jax.random.split(key, 24)
    f32 = jnp.float32

    def nrm(k, shape, scale):
        return jax.random.normal(k, shape, f32) * scale

    x = nrm(ks[0], (BATCH, SEQ, D_MODEL), 1.0)
    c = nrm(ks[1], (BATCH, D_MODEL), 1.0)
    ctx = nrm(ks[2], (BATCH, CTX_LEN, D_MODEL), 1.0)
    c_ctx = nrm(ks[3], (D_MODEL,), 1.0)
    w_ada = nrm(ks[4], (DEPTH_2, D_MODEL, ADA_CHUNKS * D_MODEL), D_MODEL ** -0.5)
    b_ada = nrm(ks[5], (DEPTH_2, ADA_CHUNKS * D_MODEL), 0.02)
    norm1_g = 1.0 + nrm(ks[6], (DEPTH_2, D_MODEL), 0.02)
    w_in = nrm(ks[7], (DEPTH_2, D_MODEL, IN_COLS), D_MODEL ** -0.5)
    decay_logit = jnp.log(2.0 ** (5.0 + jnp.arange(R_HEADS, dtype=f32)) - 1.0)
    ret_decay = decay_logit[None, None, :] + nrm(ks[8], (DEPTH_2, 2, R_HEADS), 0.05)
    m_conv = nrm(ks[9], (DEPTH_2, M_CONV, 2 * M_QK), M_CONV ** -0.5)
    gate_base = jnp.stack([jnp.zeros((M_HEADS,), f32), jnp.linspace(3.0, 6.0, M_HEADS, dtype=f32)])
    m_gate_bias = gate_base[None, None] + nrm(ks[10], (DEPTH_2, 2, 2, M_HEADS), 0.1)
    w_ret_out = nrm(ks[11], (DEPTH_2, R_WIDTH, D_MODEL), R_WIDTH ** -0.5)
    w_mlstm_out = nrm(ks[12], (DEPTH_2, M_WIDTH, D_MODEL), M_WIDTH ** -0.5)
    w_out = nrm(ks[13], (DEPTH_2, D_MODEL, D_MODEL), D_MODEL ** -0.5)
    norm2_g = 1.0 + nrm(ks[14], (DEPTH_2, D_MODEL), 0.02)
    peer_query = nrm(ks[15], (DEPTH_2, D_MODEL, P_HEADS * P_DQ), D_MODEL ** -0.5)
    peer_keys = nrm(ks[16], (DEPTH_2, P_HEADS, 2, P_NKEYS, P_DQ // 2), (P_DQ // 2) ** -0.5)
    peer_down = nrm(ks[17], (DEPTH_2, P_EXPERTS, D_MODEL), D_MODEL ** -0.5)
    peer_up = nrm(ks[18], (DEPTH_2, P_EXPERTS, D_MODEL), P_HEADS ** -0.5)
    final_g = 1.0 + nrm(ks[19], (D_MODEL,), 0.02)
    return {'x': x, 'c': c, 'ctx': ctx, 'c_ctx': c_ctx, 'w_ada': w_ada, 'b_ada': b_ada,
            'norm1_g': norm1_g, 'w_in': w_in, 'ret_decay': ret_decay, 'm_conv': m_conv,
            'm_gate_bias': m_gate_bias, 'w_ret_out': w_ret_out, 'w_mlstm_out': w_mlstm_out,
            'w_out': w_out, 'norm2_g': norm2_g, 'peer_query': peer_query, 'peer_keys': peer_keys,
            'peer_down': peer_down, 'peer_up': peer_up, 'final_g': final_g}

def second_block(x, c, ctx, c_ctx, w_ada, b_ada, norm1_g, w_in, ret_decay, m_conv, m_gate_bias,
              w_ret_out, w_mlstm_out, w_out, norm2_g, peer_query, peer_keys, peer_down, peer_up, final_g):
    length = x.shape[1]
    ROWS = length // GRID_W
    row = jnp.repeat(jnp.arange(ROWS, dtype=jnp.float32), GRID_W)
    col = jnp.tile(jnp.arange(GRID_W, dtype=jnp.float32), ROWS)
    for layer in range(DEPTH_2):
        x, ctx = _layer(x, ctx, c, c_ctx, row, col, w_ada[layer], b_ada[layer], norm1_g[layer], w_in[layer],
                        ret_decay[layer], m_conv[layer], m_gate_bias[layer], w_ret_out[layer],
                        w_mlstm_out[layer], w_out[layer], norm2_g[layer], peer_query[layer],
                        peer_keys[layer], peer_down[layer], peer_up[layer], update_ctx=layer < DEPTH_2 - 1)
    return _rmsnorm(x, final_g)


def setup_inputs(seed=0):
    out = dict(first_inputs(seed))
    for name, value in second_inputs(seed + 1).items():
        if name != "x":
            out[name + "_2"] = value
    return out


def reference(
    x, p, positions, w_in, w_uq, w_ukv, w_o, norm_g, q_norm_g, kv_norm_g, lam_q1, lam_k1,
    lam_q2, lam_k2, subln_g, w_ple, w_pg, final_g, c_2, ctx_2, c_ctx_2, w_ada_2, b_ada_2,
    norm1_g_2, w_in_2, ret_decay_2, m_conv_2, m_gate_bias_2, w_ret_out_2, w_mlstm_out_2,
    w_out_2, norm2_g_2, peer_query_2, peer_keys_2, peer_down_2, peer_up_2, final_g_2,
):
    x = first_block(
        x, p, positions, w_in, w_uq, w_ukv, w_o, norm_g, q_norm_g, kv_norm_g, lam_q1, lam_k1,
        lam_q2, lam_k2, subln_g, w_ple, w_pg, final_g,
    )
    return second_block(
        x, c_2, ctx_2, c_ctx_2, w_ada_2, b_ada_2, norm1_g_2, w_in_2, ret_decay_2, m_conv_2,
        m_gate_bias_2, w_ret_out_2, w_mlstm_out_2, w_out_2, norm2_g_2, peer_query_2,
        peer_keys_2, peer_down_2, peer_up_2, final_g_2,
    )


_drawn_inputs = setup_inputs


def setup_inputs(seed=0):
    import zlib

    import numpy as np

    out = dict(_drawn_inputs(seed))
    spreads = {}
    factors = {'q_norm_g': 8.0,
     'kv_norm_g': 8.0,
     'lam_k1': 3.21,
     'subln_g': 4.242,
     'norm1_g_2': 3.548,
     'norm2_g_2': 3.113,
     'final_g_2': 2.819}
    for name, (base, spread) in spreads.items():
        noise = np.random.default_rng([zlib.crc32(name.encode()), seed]).standard_normal(out[name].shape)
        drawn = base * np.exp(spread * noise) if base else spread * noise
        out[name] = jnp.asarray(drawn.astype(out[name].dtype))
    for name, factor in factors.items():
        out[name] = (out[name] * factor).astype(out[name].dtype)
    return out
```

```python
from contextlib import ExitStack

import numpy as np

import concourse.bass as bass
from concourse import mybir

F32 = mybir.dt.float32
I32 = mybir.dt.int32
U32 = mybir.dt.uint32
ALU = mybir.AluOpType
ACT = mybir.ActivationFunctionType
AX_X = mybir.AxisListType.X

P = 128
D = 2048
TOK = 256
NT = TOK // P
KT = D // P
PIECE_KT = 4
CHUNK = 512
PIECE = PIECE_KT * CHUNK
PIECES = 8
DEPTH = 2
EPS = 1e-6
NEG = -1e30
TWO_PI = 2 * np.pi

A_Q, A_KV, A_ROPE, A_HEADS, HD = 384, 256, 64, 6, 128
B_HEADS, C_HEADS, IDX_HEADS, IDX_DIM, C_QK = 5, 5, 8, 64, 64
CQ0 = 0
CKV0 = CQ0 + A_Q
KR0 = CKV0 + A_KV
GA0 = KR0 + A_ROPE
QB0 = GA0 + A_HEADS * HD
KB0 = QB0 + B_HEADS * HD
VB0 = KB0 + B_HEADS * HD
QI0 = VB0 + B_HEADS * HD
KI0 = QI0 + IDX_HEADS * IDX_DIM
GB0 = KI0 + IDX_DIM
QC0 = GB0 + B_HEADS * HD
KC0 = QC0 + C_HEADS * HD
VC0 = KC0 + C_HEADS * HD
GC0 = VC0 + C_HEADS * HD
WI0 = GC0 + C_HEADS * HD
ZW = WI0 + IDX_HEADS
N_SEL = 64
MIX0 = (GA0, GB0, GC0)
MIXW = (A_HEADS * HD, B_HEADS * HD, C_HEADS * HD)

R_HEADS, R_DK, R_DV = 8, 64, 128
M_HEADS, M_DK, M_DV = 4, 128, 256
P_HEADS, P_KEYS, P_TOPK = 8, 128, 16
GROUPS = 32

STREAM = []
for _l in range(DEPTH):
    STREAM += [(f"in{_l}", 7, 2), (f"out{_l}", 2, 2), (f"gate{_l}", 2, 2)]
STREAM += [("ada", 12, 1), ("kv", 2, 4), ("mvmk", 1, 4), ("mqrq", 1, 4), ("rgmo", 2, 2), ("merge", 6, 0),
           ("out2", 2, 2), ("query", 2, 4), ("experts", GROUPS, 0)]
PAIR0, EVAC0, _pair, _evac = {}, {}, 0, 0
for _n, _p, _e in STREAM:
    PAIR0[_n], EVAC0[_n] = _pair, _evac
    _pair += _p
    _evac += _p * _e
N_PAIRS = _pair

C_NORM = 0
C_QN = C_NORM + DEPTH * KT
C_KVN = C_QN + DEPTH * 3
C_N1 = C_KVN + DEPTH * 2
C_N2 = C_N1 + KT
C_CONV = C_N2 + KT
C_SILU = C_CONV + 3 * 8
NCOLS = C_SILU + 2 * KT
B_SUB = 0
B_MGB = B_SUB + DEPTH * HD
B_RDEC = B_MGB + 16
NBC = B_RDEC + 16


def build_program(nc, t, stop=99):
    ctx = ExitStack()
    with ctx:
        def sb(name, shape, dt=F32):
            return ctx.enter_context(nc.sbuf_tensor(name, shape, dt))

        def sem(name):
            return ctx.enter_context(nc.semaphore(name))

        ring = sb("ring", [P, PIECES, PIECE])
        h = sb("h", [P, NT * D])
        act = sb("act", [P, 4096 + 6528])
        z = sb("z", [P, NT * ZW])
        r2 = sb("r2", [P, 5120])
        ident = sb("ident", [P, P])
        iota = sb("iota", [P, P])
        mask = sb("mask", [P, P + TOK])
        trig = sb("trig", [P, 2, NT, 32])
        cols = sb("cols", [P, NCOLS])
        bc = sb("bc", [P, NBC])
        wsmall = sb("wsmall", [P, 512])
        st = sb("st", [P, 128])
        rs = sb("rs", [P, 96])
        sti = sb("sti", [P, 2], I32)
        ones = sb("ones", [P, P])
        mcols = sb("mcols", [P, 12, M_HEADS])
        ps = ctx.enter_context(nc.psum_tensor("ps", [P, 8, 512], F32))

        xT = act[:, 0:KT * TOK].rearrange("p (k n) -> p k n", k=KT)
        W0 = KT * TOK
        wtail = wsmall[:, 0:256].rearrange("p (l k n) -> p l k n", l=DEPTH, k=KT)
        wgates = wsmall[:, 256:512].rearrange("p (k n) -> p k n", k=KT)
        zt = z[:, :].rearrange("p (t n) -> p t n", t=NT)
        ht = h[:, :].rearrange("p (t n) -> p t n", t=NT)

        piece_full = [sem(f"piece_full{j}") for j in range(PIECES)]
        piece_used = [sem(f"piece_used{j}") for j in range(PIECES)]
        evac = [sem(f"evac{i}") for i in range(2)]
        stage_done = {e: sem(f"stage_done_{e}") for e in ("pe", "act", "dve", "pool")}
        pe_full = sem("pe_full")
        dve_step = sem("dve_step")
        act_step = sem("act_step")
        pool_step = sem("pool_step")
        rms_sums = sem("rms_sums")
        rms_inv = sem("rms_inv")
        rms_root = sem("rms_root")
        att_scores = sem("att_scores")
        att_logits = sem("att_logits")
        att_probs = sem("att_probs")
        att_mixed = sem("att_mixed")
        att_turned = sem("att_turned")
        att_pT = sem("att_pT")
        att_out = sem("att_out")
        att_done = sem("att_done")
        rel_done = sem("rel_done")
        gate_sig = sem("gate_sig")
        gate_used = sem("gate_used")
        consts = sem("consts")
        consts_p = sem("consts_p")
        aux = sem("aux")
        stored = sem("stored")
        made = sem("made")

        n_step = {"act": 0, "dve": 0, "pool": 0}
        step_sem = {"act": act_step, "dve": dve_step, "pool": pool_step}

        def chain(eng, who, ins):
            n_step[who] += 1
            ins.then_inc(step_sem[who], 1)
            eng.wait_ge(step_sem[who], n_step[who])

        ALL = ("pe", "act", "dve", "pool")

        def begin(eng, n, wait_for=ALL):
            if n >= 1:
                for who in wait_for:
                    eng.wait_ge(stage_done[who], n)

        def end(eng, who):
            eng.drain().then_inc(stage_done[who], 1)

        def stream_pe(pe, name, n_pairs, evacs, lhs, M=P, tiles=NT, first=0):
            base, e0 = PAIR0[name] + first, EVAC0[name] + first * evacs
            def body(i):
                for par in range(2):
                    if base > 0 or not isinstance(i, int) or i > 0:
                        pe.wait_ge(evac[par], i * evacs + e0)
                    for k in range(KT):
                        j = par * 4 + k // PIECE_KT
                        if k % PIECE_KT == 0:
                            pe.wait_ge(piece_full[j], i * 16 + 16 * (base + 1))
                        w = ring[:, j, (k % PIECE_KT) * CHUNK:(k % PIECE_KT + 1) * CHUNK]
                        for s in range(tiles):
                            mm = pe.matmul(ps[0:M, par * tiles + s, :], lhs(s, k), w,
                                           start=(k == 0), stop=(k == KT - 1))
                        if k % PIECE_KT == PIECE_KT - 1:
                            mm.then_inc(piece_used[j], 1)
            if base == 0 and e0 == 0:
                body(0)
                with pe.Fori(1, n_pairs) as i:
                    body(i)
            else:
                with pe.Fori(0, n_pairs) as i:
                    body(i)

        def turn_pe(pe, src, blocks=KT, tiles=NT):
            for j in range((blocks + 1) // 2):
                for k in range(2 * j, min(2 * j + 2, blocks)):
                    for s in range(tiles):
                        mm = pe.transpose(ps[:, j, (k % 2) * TOK + s * P:(k % 2) * TOK + (s + 1) * P], src(s, k), ident[:, :])
                mm.then_inc(pe_full, 1)

        def turn_evac(eng, who, base, dst, blocks=KT, scale=None, bias=None):
            for j in range((blocks + 1) // 2):
                if (j % 2 == 0) != (who == "dve"):
                    continue
                eng.wait_ge(pe_full, base + j + 1)
                for k in range(2 * j, min(2 * j + 2, blocks)):
                    src = ps[:, j, (k % 2) * TOK:(k % 2 + 1) * TOK]
                    s = None if scale is None else scale(k)
                    b = None if bias is None else bias(k)
                    if who == "dve":
                        if s is None:
                            eng.tensor_copy(dst(k), src)
                        elif b is None:
                            eng.tensor_scalar(dst(k), src, s, None, ALU.mult)
                        else:
                            eng.tensor_scalar(dst(k), src, s, b, ALU.mult, ALU.add)
                    elif s is None:
                        eng.copy(dst(k), src)
                    elif b is None:
                        eng.activation(dst(k), src, ACT.Copy, scale=s)
                    else:
                        eng.activation(dst(k), src, ACT.Identity, scale=s, bias=b)


        def rms_act(act_, k, sources, n, have_sums=False):
            if not have_sums:
                for c, (src, width, junk) in enumerate(sources):
                    last = act_.activation(junk, src, ACT.Square, scale=float(width) ** -0.5, accum_out=rs[:, c:c + 1])
                last.then_inc(rms_sums, 1)
            act_.wait_ge(rms_inv, k + 1)
            act_.activation(rs[:, 64:64 + n], rs[:, 32:32 + n], ACT.Sqrt).then_inc(rms_root, 1)

        def rms_dve(dve, k, n, sums=None):
            if sums is not None:
                dve.wait_ge(rms_sums, sums + 1)
            chain(dve, "dve", dve.tensor_scalar(rs[:, 32:32 + n], rs[:, 0:n], EPS, None, ALU.add))
            dve.reciprocal(rs[:, 32:32 + n], rs[:, 32:32 + n]).then_inc(rms_inv, 1)
            dve.wait_ge(rms_root, k + 1)

        def rope(dve, x1, x2, heads, half, tmp, out1=None, out2=None):
            cs, sn = (trig[:, f, :, 0:32:32 // half].unsqueeze(2).to_broadcast([P, NT, heads, half]) for f in range(2))
            a, b, c, d = (tmp(i, NT * heads * half).rearrange("p (t h d) -> p t h d", t=NT, h=heads) for i in range(4))
            dve.tensor_tensor(a, x1, cs, ALU.mult)
            dve.tensor_tensor(b, x2, sn, ALU.mult)
            dve.tensor_tensor(c, x2, cs, ALU.mult)
            chain(dve, "dve", dve.tensor_tensor(d, x1, sn, ALU.mult))
            dve.tensor_tensor(x1 if out1 is None else out1, a, b, ALU.subtract)
            chain(dve, "dve", dve.tensor_tensor(x2 if out2 is None else out2, c, d, ALU.add))

        def heads_of(col, heads, width, lo, hi):
            return zt[:, :, col:col + heads * width].rearrange("p t (h d) -> p t h d", h=heads)[:, :, :, lo:hi]

        va = r2[:, 0:1536].rearrange("p (t n) -> p t n", t=NT)
        qr = r2[:, 1536:2304].rearrange("p (t n) -> p t n", t=NT)
        qrT = r2[:, 2304:3072].rearrange("p (k n) -> p k n", k=3)
        kd = r2[:, 3072:3328].rearrange("p (t n) -> p t n", t=NT)
        kpeT = r2[:, 3328:3584]
        ckvT = r2[:, 3584:4096].rearrange("p (k n) -> p k n", k=2)
        qnT = act[:, 0:1536].rearrange("p (k n) -> p k n", k=6)
        knT = act[:, 1536:3072].rearrange("p (k n) -> p k n", k=6)
        cqT = act[:, 3072:3840].rearrange("p (k n) -> p k n", k=3)
        w_uq = act[:, W0:W0 + 3456].rearrange("p (k n) -> p k n", k=3)
        w_ukv = act[:, W0 + 3456:W0 + 6528].rearrange("p (k n) -> p k n", k=2)
        w_ple = act[:, W0:W0 + 4096].rearrange("p (k n) -> p k n", k=2)
        pT = act[:, W0 + 4096:W0 + 4608].rearrange("p (k n) -> p k n", k=2)
        hqT = act[:, 0:1280].rearrange("p (k n) -> p k n", k=5)
        hkT = act[:, 1280:2560].rearrange("p (k n) -> p k n", k=5)
        qiT = act[:, 2560:3584].rearrange("p (k n) -> p k n", k=4)
        kiT = act[:, 3584:3840]
        score = r2[:, 0:384]
        rel = r2[:, 384:3456].rearrange("p (h n) -> p h n", h=IDX_HEADS)
        kept = r2[:, 3456:3840]
        kid = r2[:, 3840:4096].rearrange("p (t n) -> p t n", t=NT)

        def keys(s):
            return (s + 1) * P, s * P

        def units(heads):
            return [(hd, s) for hd in range(heads) for s in range(NT)]

        UNITS = {"A": units(A_HEADS), "B": units(B_HEADS), "C": units(C_HEADS)}
        UNIT0 = {}
        nu = 0
        for l in range(DEPTH):
            for m in "ABC":
                UNIT0[m, l] = nu
                nu += len(UNITS[m])
        MIXED0 = {l: l * len(UNITS["C"]) for l in range(DEPTH)}
        SCALE = {"A": (A_ROPE + HD) ** -0.5, "B": HD ** -0.5, "C": C_QK ** -0.5}

        def scbuf(m, slot, sub=0):
            return r2[:, slot * 512 + sub * 256:][:, 0:256] if m == "C" else r2[:, 4096 + slot * 256:4352 + slot * 256]

        def prbuf(m, slot, sub=0):
            return r2[:, 1024 + slot * 512 + sub * 256:][:, 0:256] if m == "C" else r2[:, 4608 + slot * 256:4864 + slot * 256]

        def mixbuf(slot):
            return r2[:, 2048 + slot * 256:2304 + slot * 256]

        def pTbuf(m, slot):
            b = 2560 if m == "C" else 1536
            return r2[:, b + slot * 256:b + slot * 256 + 256]

        def values(m, j, hd):
            return va[:, j, hd * HD:(hd + 1) * HD] if m == "A" else zt[:, j, (VB0 if m == "B" else VC0) + hd * HD:][:, 0:HD]

        def attend_pe(pe, m, l):
            u0, us = UNIT0[m, l], UNITS[m]
            subs = 2 if m == "C" else 1

            def scores(u):
                hd, s = us[u]
                nk, _ = keys(s)
                if u >= 2:
                    pe.wait_ge(att_logits, u0 + u - 1)
                q0, q1 = s * P, (s + 1) * P
                b = u % 2
                if m == "A":
                    r = (hd % 2) * A_ROPE
                    pe.matmul(ps[:, b, 0:nk], qnT[:, hd, q0:q1], knT[:, hd, 0:nk], start=True, stop=False)
                    mm = pe.matmul(ps[:, b, 0:nk], qrT[r:r + A_ROPE, hd // 2, q0:q1], kpeT[r:r + A_ROPE, 0:nk],
                                   start=False, stop=True)
                elif m == "B":
                    mm = pe.matmul(ps[:, b, 0:nk], hqT[:, hd, q0:q1], hkT[:, hd, 0:nk], start=True, stop=True)
                else:
                    for c in range(2):
                        r = c * C_QK
                        mm = pe.matmul(ps[:, 2 * b + c, 0:nk], hqT[r:r + C_QK, hd, q0:q1], hkT[r:r + C_QK, hd, 0:nk],
                                       start=True, stop=True)
                mm.then_inc(att_scores, 1)

            def turn(u):
                _, s = us[u]
                if m == "C":
                    pe.wait_ge(att_mixed, MIXED0[l] + u + 1)
                else:
                    pe.wait_ge(att_probs, u0 + u + 1)
                if u >= 2:
                    pe.wait_ge(att_pT, u0 + u - 1)
                src = mixbuf(u % 2) if m == "C" else prbuf(m, u % 2)
                for j in range(s + 1):
                    mm = pe.transpose(ps[:, 4 + u % 2, j * P:(j + 1) * P], src[:, j * P:(j + 1) * P], ident[:, :])
                mm.then_inc(att_turned, 1)

            def out(u):
                hd, s = us[u]
                pe.wait_ge(att_pT, u0 + u + 1)
                if u >= 2:
                    pe.wait_ge(att_done, u0 + u - 1)
                for j in range(s + 1):
                    mm = pe.matmul(ps[:, 6 + u % 2, 0:HD], pTbuf(m, u % 2)[:, j * P:(j + 1) * P], values(m, j, hd),
                                   start=(j == 0), stop=(j == s))
                mm.then_inc(att_out, 1)

            n = len(us)
            for u in range(n + 2):
                if u < n:
                    scores(u)
                if 1 <= u <= n:
                    turn(u - 1)
                if u >= 2:
                    out(u - 2)

        def attend_act(act_, m, l):
            u0, us = UNIT0[m, l], UNITS[m]

            def probs(u):
                _, s = us[u]
                nk, _ = keys(s)
                act_.wait_ge(att_logits, u0 + u + 1)
                if u >= 2:
                    if m == "C":
                        act_.wait_ge(att_mixed, MIXED0[l] + u - 1)
                    else:
                        act_.wait_ge(att_turned, u0 + u - 1)
                for c in range(2 if m == "C" else 1):
                    k = 2 * (u % 2) + c
                    last = act_.activation(prbuf(m, u % 2, c)[:, 0:nk], scbuf(m, u % 2, c)[:, 0:nk], ACT.Exp,
                                           bias=st[:, 34 + k:35 + k], accum_out=st[:, 38 + k:39 + k])
                last.then_inc(att_probs, 1)

            def turned(u):
                _, s = us[u]
                act_.wait_ge(att_turned, u0 + u + 1)
                if u >= 2:
                    act_.wait_ge(att_out, u0 + u - 1)
                act_.copy(pTbuf(m, u % 2)[:, 0:(s + 1) * P], ps[:, 4 + u % 2, 0:(s + 1) * P]).then_inc(att_pT, 1)

            n = len(us)
            for u in range(n + 1):
                if u < n:
                    probs(u)
                if u >= 1:
                    turned(u - 1)

        def attend_dve(dve, m, l):
            u0, us = UNIT0[m, l], UNITS[m]
            subs = 2 if m == "C" else 1
            masks = score if m == "B" else mask

            def logits(u):
                _, s = us[u]
                nk, m0 = keys(s)
                dve.wait_ge(att_scores, u0 + u + 1)
                if u >= 2:
                    dve.wait_ge(att_probs, u0 + u - 1)
                for c in range(subs):
                    k = 2 * (u % 2) + c
                    bank = 2 * (u % 2) + c if m == "C" else u % 2
                    last = dve.tensor_tensor_reduce(scbuf(m, u % 2, c)[:, 0:nk], ps[:, bank, 0:nk], masks[:, m0:m0 + nk],
                                                    SCALE[m], NEG, ALU.add, ALU.max, st[:, 30 + k:31 + k])
                chain(dve, "dve", last)
                k = 2 * (u % 2)
                dve.tensor_scalar(st[:, 34 + k:34 + k + subs], st[:, 30 + k:30 + k + subs], -1.0, None, ALU.mult)\
                   .then_inc(att_logits, 1)

            def mix(u):
                _, s = us[u]
                nk, _ = keys(s)
                k = 2 * (u % 2)
                dve.wait_ge(att_probs, u0 + u + 1)
                chain(dve, "dve", dve.reciprocal(st[:, 42 + k:44 + k], st[:, 38 + k:40 + k]))
                if u >= 2:
                    dve.wait_ge(att_turned, u0 + u - 1)
                dve.tensor_scalar(prbuf(m, u % 2, 0)[:, 0:nk], prbuf(m, u % 2, 0)[:, 0:nk], st[:, 42 + k:43 + k], None, ALU.mult)
                chain(dve, "dve", dve.tensor_scalar(st[:, 43 + k:44 + k], st[:, 43 + k:44 + k], st[:, 60 + l:61 + l], None, ALU.mult))
                dve.scalar_tensor_tensor(mixbuf(u % 2)[:, 0:nk], prbuf(m, u % 2, 1)[:, 0:nk], st[:, 43 + k:44 + k],
                                         prbuf(m, u % 2, 0)[:, 0:nk], ALU.mult, ALU.add).then_inc(att_mixed, 1)

            def done(u):
                hd, s = us[u]
                dve.wait_ge(att_out, u0 + u + 1)
                src = ps[:, 6 + u % 2, 0:HD]
                if m == "C":
                    dve.tensor_copy(zt[:, s, QC0 + hd * HD:QC0 + (hd + 1) * HD], src).then_inc(att_done, 1)
                    return
                k = 2 * (u % 2)
                g = zt[:, s, (GA0 if m == "A" else GB0) + hd * HD:][:, 0:HD]
                dve.scalar_tensor_tensor(g, src, st[:, 46 + u % 2:47 + u % 2], g, ALU.mult, ALU.mult).then_inc(att_done, 1)

            def sums(u):
                dve.wait_ge(att_probs, u0 + u + 1)
                k = 2 * (u % 2)
                chain(dve, "dve", dve.reciprocal(st[:, 46 + u % 2:47 + u % 2], st[:, 38 + k:39 + k]))

            n = len(us)
            for u in range(n + 2):
                if u < n:
                    logits(u)
                if m == "C" and 1 <= u <= n:
                    mix(u - 1)
                if u >= 2:
                    done(u - 2)
                if m != "C" and 1 <= u <= n:
                    sums(u - 1)

        STAGES = [("setup", 0), ("angles", 0)]
        for l in range(DEPTH):
            STAGES += [("norm", l), ("turn_in", l), ("project", l), ("prep_a", l), ("turn_a", l), ("heads_a", l),
                       ("values_a", l), ("turn_ar", l), ("attend_a", l), ("prep_b", l), ("turn_b", l), ("turn_idx", l),
                       ("index", l), ("select", l), ("attend_b", l), ("prep_c", l), ("turn_c", l), ("attend_c", l),
                       ("norm_c", l), ("turn_mix", l), ("project_out", l), ("turn_h", l), ("embed", l), ("gate", l)]
        STAGES += [(name, 0) for name in (
            "final1", "silu_c", "ada", "ada_cols", "mod_cols", "norm_x", "turn_x", "turn_ctx",
            "gates", "gates_exp", "gates_log", "gate_rows", "gate_clamp", "gate_back",
            "kv", "mvmk", "mqrq", "rgmo", "conv", "conv_silu", "turn_r", "retention", "mlstm", "head_norm",
            "turn_y", "merge", "turn_m", "out2", "norm_2", "turn_2", "query", "key_scores", "top_keys",
            "soft", "experts_of", "turn_sel", "spread", "experts", "final2")]
        STAGES = STAGES[:stop]
        FULL_OF = {"turn_in": 8, "project": 2, "turn_a": 3, "heads_a": 8, "values_a": 4, "turn_ar": 2, "turn_b": 5,
                   "turn_idx": 3, "index": 6, "turn_c": 5, "turn_mix": 8, "turn_h": 8, "embed": 8,
                   "ada_cols": 1, "turn_x": 8, "turn_ctx": 8, "gates": 4, "gate_rows": 4, "gate_back": 3, "turn_r": 6,
                   "turn_y": 8, "turn_m": 8, "turn_2": 8, "key_scores": 8, "turn_sel": 3}
        full, _f = [], 0
        for name, _ in STAGES:
            full.append(_f)
            _f += FULL_OF.get(name, 0)
        RMS_OF = {"norm": (1, 1), "prep_a": (1, 1), "norm_c": (1, 0), "final1": (1, 1), "norm_x": (1, 1),
                  "head_norm": (1, 0), "norm_2": (1, 1), "final2": (1, 1)}
        rms_k, rms_s, _k, _s = [], [], 0, 0
        for name, _ in STAGES:
            rms_k.append(_k)
            rms_s.append(_s)
            _k += RMS_OF.get(name, (0, 0))[0]
            _s += RMS_OF.get(name, (0, 0))[1]

        def ztiles(s):
            return z[:, s * D:(s + 1) * D]

        def col(c):
            return cols[:, c:c + 1]

        MIX_COL = [MIX0[0] + i * HD for i in range(6)] + [MIX0[1] + i * HD for i in range(5)] + \
                  [MIX0[2] + i * HD for i in range(5)]
        norm_c_in = zt[:, :, QC0:QC0 + C_HEADS * HD].rearrange("p t (h d) -> p t h d", h=C_HEADS)
        norm_c_sq = r2[:, 0:NT * C_HEADS * HD].rearrange("p (t h d) -> p t h d", t=NT, h=C_HEADS)

        def turn_ab_src(m):
            q0, k0 = (QB0, KB0) if m == "B" else (QC0, KC0)
            return lambda s, k: zt[:, s, (q0 + k * HD if k < 5 else k0 + (k - 5) * HD):][:, 0:HD]

        def turn_ab_dst(k):
            return act[:, k * TOK:(k + 1) * TOK]

        def turn_a_src(s, k):
            return zt[:, s, CQ0 + k * P:][:, 0:P] if k < 5 else kd[:, s, :]

        def turn_a_dst(k):
            return cqT[:, k, :] if k < 3 else ckvT[:, k - 3, :] if k < 5 else kpeT

        def idx_src(s, k):
            return zt[:, s, QI0 + k * P:][:, 0:P] if k < 4 else kid[:, s, :]

        aux_at, _a = {}, 0
        for l in range(DEPTH):
            for what, n in (("a", 2), ("ple", 2)):
                _a += n * 16
                aux_at[what, l] = _a
        _a += 16
        aux_at["final"] = _a
        for what in ("trig2", "wgates", "ctx", "dist", "gt1", "keys", "gt2", "final2"):
            _a += 16
            aux_at[what] = _a

        cT = act[:, 4096:8192].rearrange("p (k n) -> p k n", k=KT)
        both = act[:, 0:8192].rearrange("p (s n) -> p s n", s=2)
        czt = r2[:, :].rearrange("p (t n) -> p t n", t=NT)
        RK, RV, MV, RQ, RG, MO, RAW = 0, 512, 1536, 2560, 3072, 4096, 5120
        raw_x = zt[:, 0, RAW:RAW + 2048].rearrange("p (b n) -> p b n", b=8)
        raw_c = zt[:, 1, RAW:RAW + 1024].rearrange("p (b n) -> p b n", b=4)
        conv = act[:, 4096:7168].rearrange("p (b n) -> p b n", b=12)
        rT = act[:, 7168:10240].rearrange("p (b n) -> p b n", b=12)
        dist = zt[:, 0, RAW:RAW + 2048].rearrange("p (d i n) -> p d i n", d=2, i=4)
        work = zt[:, 1, RAW:RAW + 2048].rearrange("p (b n) -> p b n", b=4)
        adac = mask[:, 0:128].rearrange("p (b r) -> p b r", r=2)
        modc = mask[:, 128:176].rearrange("p (m k) -> p m k", m=3)
        SEC = {"sh1": 0, "sc1": 1, "sh2": 3, "sc2": 4}
        SECS = ["sh1", "sc1", "sh2", "sc2"]
        gpad = z[:, 0:2048].rearrange("p (d s n) -> p d s n", d=4, s=4)

        def row(i):
            return z[:, 4096 + i * 512:4608 + i * 512]

        negm = wsmall[:, :].rearrange("p (d n) -> p d n", d=2)
        yT = act[:, 4096:8192].rearrange("p (k n) -> p k n", k=KT)
        qT = yT
        keysT = r2[:, 0:2048].rearrange("p (b n) -> p b n", b=16)
        gt = act[:, 8192:8192 + D]
        S = z[:, 0:4096].rearrange("p (s b n) -> p s b n", s=NT, b=16)
        sv = z[:, 4096:4608].rearrange("p (s b n) -> p s b n", s=NT, b=16)
        si = z[:, 4608:5120].bitcast(U32).rearrange("p (s b n) -> p s b n", s=NT, b=16)
        sif = z[:, 5120:5632].rearrange("p (s b n) -> p s b n", s=NT, b=16)
        cand = z[:, 5632:9728].rearrange("p (s b n) -> p s b n", s=NT, b=P_HEADS)
        bs = z[:, 9728:9984].rearrange("p (s b n) -> p s b n", s=NT, b=P_HEADS)
        bj = z[:, 9984:10240].bitcast(U32)
        bjv = bj.rearrange("p (s b n) -> p s b n", s=NT, b=P_HEADS)
        j12 = [z[:, 10240 + i * 256:10496 + i * 256].bitcast(U32) for i in range(2)]
        j12f = [z[:, 10752 + i * 256:11008 + i * 256].rearrange("p (s n) -> p s n", s=NT) for i in range(2)]
        sel = [z[:, 11264 + i * 256:11520 + i * 256].rearrange("p (s n) -> p s n", s=NT) for i in range(3)]
        hot = z[:, 12032:14080].rearrange("p (a n) -> p a n", n=P_TOPK)
        selT = act[:, 4096:4864].rearrange("p (m n) -> p m n", m=3)
        hots = r2[:, 2048:4096].rearrange("p (b m n) -> p b m n", b=8, m=2)
        SB = 32
        stage = z[:, 0:8192].rearrange("p (b i n) -> p b i n", b=2, n=SB)
        slab = r2[:, 0:2048].rearrange("p (a b i n) -> p a b i n", a=2, b=TOK // SB, i=4)
        hid = r2[:, 2048:3072].rearrange("p (i n) -> p i n", i=4)
        yacc = z[:, 0:4096].rearrange("p (t n) -> p t n", t=NT)
        GT = nc.dram_tensor("gate_matrix", [TOK // SB, P, P, SB], F32).ap()
        GTROWS = nc.dram_tensor("gate_rows", [2, D], F32).ap()

        re_att = sem("re_att")
        re_exp = sem("re_exp")
        re_ready = sem("re_ready")
        re_out = sem("re_out")
        re_done = sem("re_done")
        ml_att = sem("ml_att")
        ml_arg = sem("ml_arg")
        ml_exp = sem("ml_exp")
        ml_ready = sem("ml_ready")
        ml_out = sem("ml_out")
        ml_done = sem("ml_done")
        mg_sig = sem("mg_sig")
        mg_sum = sem("mg_sum")
        hot_made = sem("hot_made")
        hot_used = sem("hot_used")
        sp_read = sem("sp_read")
        sp_stored = [sem(f"sp_stored{i}") for i in range(2)]
        slab_full = [sem(f"slab_full{i}") for i in range(2)]
        hid_act = sem("hid_act")
        hid_done = sem("hid_done")
        up_full = sem("up_full")
        up_read = sem("up_read")
        yacc_zero = sem("yacc_zero")
        h_sum = sem("h_sum")
        bias_in = sem("bias_in")
        stored_rows = sem("stored_rows")
        result = sem("result")

        block = ctx.enter_context(nc.Block())

        @block.sync
        def _(sp):
            sp.dma_start(ht, t["x"].rearrange("(t p) d -> p t d", p=P)).then_inc(consts, 16)
            sp.dma_start(cols[:, :], t["cols"]).then_inc(consts, 16)
            for j in range(PIECES):
                sp.dma_start(ring[:, j, :], t["stream"][0, j]).then_inc(piece_full[j], 16)
            with sp.Fori(1, N_PAIRS) as c:
                for j in range(PIECES):
                    sp.wait_ge(piece_used[j], c)
                    sp.dma_start(ring[:, j, :], t["stream"][bass.ds(c, 1), j].rearrange("a p n -> p (a n)"))\
                      .then_inc(piece_full[j], 16)
            if stop >= 90:
                sp.wait_ge(stage_done["dve"], len(STAGES))
                sp.dma_start(t["out"].rearrange("(t p) d -> p t d", p=P), ht).then_inc(result, 16)
                sp.wait_ge(result, 16)

        @block.gpsimd
        def _(pool):
            for n, (name, l) in enumerate(STAGES):
                begin(pool, n)
                if name == "setup":
                    pool.dma_start(sti[:, 0:NT], t["positions"]).then_inc(consts_p, 16)
                    pool.dma_start(bc[:, :], t["bc"].partition_broadcast(P)).then_inc(consts_p, 16)
                    pool.dma_start(wsmall[:, :], t["wsmall"]).then_inc(consts_p, 16)
                    pool.dma_start(z[:, 0:32], t["inv_freq"].partition_broadcast(P)).then_inc(consts_p, 16)
                    pool.dma_start(z[:, 512:1024], t["lam"].partition_broadcast(P)).then_inc(consts_p, 16)
                    pool.dma_start(w_uq, t["w_uq"][0].rearrange("(k p) n -> p k n", p=P)).then_inc(aux, 16)
                    pool.dma_start(w_ukv, t["w_ukv"][0].rearrange("(k p) n -> p k n", p=P)).then_inc(aux, 16)
                    chain(pool, "pool", pool.memset(ident[:, :], 0.0))
                    pool.affine_select(out=ident[:, :], in_=ident[:, :], compare_op=ALU.not_equal, fill=1.0,
                                       base=0, pattern=[[-1, P]], channel_multiplier=1)
                    pool.memset(ones[:, :], 1.0)
                    pool.iota(iota[:, :], pattern=[[1, P]], base=0, channel_multiplier=0,
                              allow_small_or_imprecise_dtypes=True)
                elif name == "attend_a":
                    pool.dma_start(w_ple, t["w_ple"][l].rearrange("(k p) n -> p k n", p=P)).then_inc(aux, 16)
                    pool.dma_start(pT, t["pT"][l].rearrange("(k p) n -> p k n", p=P)).then_inc(aux, 16)
                elif name == "gate" and l + 1 < DEPTH:
                    pool.dma_start(w_uq, t["w_uq"][l + 1].rearrange("(k p) n -> p k n", p=P)).then_inc(aux, 16)
                    pool.dma_start(w_ukv, t["w_ukv"][l + 1].rearrange("(k p) n -> p k n", p=P)).then_inc(aux, 16)
                elif name == "final1":
                    pool.dma_start(act[:, W0:W0 + D], t["final_g"].partition_broadcast(P)).then_inc(aux, 16)
                elif name == "silu_c":
                    for r in range(2):
                        pool.dma_start(z[r:r + 1, 0:6 * D], t["b_ada"]).then_inc(bias_in, 16)
                    pool.dma_start(trig[:, :, :, :], t["trig2"]).then_inc(aux, 16)
                    pool.dma_start(wgates, t["wgates"]).then_inc(aux, 16)
                    pool.dma_start(r2[:, 0:4096].rearrange("p (t n) -> p t n", t=NT),
                                   t["ctx"].rearrange("(t p) d -> p t d", p=P)).then_inc(aux, 16)
                elif name == "ada_cols":
                    pool.dma_start(GTROWS[0:1, :], z[0:1, 2 * D:3 * D]).then_inc(stored_rows, 16)
                    pool.dma_start(GTROWS[1:2, :], z[0:1, 5 * D:6 * D]).then_inc(stored_rows, 16)
                    pool.wait_ge(stored_rows, 32)
                elif name == "conv_silu":
                    pool.dma_start(dist.rearrange("p d i n -> p (d i n)"), t["dist"]).then_inc(aux, 16)
                elif name == "merge":
                    pool.dma_start(gt, GTROWS[0].partition_broadcast(P)).then_inc(aux, 16)
                elif name == "turn_m":
                    pool.dma_start(keysT.rearrange("p b n -> p (b n)"), t["keysT"]).then_inc(aux, 16)
                elif name == "spread":
                    for b in range(TOK // SB):
                        pool.wait_ge(sp_read, (b + 1) * SB // 4)
                        pool.dma_start(GT[b], stage[:, b % 2]).then_inc(sp_stored[b % 2], 16)
                    for b in range(2):
                        pool.wait_ge(sp_stored[b], 8 * (TOK // SB))
                    pool.dma_start(gt, GTROWS[1].partition_broadcast(P)).then_inc(aux, 16)
                elif name == "experts":
                    def load_slab(g, b):
                        pool.dma_start(slab[:, b].rearrange("p b i n -> p b (i n)"),
                                       GT[:, :, bass.ds(g * 4, 4), :].rearrange("b p i n -> p b (i n)")).then_inc(slab_full[b], 16)
                    load_slab(0, 0)
                    load_slab(1, 1)
                    with pool.Fori(1, GROUPS // 2) as g:
                        for b in range(2):
                            pool.wait_ge(hid_done, g * 8 + (4 * b - 4))
                            load_slab(g * 2 + b, b)
                elif name == "final2":
                    pool.dma_start(act[:, 4096:4096 + D], t["final_g2"].partition_broadcast(P)).then_inc(aux, 16)
                end(pool, "pool")

        @block.tensor
        def _(pe):
            def xTk(s, k):
                return xT[:, k, s * P:(s + 1) * P]

            for n, (name, l) in enumerate(STAGES):
                begin(pe, n)
                if name == "turn_in":
                    turn_pe(pe, lambda s, k: ztiles(s)[:, k * P:(k + 1) * P])
                elif name == "project":
                    for s in range(NT):
                        for k in range(KT):
                            mm = pe.matmul(ps[:, 6 + s, 0:IDX_HEADS], xTk(s, k), wtail[:, l, k, :],
                                           start=(k == 0), stop=(k == KT - 1))
                        mm.then_inc(pe_full, 1)
                    stream_pe(pe, f"in{l}", 7, 2, xTk)
                elif name == "turn_a":
                    turn_pe(pe, turn_a_src, blocks=6)
                elif name == "heads_a":
                    pe.wait_ge(aux, aux_at["a", l])
                    for j in range(3):
                        for hd in (2 * j, 2 * j + 1):
                            for k in range(3):
                                mm = pe.matmul(ps[:, j, (hd % 2) * TOK:(hd % 2 + 1) * TOK], w_uq[:, k, hd * HD:(hd + 1) * HD],
                                               cqT[:, k, :], start=(k == 0), stop=(k == 2))
                        mm.then_inc(pe_full, 1)
                    for j in range(3):
                        for hd in (2 * j, 2 * j + 1):
                            for k in range(2):
                                mm = pe.matmul(ps[:, 3 + j, (hd % 2) * TOK:(hd % 2 + 1) * TOK],
                                               w_ukv[:, k, hd * HD:(hd + 1) * HD], ckvT[:, k, :], start=(k == 0), stop=(k == 1))
                        mm.then_inc(pe_full, 1)
                    for s in range(NT):
                        for k in range(3):
                            mm = pe.matmul(ps[:, 6 + s, 0:A_HEADS * A_ROPE], cqT[:, k, s * P:(s + 1) * P],
                                           w_uq[:, k, A_HEADS * HD:], start=(k == 0), stop=(k == 2))
                        mm.then_inc(pe_full, 1)
                elif name == "values_a":
                    for j in range(2):
                        for s in range(NT):
                            for k in range(2):
                                mm = pe.matmul(ps[:, 2 * j + s, 0:384], ckvT[:, k, s * P:(s + 1) * P],
                                               w_ukv[:, k, 768 + j * 384:768 + (j + 1) * 384], start=(k == 0), stop=(k == 1))
                            mm.then_inc(pe_full, 1)
                elif name == "turn_ar":
                    turn_pe(pe, lambda s, k: qr[:, s, k * P:(k + 1) * P], blocks=3)
                elif name in ("attend_a", "attend_b", "attend_c"):
                    attend_pe(pe, name[-1].upper(), l)
                elif name == "turn_b":
                    turn_pe(pe, turn_ab_src("B"), blocks=10)
                elif name == "turn_c":
                    turn_pe(pe, turn_ab_src("C"), blocks=10)
                elif name == "turn_idx":
                    turn_pe(pe, idx_src, blocks=5)
                elif name == "index":
                    for c in range(2):
                        r = c * IDX_DIM
                        for j in range(4):
                            mm = pe.matmul(ps[:, c, j * P:(j + 1) * P], qiT[r:r + IDX_DIM, j, 0:P], kiT[r:r + IDX_DIM, 0:P],
                                           start=True, stop=True)
                        mm.then_inc(pe_full, 1)
                    for c in range(2):
                        r = c * IDX_DIM
                        for j in range(4):
                            mm = pe.matmul(ps[:, 2 + 2 * c + j // 2, (j % 2) * TOK:(j % 2 + 1) * TOK],
                                           qiT[r:r + IDX_DIM, j, P:2 * P], kiT[r:r + IDX_DIM, :], start=True, stop=True)
                            if j % 2:
                                mm.then_inc(pe_full, 1)
                elif name == "turn_mix":
                    turn_pe(pe, lambda s, k: zt[:, s, MIX_COL[k]:][:, 0:HD])
                elif name == "project_out":
                    stream_pe(pe, f"out{l}", 2, 2, xTk)
                elif name == "turn_h":
                    turn_pe(pe, lambda s, k: ht[:, s, k * P:(k + 1) * P])
                elif name == "embed":
                    pe.wait_ge(aux, aux_at["ple", l])
                    for c in range(4):
                        for s in range(NT):
                            for k in range(2):
                                mm = pe.matmul(ps[:, 2 * c + s, :], pT[:, k, s * P:(s + 1) * P],
                                               w_ple[:, k, c * CHUNK:(c + 1) * CHUNK], start=(k == 0), stop=(k == 1))
                            mm.then_inc(pe_full, 1)
                elif name == "gate":
                    stream_pe(pe, f"gate{l}", 2, 2, xTk)
                elif name == "ada":
                    stream_pe(pe, "ada", 12, 1, lambda s, k: cols[:, C_SILU + 2 * k:C_SILU + 2 * k + 2], M=2, tiles=1)
                elif name == "ada_cols":
                    for b in range(4 * KT):
                        c0 = SEC[SECS[b // KT]] * D + (b % KT) * P
                        mm = pe.transpose(ps[:, 0, 2 * b:2 * b + 2], z[0:2, c0:c0 + P], ident[0:2, 0:2])
                    mm.then_inc(pe_full, 1)
                elif name == "turn_x":
                    turn_pe(pe, lambda s, k: ztiles(s)[:, k * P:(k + 1) * P])
                elif name == "turn_ctx":
                    turn_pe(pe, lambda s, k: r2[:, s * D + k * P:][:, 0:P])
                elif name == "gates":
                    for s in range(4):
                        src = (xT if s < 2 else cT)
                        for k in range(KT):
                            mm = pe.matmul(ps[:, s, 0:16], src[:, k, (s % 2) * P:(s % 2 + 1) * P], wgates[:, k, :],
                                           start=(k == 0), stop=(k == KT - 1))
                        mm.then_inc(pe_full, 1)
                elif name == "gate_rows":
                    for dk in range(4):
                        for i, s in enumerate((2, 3, 0, 1)):
                            mm = pe.transpose(ps[:, dk, i * P:(i + 1) * P], gpad[:, dk, s, :], ident[:, :])
                        mm.then_inc(pe_full, 1)
                elif name == "gate_back":
                    for d in range(2):
                        for i in range(4):
                            mm = pe.transpose(ps[:, d, i * P:(i + 1) * P], row((7, 13)[d])[:, i * P:(i + 1) * P], ident[:, :])
                        mm.then_inc(pe_full, 1)
                    for d in range(2):
                        for s in range(NT):
                            c0 = (TOK, 0)[d] + s * P
                            mm = pe.transpose(ps[:, 2, (2 * d + s) * P:(2 * d + s + 1) * P],
                                              row((11, 14)[d])[:, c0:c0 + P], ident[:, :])
                    mm.then_inc(pe_full, 1)
                elif name == "kv":
                    stream_pe(pe, "kv", 2, 4, lambda s, k: (xT if s < 2 else cT)[:, k, (s % 2) * P:(s % 2 + 1) * P], tiles=4)
                elif name in ("mvmk", "mqrq", "query"):
                    for i in range(2 if name == "query" else 1):
                        for par in range(2):
                            pair = PAIR0[name] + i
                            pe.wait_ge(evac[par], EVAC0[name] + 4 * i)
                            turned = name == "query" or (name == "mvmk") == (par == 1)
                            for k in range(KT):
                                j = par * 4 + k // PIECE_KT
                                if k % PIECE_KT == 0:
                                    pe.wait_ge(piece_full[j], 16 * (pair + 1))
                                w = ring[:, j, (k % PIECE_KT) * CHUNK:(k % PIECE_KT + 1) * CHUNK]
                                flags = dict(start=(k == 0), stop=(k == KT - 1))
                                if turned:
                                    for b in range(4):
                                        wb = w[:, b * P:(b + 1) * P]
                                        if name == "mvmk":
                                            mm = pe.matmul(ps[:, par * 4 + b, :], wb, both[:, :, k * TOK:(k + 1) * TOK], **flags)
                                        else:
                                            mm = pe.matmul(ps[:, par * 4 + b, 0:TOK], wb, xT[:, k, :], **flags)
                                else:
                                    for s in range(4 if name == "mvmk" else 2):
                                        lhs = (xT if s < 2 else cT)[:, k, (s % 2) * P:(s % 2 + 1) * P]
                                        mm = pe.matmul(ps[:, par * 4 + s, :], lhs, w, **flags)
                                if k % PIECE_KT == PIECE_KT - 1:
                                    mm.then_inc(piece_used[j], 1)
                elif name == "rgmo":
                    stream_pe(pe, "rgmo", 2, 2, xTk)
                elif name == "turn_r":
                    def src(s, k):
                        if k < 4:
                            return zt[:, s, RQ + k * P:][:, 0:P]
                        return zt[:, s, RK + (k - 4) * P:][:, 0:P] if k < 8 else czt[:, s, RK + (k - 8) * P:][:, 0:P]
                    turn_pe(pe, src, blocks=12)
                elif name == "retention":
                    def att(u):
                        hd, half = u // 2, u % 2
                        r, b = (hd % 2) * R_DK, hd // 2
                        if u >= 2:
                            pe.wait_ge(re_ready, u - 1)
                        keys_ = rT[:, (4 if half else 8) + b, :]
                        for i in range(2):
                            mm = pe.matmul(ps[:, u % 2, i * TOK:(i + 1) * TOK], keys_[r:r + R_DK, i * P:(i + 1) * P],
                                           rT[r:r + R_DK, b, :], start=True, stop=True)
                        mm.then_inc(re_att, 1)

                    def out(u):
                        hd, half = u // 2, u % 2
                        pe.wait_ge(re_ready, u + 1)
                        if half == 0 and hd >= 2:
                            pe.wait_ge(re_done, hd - 1)
                        v = zt if half else czt
                        for s in range(NT):
                            for i in range(2):
                                mm = pe.matmul(ps[:, 2 + 2 * (hd % 2) + s, 0:R_DV],
                                               work[:, 2 * (u % 2) + 1, i * TOK + s * P:i * TOK + (s + 1) * P],
                                               v[:, i, RV + hd * R_DV:RV + (hd + 1) * R_DV],
                                               start=(half == 0 and i == 0), stop=(half == 1 and i == 1))
                        mm.then_inc(re_out, 1)

                    for u in range(2 * R_HEADS + 1):
                        if u < 2 * R_HEADS:
                            att(u)
                        if u >= 1:
                            out(u - 1)
                elif name == "mlstm":
                    def att(v):
                        hd, d = v // 2, v % 2
                        if d == 0:
                            if hd >= 2:
                                pe.wait_ge(ml_ready, 2 * hd - 2)
                            for i in range(4):
                                kT = conv[:, 8 + hd, i * P:(i + 1) * P] if i < 2 else conv[:, hd, (i - 2) * P:(i - 1) * P]
                                pe.matmul(ps[:, 2 * (hd % 2) + i // 2, (i % 2) * TOK:(i % 2 + 1) * TOK], kT, conv[:, 4 + hd, :],
                                          start=True, stop=True)
                        if v >= 2:
                            pe.wait_ge(ml_arg, v - 1)
                        mm = pe.matmul(ps[:, 4 + v % 2, 0:TOK], ones[32 * hd:32 * hd + 1, :], negm[32 * hd:32 * hd + 1, d, :],
                                       start=True, stop=True, tile_position=(32 * hd, 0))
                        mm.then_inc(ml_att, 1)

                    def out(v):
                        hd, d = v // 2, v % 2
                        pe.wait_ge(ml_ready, v + 1)
                        if v >= 1:
                            pe.wait_ge(ml_done, v)
                        w = work[:, 2 * (v % 2):2 * (v % 2) + 2, :].rearrange("p b n -> p (b n)")
                        for s in range(NT):
                            see = [i for i in range(4) if i < 2 or (i - 2 <= s if d == 0 else i - 2 >= s)]
                            for what in range(2):
                                for i in see:
                                    vals = ones[:, 0:1] if what else (czt if i < 2 else zt)[:, i % 2, MV + hd * M_DV:MV + (hd + 1) * M_DV]
                                    dst = ps[:, 6 + s, M_DV:M_DV + 1] if what else ps[:, 6 + s, 0:M_DV]
                                    mm = pe.matmul(dst, w[:, i * TOK + s * P:i * TOK + (s + 1) * P], vals,
                                                   start=(i == see[0]), stop=(i == see[-1]))
                        mm.then_inc(ml_out, 1)

                    for v in range(2 * M_HEADS + 1):
                        if v < 2 * M_HEADS:
                            att(v)
                        if v >= 1:
                            out(v - 1)
                elif name == "turn_y":
                    turn_pe(pe, lambda s, k: zt[:, s, RG + k * P:][:, 0:P])
                elif name == "merge":
                    for n4 in range(4):
                        for which in range(3):
                            c = 3 * n4 + which
                            par, pair = c % 2, PAIR0["merge"] + c // 2
                            if n4 >= 1 and which == 0:
                                pe.wait_ge(mg_sig, 2 * n4)
                            if n4 >= 1 and which == 2:
                                pe.wait_ge(mg_sum, n4)
                            for k in range(KT):
                                j = par * 4 + k // PIECE_KT
                                if k % PIECE_KT == 0:
                                    pe.wait_ge(piece_full[j], 16 * (pair + 1))
                                w = ring[:, j, (k % PIECE_KT) * CHUNK:(k % PIECE_KT + 1) * CHUNK]
                                for s in range(NT):
                                    if which < 2:
                                        mm = pe.matmul(ps[:, 2 * which + s, :], xTk(s, k), w, start=(k == 0), stop=(k == KT - 1))
                                    else:
                                        mm = pe.matmul(ps[:, 4 + 2 * (k // 8) + s, :], yT[:, k, s * P:(s + 1) * P], w,
                                                       start=(k % 8 == 0), stop=(k % 8 == 7))
                                if k % PIECE_KT == PIECE_KT - 1:
                                    mm.then_inc(piece_used[j], 1)
                elif name == "turn_m":
                    turn_pe(pe, lambda s, k: ztiles(s)[:, k * P:(k + 1) * P])
                elif name == "out2":
                    stream_pe(pe, "out2", 2, 2, xTk)
                elif name == "turn_2":
                    turn_pe(pe, lambda s, k: ztiles(s)[:, k * P:(k + 1) * P])
                elif name == "key_scores":
                    for s in range(NT):
                        for b in range(16):
                            mm = pe.matmul(ps[:, 4 * s + b // 4, (b % 4) * P:(b % 4 + 1) * P], qT[:, b, s * P:(s + 1) * P],
                                           keysT[:, b, :], start=True, stop=True)
                            if b % 4 == 3:
                                mm.then_inc(pe_full, 1)
                elif name == "turn_sel":
                    for m in range(3):
                        for s in range(NT):
                            mm = pe.transpose(ps[:, m, s * P:(s + 1) * P], sel[m][:, s, :], ident[:, :])
                        mm.then_inc(pe_full, 1)
                elif name == "spread":
                    def block_of_tokens(b, first):
                        for i in range(SB):
                            pe.wait_ge(hot_made, b * SB + (i + 1))
                            if i % 4 == 0 and not first:
                                pe.wait_ge(sp_read, b * 8 + (i // 4 - 7))
                            mm = pe.matmul(ps[:, i // 4, (i % 4) * P:(i % 4 + 1) * P], hots[:, i % 8, 0, :], hots[:, i % 8, 1, :],
                                           start=True, stop=True)
                            mm.then_inc(hot_used, 1)

                    block_of_tokens(0, True)
                    with pe.Fori(1, TOK // SB) as b:
                        block_of_tokens(b, False)
                elif name == "experts":
                    base = PAIR0["experts"]

                    def down(g):
                        for k in range(KT):
                            if k % PIECE_KT == 0:
                                pe.wait_ge(piece_full[k // PIECE_KT], g * 16 + 16 * (base + 1))
                            w = ring[:, k // PIECE_KT, (k % PIECE_KT) * CHUNK:(k % PIECE_KT + 1) * CHUNK]
                            for b in range(4):
                                mm = pe.matmul(ps[:, b, 0:TOK], w[:, b * P:(b + 1) * P], xT[:, k, :],
                                               start=(k == 0), stop=(k == KT - 1))
                            if k % PIECE_KT == PIECE_KT - 1:
                                mm.then_inc(piece_used[k // PIECE_KT], 1)

                    def up(g):
                        for dc in range(4):
                            if dc >= 2 or not isinstance(g, int) or g > 0:
                                pe.wait_ge(up_read, g * 4 + (dc - 1))
                            for i in range(4):
                                if dc == 0:
                                    pe.wait_ge(hid_done, g * 4 + (i + 1))
                                    pe.wait_ge(piece_full[4 + i], g * 16 + 16 * (base + 1))
                                for s in range(NT):
                                    mm = pe.matmul(ps[:, 4 + 2 * (dc % 2) + s, :], hid[:, i, s * P:(s + 1) * P],
                                                   ring[:, 4 + i, dc * CHUNK:(dc + 1) * CHUNK], start=(i == 0), stop=(i == 3))
                                if dc == 3 and i < 3:
                                    mm.then_inc(piece_used[4 + i], 1)
                            if dc == 3:
                                mm.then_inc(piece_used[7], 1)
                            else:
                                mm.then_inc(up_full, 1)

                    down(0)
                    up(0)
                    with pe.Fori(1, GROUPS) as g:
                        down(g)
                        up(g)
                end(pe, "pe")

        @block.scalar
        def _(sc):
            for n, (name, l) in enumerate(STAGES):
                begin(sc, n)
                f0 = full[n]
                if name == "angles":
                    sc.activation(trig[:, 1, :, :], z[:, 128:192].rearrange("p (t n) -> p t n", t=NT), ACT.Sin)
                    sc.activation(trig[:, 0, :, :], z[:, 192:256].rearrange("p (t n) -> p t n", t=NT), ACT.Sin)
                    sc.activation(st[:, 64:68], st[:, 68:72], ACT.Exp)
                elif name == "norm":
                    rms_act(sc, rms_k[n], [(ht[:, s, :], D, z[:, 2 * D + s * D:][:, 0:D]) for s in range(NT)], NT)
                elif name == "turn_in":
                    turn_evac(sc, "act", f0, lambda k: xT[:, k, :], scale=lambda k: col(C_NORM + l * KT + k))
                elif name == "project":
                    base = PAIR0[f"in{l}"]
                    with sc.Fori(0, 7) as i:
                        for par in range(2):
                            sc.wait_ge(piece_used[par * 4 + 3], i + (base + 1))
                            sc.copy(zt[:, 0, bass.ds(i * 1024 + par * CHUNK, CHUNK)], ps[:, par * 2, :]).then_inc(evac[par], 1)
                elif name == "prep_a":
                    junk = [act[:, 0:A_Q], act[:, A_Q:2 * A_Q], act[:, 1024:1024 + A_KV], act[:, 1536:1536 + A_KV]]
                    rms_act(sc, rms_k[n], [(zt[:, s, CQ0:CQ0 + A_Q], A_Q, junk[s]) for s in range(NT)] +
                            [(zt[:, s, CKV0:CKV0 + A_KV], A_KV, junk[2 + s]) for s in range(NT)], 4)
                    for g0, w in zip(MIX0, MIXW):
                        sc.activation(zt[:, :, g0:g0 + w], zt[:, :, g0:g0 + w], ACT.Silu)
                elif name == "turn_a":
                    turn_evac(sc, "act", f0, turn_a_dst, blocks=6,
                              scale=lambda k: col(C_QN + l * 3 + k if k < 3 else C_KVN + l * 2 + k - 3))
                elif name == "heads_a":
                    for j in (3, 4, 5):
                        sc.wait_ge(pe_full, f0 + j + 1)
                        sc.copy(knT[:, 2 * j - 6:2 * j - 4, :], ps[:, j, :].rearrange("p (h n) -> p h n", h=2))
                    sc.wait_ge(pe_full, f0 + 8)
                    sc.copy(qr[:, 1, :], ps[:, 7, 0:384])
                elif name == "values_a":
                    for j in range(2):
                        sc.wait_ge(pe_full, f0 + 2 * j + 2)
                        sc.copy(va[:, 1, j * 384:(j + 1) * 384], ps[:, 2 * j + 1, 0:384])
                        sc.copy(va[:, 0, j * 384:(j + 1) * 384], ps[:, 2 * j, 0:384])
                elif name == "turn_ar":
                    turn_evac(sc, "act", f0, lambda k: qrT[:, k, :], blocks=3)
                elif name in ("attend_a", "attend_b", "attend_c"):
                    attend_act(sc, name[-1].upper(), l)
                elif name in ("turn_b", "turn_c"):
                    turn_evac(sc, "act", f0, turn_ab_dst, blocks=10)
                elif name == "turn_idx":
                    turn_evac(sc, "act", f0, lambda k: act[:, 2560 + k * TOK:][:, 0:TOK], blocks=5)
                elif name == "index":
                    for c in range(2):
                        sc.wait_ge(pe_full, f0 + c + 1)
                        sc.activation(rel[:, c:8:2, 0:P], ps[:, c, :].rearrange("p (h n) -> p h n", h=4), ACT.Relu)\
                          .then_inc(rel_done, 1)
                    for c in range(2):
                        for j in range(2):
                            b = 2 + 2 * c + j
                            sc.wait_ge(pe_full, f0 + b + 1)
                            sc.activation(rel[:, 4 * j + c:4 * j + c + 3:2, P:], ps[:, b, :].rearrange("p (h n) -> p h n", h=2), ACT.Relu)\
                              .then_inc(rel_done, 1)
                elif name == "norm_c":
                    rms_act(sc, rms_k[n], None, NT * C_HEADS, have_sums=True)
                elif name == "turn_mix":
                    turn_evac(sc, "act", f0, lambda k: xT[:, k, :])
                elif name == "turn_h":
                    turn_evac(sc, "act", f0, lambda k: xT[:, k, :])
                elif name == "embed":
                    for c in range(4):
                        sc.wait_ge(pe_full, f0 + 2 * c + 1)
                        sc.copy(z[:, c * CHUNK:(c + 1) * CHUNK], ps[:, 2 * c, :])
                elif name == "gate":
                    base = PAIR0[f"gate{l}"]
                    for i in range(2):
                        for par in range(2):
                            c = 2 * i + par
                            sc.wait_ge(piece_used[par * 4 + 3], i + base + 1)
                            if c >= 2:
                                sc.wait_ge(gate_used, l * 4 + c - 1)
                            for s in range(NT):
                                m = sc.activation(r2[:, (par * 2 + s) * 512:][:, 0:512], ps[:, par * 2 + s, :], ACT.Sigmoid)
                                m.then_inc(evac[par], 1)
                elif name == "final1":
                    rms_act(sc, rms_k[n], [(ht[:, s, :], D, z[:, 2 * D + s * D:][:, 0:D]) for s in range(NT)], NT)
                elif name == "silu_c":
                    sc.activation(cols[:, C_SILU:C_SILU + 2 * KT], cols[:, C_SILU:C_SILU + 2 * KT], ACT.Silu)
                elif name == "norm_x":
                    sc.wait_ge(aux, aux_at["ctx"])
                    rms_act(sc, rms_k[n], [(ht[:, s, :], D, z[:, 2 * D + s * D:][:, 0:D]) for s in range(NT)] +
                            [(r2[:, s * D:(s + 1) * D], D, z[:, 4 * D + s * D:][:, 0:D]) for s in range(NT)], 4)
                elif name == "turn_x":
                    turn_evac(sc, "act", f0, lambda k: xT[:, k, :], scale=lambda k: modc[:, 0, k:k + 1],
                              bias=lambda k: adac[:, k, 0:1])
                elif name == "turn_ctx":
                    turn_evac(sc, "act", f0, lambda k: cT[:, k, :], scale=lambda k: modc[:, 1, k:k + 1],
                              bias=lambda k: adac[:, k, 1:2])
                elif name == "gates_exp":
                    chain(sc, "act", sc.activation(z[:, 2304:2352], z[:, 2304:2352], ACT.Exp, scale=-1.0))
                    sc.activation(z[:, 2304:2352], z[:, 2304:2352], ACT.Ln, bias=1.0)
                elif name == "gate_clamp":
                    sc.activation(row(11)[:, TOK:], row(11)[:, TOK:], ACT.Exp)
                    sc.activation(row(14)[:, 0:TOK], row(12)[:, 2 * TOK - 1:TOK - 1:-1], ACT.Exp)
                elif name == "kv":
                    base = PAIR0["kv"]
                    for i in range(2):
                        for par in range(2):
                            sc.wait_ge(piece_used[par * 4 + 3], i + base + 1)
                            c0 = (2 * i + par) * CHUNK
                            for s in (0, 2):
                                sc.copy((zt if s < 2 else czt)[:, 0, c0:c0 + CHUNK], ps[:, par * 4 + s, :]).then_inc(evac[par], 1)
                elif name == "mvmk":
                    sc.wait_ge(piece_used[3], PAIR0[name] + 1)
                    for s in (0, 2):
                        sc.copy((zt if s < 2 else czt)[:, 0, 2048:2560], ps[:, s, :]).then_inc(evac[0], 1)
                    sc.wait_ge(piece_used[7], PAIR0[name] + 1)
                    for b in (0, 2):
                        sc.copy(raw_x[:, b, :], ps[:, 4 + b, 0:TOK])
                        sc.copy(raw_c[:, b, :], ps[:, 4 + b, TOK:]).then_inc(evac[1], 1)
                elif name == "mqrq":
                    sc.wait_ge(piece_used[3], PAIR0[name] + 1)
                    for b in (0, 2):
                        sc.copy(raw_x[:, 4 + b, :], ps[:, b, 0:TOK]).then_inc(evac[0], 1)
                    sc.wait_ge(piece_used[7], PAIR0[name] + 1)
                    for c in range(2):
                        sc.copy(zt[:, 0, RQ + c * 256:][:, 0:256], ps[:, 4, c * 256:(c + 1) * 256]).then_inc(evac[1], 1)
                elif name == "rgmo":
                    base = PAIR0["rgmo"]
                    for i in range(2):
                        for par in range(2):
                            sc.wait_ge(piece_used[par * 4 + 3], i + base + 1)
                            c0 = RG + (2 * i + par) * CHUNK
                            sc.activation(zt[:, 0, c0:c0 + CHUNK], ps[:, par * 2, :], ACT.Silu if i == 0 else ACT.Sigmoid)\
                              .then_inc(evac[par], 1)
                elif name == "conv":
                    for f, c0 in ((ACT.Silu, RG), (ACT.Sigmoid, MO)):
                        sc.activation(zt[:, 1, c0:c0 + 1024], zt[:, 1, c0:c0 + 1024], f)
                elif name == "conv_silu":
                    sc.activation(act[:, 4096:7168], act[:, 4096:7168], ACT.Silu)
                elif name == "turn_r":
                    turn_evac(sc, "act", f0, lambda k: rT[:, k, :], blocks=12)
                elif name == "retention":
                    sc.wait_ge(aux, aux_at["dist"])
                    for u in range(2 * R_HEADS):
                        hd, half = u // 2, u % 2
                        if u >= 2:
                            sc.wait_ge(re_out, u - 1)
                        for d in range(2):
                            last = sc.activation(work[:, 2 * (u % 2) + d, :].rearrange("p (i n) -> p i n", i=2), dist[:, d, 2 * half:2 * half + 2, :],
                                                 ACT.Exp, scale=st[:, 112 + 8 * d + hd:113 + 8 * d + hd])
                        last.then_inc(re_exp, 1)
                elif name == "mlstm":
                    for v in range(2 * M_HEADS):
                        sc.wait_ge(ml_arg, v + 1)
                        w = work[:, 2 * (v % 2):2 * (v % 2) + 2, :]
                        sc.activation(w, w, ACT.Exp).then_inc(ml_exp, 1)
                elif name == "head_norm":
                    rms_act(sc, rms_k[n], None, 24, have_sums=True)
                elif name == "turn_y":
                    turn_evac(sc, "act", f0, lambda k: yT[:, k, :])
                elif name == "merge":
                    for n4 in range(4):
                        if n4 >= 1:
                            sc.wait_ge(mg_sum, n4)
                        for which in range(2):
                            c = 3 * n4 + which
                            sc.wait_ge(piece_used[(c % 2) * 4 + 3], PAIR0["merge"] + c // 2 + 1)
                            for s in range(NT):
                                a = sc.activation(r2[:, 2048 + (2 * which + s) * 512:][:, 0:512], ps[:, 2 * which + s, :], ACT.Sigmoid)
                            a.then_inc(mg_sig, 1)
                elif name == "turn_m":
                    turn_evac(sc, "act", f0, lambda k: xT[:, k, :])
                elif name == "norm_2":
                    rms_act(sc, rms_k[n], [(ht[:, s, :], D, z[:, 2 * D + s * D:][:, 0:D]) for s in range(NT)], NT)
                elif name == "turn_2":
                    turn_evac(sc, "act", f0, lambda k: xT[:, k, :], scale=lambda k: modc[:, 2, k:k + 1],
                              bias=lambda k: adac[:, 2 * KT + k, 0:1])
                elif name == "query":
                    for i in range(2):
                        for par in range(2):
                            sc.wait_ge(piece_used[par * 4 + 3], PAIR0[name] + i + 1)
                            for b in (0, 2):
                                sc.copy(qT[:, (2 * i + par) * 4 + b, :], ps[:, par * 4 + b, 0:TOK]).then_inc(evac[par], 1)
                elif name == "key_scores":
                    for b in range(4):
                        sc.wait_ge(pe_full, f0 + b + 1)
                        sc.copy(S[:, 0, 4 * b:4 * b + 4, :], ps[:, b, :].rearrange("p (b n) -> p b n", b=4))
                elif name == "soft":
                    for s in range(NT):
                        sc.activation(sel[2][:, s, :], sel[2][:, s, :], ACT.Exp)
                elif name == "spread":
                    def two_blocks(bb, first):
                        for half in range(2):
                            if not first:
                                sc.wait_ge(sp_stored[half], bb * 16)
                            for i in range(SB // 4):
                                sc.wait_ge(hot_used, bb * 64 + (half * SB + 4 * i + 4))
                                sc.copy(stage[:, half, :, 4 * i:4 * i + 4].rearrange("p i n -> p n i"),
                                        ps[:, i, :].rearrange("p (n i) -> p n i", n=4)).then_inc(sp_read, 1)

                    two_blocks(0, True)
                    with sc.Fori(1, TOK // (2 * SB)) as bb:
                        two_blocks(bb, False)
                elif name == "experts":
                    base = PAIR0["experts"]
                    with sc.Fori(0, GROUPS) as g:
                        sc.wait_ge(piece_used[3], g + (base + 1))
                        for b in range(4):
                            sc.activation(hid[:, b, :], ps[:, b, 0:TOK], ACT.Gelu).then_inc(hid_act, 1)
                elif name == "final2":
                    sc.wait_ge(h_sum, 1)
                    rms_act(sc, rms_k[n], [(ht[:, s, :], D, z[:, 2 * D + s * D:][:, 0:D]) for s in range(NT)], NT)
                end(sc, "act")

        @block.vector
        def _(dve):
            for n, (name, l) in enumerate(STAGES):
                begin(dve, n)
                f0 = full[n]
                if name == "setup":
                    chain(dve, "dve", dve.memset(mask[:, :], 0.0))
                    dve.memset(mask[0:64, 64:128], NEG)
                    dve.memset(mask[0:64, 128 + 192:], NEG)
                    dve.wait_ge(consts, 16 * 2)
                    dve.wait_ge(consts_p, 16 * 5)
                    pos, inv = st[:, 80:82], z[:, 0:32]
                    chain(dve, "dve", dve.tensor_copy(pos, sti[:, 0:NT]))
                    for s in range(NT):
                        a = dve.tensor_scalar(z[:, 32 + s * 32:64 + s * 32], inv, pos[:, s:s + 1], None, ALU.mult)
                    chain(dve, "dve", a)
                    ang, turns, r = z[:, 32:96], z[:, 96:160], z[:, 128:192]
                    turns = z[:, 256:320]
                    chain(dve, "dve", dve.tensor_scalar(turns, ang, float(np.float32(1 / TWO_PI)), 12582912.0, ALU.mult, ALU.add))
                    chain(dve, "dve", dve.tensor_scalar(turns, turns, 12582912.0, None, ALU.subtract))
                    c1 = 6.28125
                    c2 = float(np.float32(np.round((TWO_PI - c1) * 2 ** 20) / 2 ** 20))
                    c3 = float(np.float32(TWO_PI - c1 - c2))
                    prev = ang
                    for cc in (c1, c2, c3):
                        chain(dve, "dve", dve.scalar_tensor_tensor(r, turns, -cc, prev, ALU.mult, ALU.add))
                        prev = r
                    pi = float(np.nextafter(np.float32(np.pi), np.float32(0)))
                    chain(dve, "dve", dve.tensor_scalar(r, r, pi, -pi, ALU.min, ALU.max))
                    c = z[:, 192:256]
                    chain(dve, "dve", dve.scalar_tensor_tensor(c, r, -1.0, r, ALU.mult, ALU.max))
                    dve.tensor_scalar(c, c, -1.0, float(np.float32(np.pi / 2)), ALU.mult, ALU.add)
                    lam = z[:, 512:1024].rearrange("p (k l n) -> p k l n", k=4, l=DEPTH)
                    for ly in range(DEPTH):
                        for pr in range(2):
                            k = 2 * ly + pr
                            dve.tensor_tensor_reduce(z[:, 1024 + k * 64:][:, 0:64], lam[:, 2 * pr, ly, :], lam[:, 2 * pr + 1, ly, :],
                                                     1.0, 0.0, ALU.mult, ALU.add, st[:, 68 + k:69 + k])
                elif name == "norm":
                    if l == 0:
                        e = st[:, 64:68].rearrange("p (l k) -> p l k", k=2)
                        chain(dve, "dve", dve.tensor_tensor(st[:, 60:62], e[:, :, 1], e[:, :, 0], ALU.subtract))
                        for ly in range(DEPTH):
                            init = 0.8 - 0.6 * float(np.exp(-0.3 * ly))
                            dve.tensor_scalar(st[:, 60 + ly:61 + ly], st[:, 60 + ly:61 + ly], -init, None, ALU.add)
                            dve.tensor_scalar(bc[:, B_SUB + ly * HD:][:, 0:HD], bc[:, B_SUB + ly * HD:][:, 0:HD], 1.0 - init, None, ALU.mult)
                    rms_dve(dve, rms_k[n], NT, sums=rms_s[n])
                    for s in range(NT):
                        dve.tensor_scalar(ztiles(s), ht[:, s, :], rs[:, 64 + s:65 + s], None, ALU.mult)
                elif name == "turn_in":
                    turn_evac(dve, "dve", f0, lambda k: xT[:, k, :], scale=lambda k: col(C_NORM + l * KT + k))
                elif name == "project":
                    for s in range(NT):
                        dve.wait_ge(pe_full, f0 + s + 1)
                        dve.tensor_copy(zt[:, s, WI0:WI0 + IDX_HEADS], ps[:, 6 + s, 0:IDX_HEADS])
                    base = PAIR0[f"in{l}"]
                    with dve.Fori(0, 7) as i:
                        for par in range(2):
                            dve.wait_ge(piece_used[par * 4 + 3], i + (base + 1))
                            dve.tensor_copy(zt[:, 1, bass.ds(i * 1024 + par * CHUNK, CHUNK)], ps[:, par * 2 + 1, :]).then_inc(evac[par], 1)
                elif name == "prep_a":
                    kr = zt[:, :, KR0:KR0 + A_ROPE].unsqueeze(2)
                    kd1 = kd[:, :, 0:64].unsqueeze(2)
                    rope(dve, kr[:, :, :, 0:32], kr[:, :, :, 32:64], 1, 32, lambda i, w: r2[:, i * 384:][:, 0:w],
                         kd1[:, :, :, 0:32], kd1[:, :, :, 32:64])
                    dve.tensor_copy(kd[:, :, 64:128], kd[:, :, 0:64])
                    rms_dve(dve, rms_k[n], 4, sums=rms_s[n])
                    for s in range(NT):
                        dve.tensor_scalar(zt[:, s, CQ0:CQ0 + A_Q], zt[:, s, CQ0:CQ0 + A_Q], rs[:, 64 + s:65 + s], None, ALU.mult)
                        dve.tensor_scalar(zt[:, s, CKV0:CKV0 + A_KV], zt[:, s, CKV0:CKV0 + A_KV], rs[:, 66 + s:67 + s], None, ALU.mult)
                elif name == "turn_a":
                    for j in (0, 2):
                        dve.wait_ge(pe_full, f0 + j + 1)
                        for k in (2 * j, 2 * j + 1):
                            src = ps[:, j, (k % 2) * TOK:(k % 2 + 1) * TOK]
                            if k == 5:
                                dve.tensor_copy(kpeT, src)
                            else:
                                dve.tensor_scalar(turn_a_dst(k), src, col(C_QN + l * 3 + k if k < 3 else C_KVN + l * 2 + k - 3),
                                                  None, ALU.mult)
                elif name == "heads_a":
                    for j in range(3):
                        dve.wait_ge(pe_full, f0 + j + 1)
                        dve.tensor_copy(qnT[:, 2 * j:2 * j + 2, :], ps[:, j, :].rearrange("p (h n) -> p h n", h=2))
                    dve.wait_ge(pe_full, f0 + 7)
                    dve.tensor_copy(qr[:, 0, :], ps[:, 6, 0:384])
                elif name == "values_a":
                    q = qr.rearrange("p t (h d) -> p t h d", h=A_HEADS)
                    rope(dve, q[:, :, :, 0:32], q[:, :, :, 32:64], A_HEADS, 32,
                         lambda i, w: (act[:, 3072 + i * 384:] if i < 2 else r2[:, 4096 + (i - 2) * 384:])[:, 0:w])
                elif name == "turn_ar":
                    turn_evac(dve, "dve", f0, lambda k: qrT[:, k, :], blocks=3)
                elif name in ("attend_a", "attend_b", "attend_c"):
                    attend_dve(dve, name[-1].upper(), l)
                elif name == "prep_b":
                    def tmp(i, w):
                        return r2[:, i * 160:][:, 0:w]
                    for c0 in (QB0, KB0):
                        rope(dve, heads_of(c0, B_HEADS, HD, 0, 16), heads_of(c0, B_HEADS, HD, 16, 32), B_HEADS, 16, tmp)
                    rope(dve, heads_of(QI0, IDX_HEADS, IDX_DIM, 0, 8), heads_of(QI0, IDX_HEADS, IDX_DIM, 8, 16), IDX_HEADS, 8, tmp)
                    rope(dve, heads_of(KI0, 1, IDX_DIM, 0, 8), heads_of(KI0, 1, IDX_DIM, 8, 16), 1, 8, tmp)
                    dve.tensor_copy(kid[:, :, 0:64], zt[:, :, KI0:KI0 + IDX_DIM])
                    dve.tensor_copy(kid[:, :, 64:128], zt[:, :, KI0:KI0 + IDX_DIM])
                elif name in ("turn_b", "turn_c"):
                    turn_evac(dve, "dve", f0, turn_ab_dst, blocks=10)
                elif name == "turn_idx":
                    turn_evac(dve, "dve", f0, lambda k: act[:, 2560 + k * TOK:][:, 0:TOK], blocks=5)
                elif name == "index":
                    dve.wait_ge(rel_done, l * 6 + 6)
                    for hd in range(IDX_HEADS):
                        for s in range(NT):
                            nk, m0 = keys(s)
                            wi = zt[:, s, WI0 + hd:WI0 + hd + 1]
                            o = score[:, m0:m0 + nk]
                            if hd == 0:
                                a = dve.tensor_scalar(o, rel[:, hd, m0:m0 + nk], wi, None, ALU.mult)
                            else:
                                a = dve.scalar_tensor_tensor(o, rel[:, hd, m0:m0 + nk], wi, o, ALU.mult, ALU.add)
                        chain(dve, "dve", a)
                elif name == "select":
                    TAKEN = -3e38
                    chain(dve, "dve", dve.tensor_tensor(kept, score, mask[:, :], ALU.add))
                    for r in range(N_SEL // 8):
                        for s in range(NT):
                            nk, m0 = keys(s)
                            a = dve.max(st[:, 90 + 8 * s:98 + 8 * s], kept[:, m0:m0 + nk])
                        chain(dve, "dve", a)
                        for s in range(NT):
                            nk, m0 = keys(s)
                            a = dve.match_replace(kept[:, m0:m0 + nk], st[:, 90 + 8 * s:98 + 8 * s], kept[:, m0:m0 + nk], TAKEN)
                        chain(dve, "dve", a)
                    chain(dve, "dve", dve.tensor_scalar(kept, kept, -2e38, NEG, ALU.is_gt, ALU.mult))
                    dve.tensor_tensor(score, kept, mask[:, :], ALU.add)
                elif name == "prep_c":
                    for c0 in (QC0, KC0):
                        rope(dve, heads_of(c0, 2 * C_HEADS, C_QK, 0, 8), heads_of(c0, 2 * C_HEADS, C_QK, 8, 16), 2 * C_HEADS, 8,
                             lambda i, w: r2[:, 4096 + i * 160:][:, 0:w])
                elif name == "norm_c":
                    for s in range(NT):
                        a = dve.tensor_tensor(norm_c_sq[:, s], norm_c_in[:, s], norm_c_in[:, s], ALU.mult)
                    chain(dve, "dve", a)
                    chain(dve, "dve", dve.tensor_reduce(rs[:, 0:10], r2[:, 0:1280].rearrange("p (h d) -> p h d", d=HD), AX_X, ALU.add))
                    chain(dve, "dve", dve.tensor_scalar(rs[:, 0:10], rs[:, 0:10], 1.0 / HD, None, ALU.mult))
                    rms_dve(dve, rms_k[n], 10)
                    for s in range(NT):
                        for hd in range(C_HEADS):
                            g0 = GC0 + hd * HD
                            a = dve.scalar_tensor_tensor(norm_c_sq[:, s, hd], norm_c_in[:, s, hd], rs[:, 64 + s * 5 + hd:65 + s * 5 + hd],
                                                         bc[:, B_SUB + l * HD:][:, 0:HD], ALU.mult, ALU.mult)
                        chain(dve, "dve", a)
                        dve.tensor_tensor(zt[:, s, GC0:GC0 + 640], r2[:, s * 640:(s + 1) * 640], zt[:, s, GC0:GC0 + 640], ALU.mult)
                elif name in ("turn_mix", "turn_h"):
                    turn_evac(dve, "dve", f0, lambda k: xT[:, k, :])
                elif name == "project_out":
                    base = PAIR0[f"out{l}"]
                    with dve.Fori(0, 2) as i:
                        for par in range(2):
                            dve.wait_ge(piece_used[par * 4 + 3], i + (base + 1))
                            for s in range(NT):
                                hc = ht[:, s, bass.ds(i * 1024 + par * CHUNK, CHUNK)]
                                dve.tensor_tensor(hc, ps[:, par * 2 + s, :], hc, ALU.add).then_inc(evac[par], 1)
                elif name == "embed":
                    for c in range(4):
                        dve.wait_ge(pe_full, f0 + 2 * c + 2)
                        dve.tensor_copy(z[:, D + c * CHUNK:][:, 0:CHUNK], ps[:, 2 * c + 1, :])
                elif name == "gate":
                    base, e0 = PAIR0[f"gate{l}"], EVAC0[f"gate{l}"]
                    for i in range(2):
                        for par in range(2):
                            c = 2 * i + par
                            dve.wait_ge(evac[par], e0 + 2 * i + 2)
                            for s in range(NT):
                                g = r2[:, (par * 2 + s) * 512:][:, 0:512]
                                a = dve.tensor_tensor(g, g, ztiles(s)[:, c * CHUNK:(c + 1) * CHUNK], ALU.mult)
                            chain(dve, "dve", a)
                            for s in range(NT):
                                g = r2[:, (par * 2 + s) * 512:][:, 0:512]
                                hc = ht[:, s, c * CHUNK:(c + 1) * CHUNK]
                                a = dve.tensor_tensor(hc, hc, g, ALU.add)
                            a.then_inc(gate_used, 1)
                elif name == "final1":
                    rms_dve(dve, rms_k[n], NT, sums=rms_s[n])
                    dve.wait_ge(aux, aux_at["final"])
                    for s in range(NT):
                        dve.scalar_tensor_tensor(ht[:, s, :], ht[:, s, :], rs[:, 64 + s:65 + s], act[:, W0:W0 + D], ALU.mult, ALU.mult)
                elif name == "ada":
                    base = PAIR0["ada"]
                    dve.wait_ge(bias_in, 32)
                    with dve.Fori(0, 12) as i:
                        for par in range(2):
                            dve.wait_ge(piece_used[par * 4 + 3], i + (base + 1))
                            zc = z[0:2, bass.ds(i * 1024 + par * CHUNK, CHUNK)]
                            dve.tensor_tensor(zc, ps[0:2, par, :], zc, ALU.add).then_inc(evac[par], 1)
                elif name == "ada_cols":
                    dve.wait_ge(pe_full, f0 + 1)
                    dve.tensor_copy(mask[:, 0:128], ps[:, 0, 0:128])
                elif name == "mod_cols":
                    for m, (g0, sec, r) in enumerate(((C_N1, 1, 0), (C_N1, 1, 1), (C_N2, 3, 0))):
                        chain(dve, "dve", dve.tensor_scalar(modc[:, m, :], adac[:, sec * KT:(sec + 1) * KT, r], 1.0, None, ALU.add))
                        dve.tensor_tensor(modc[:, m, :], modc[:, m, :], cols[:, g0:g0 + KT], ALU.mult)
                elif name == "norm_x":
                    dve.wait_ge(aux, aux_at["ctx"])
                    rms_dve(dve, rms_k[n], 4, sums=rms_s[n])
                    for s in range(NT):
                        dve.tensor_scalar(ztiles(s), ht[:, s, :], rs[:, 64 + s:65 + s], None, ALU.mult)
                        dve.tensor_scalar(r2[:, s * D:(s + 1) * D], r2[:, s * D:(s + 1) * D], rs[:, 66 + s:67 + s], None, ALU.mult)
                elif name == "turn_x":
                    turn_evac(dve, "dve", f0, lambda k: xT[:, k, :], scale=lambda k: modc[:, 0, k:k + 1],
                              bias=lambda k: adac[:, k, 0:1])
                elif name == "turn_ctx":
                    turn_evac(dve, "dve", f0, lambda k: cT[:, k, :], scale=lambda k: modc[:, 1, k:k + 1],
                              bias=lambda k: adac[:, k, 1:2])
                elif name == "gates":
                    chain(dve, "dve", dve.memset(z[:, 0:2048], 0.0))
                    bias = bc[:, B_MGB:B_MGB + 16].rearrange("p (d h) -> p d h", h=M_HEADS)
                    for s in range(4):
                        dve.wait_ge(pe_full, f0 + s + 1)
                        a = dve.tensor_tensor(gpad[:, :, s, 0:P:32], ps[:, s, 0:16].rearrange("p (d h) -> p d h", h=M_HEADS), bias, ALU.add)
                    chain(dve, "dve", a)
                    for d in range(2):
                        dve.scalar_tensor_tensor(z[:, 2304 + 16 * d:2320 + 16 * d].rearrange("p (s h) -> p s h", s=4),
                                                 gpad[:, 2 * d + 1, :, 0:P:32], -1.0, gpad[:, 2 * d + 1, :, 0:P:32], ALU.mult, ALU.max)
                    rd = bc[:, B_RDEC:B_RDEC + 16]
                    dve.scalar_tensor_tensor(z[:, 2336:2352], rd, -1.0, rd, ALU.mult, ALU.max)
                elif name == "gates_log":
                    for d in range(2):
                        f = gpad[:, 2 * d + 1, :, 0:P:32]
                        dve.scalar_tensor_tensor(f, f, 0.0, z[:, 2304 + 16 * d:2320 + 16 * d].rearrange("p (s h) -> p s h", s=4),
                                                 ALU.min, ALU.subtract)
                    rd = bc[:, B_RDEC:B_RDEC + 16]
                    chain(dve, "dve", dve.scalar_tensor_tensor(st[:, 112:128], rd, 0.0, z[:, 2336:2352], ALU.min, ALU.subtract))
                    dve.tensor_scalar(st[:, 112:128], st[:, 112:128], -1e-20, None, ALU.min)
                elif name == "gate_rows":
                    F, I, B, X, M, EN = (0, 1), (2, 3), (5, 6), (7, 8), (9, 10), (11, 12)
                    for dk in range(4):
                        d, kind = dk // 2, dk % 2
                        dst = row((I, F)[kind][d])
                        dve.wait_ge(pe_full, f0 + dk + 1)
                        if d == 0:
                            dve.tensor_copy(dst, ps[:, dk, :])
                        else:
                            dve.tensor_copy(dst[:, 0:TOK], ps[:, dk, TOK - 1::-1])
                            dve.tensor_copy(dst[:, TOK:], ps[:, dk, 2 * TOK - 1:TOK - 1:-1])
                    chain(dve, "dve", dve.memset(row(4), 0.0))
                    for d in range(2):
                        chain(dve, "dve", dve.tensor_tensor_scan(row(B[d]), row(F[d]), row(4), 0.0, ALU.add, ALU.add))
                    for d in range(2):
                        a = dve.tensor_tensor(row(X[d]), row(I[d]), row(B[d]), ALU.subtract)
                    chain(dve, "dve", a)
                    for d in range(2):
                        chain(dve, "dve", dve.tensor_tensor_scan(row(M[d]), row(X[d]), row(X[d]), 0.0, ALU.max, ALU.max))
                    for d in range(2):
                        chain(dve, "dve", dve.tensor_tensor(row(EN[d])[:, TOK:], row(B[d])[:, TOK:], row(M[d])[:, TOK:], ALU.add))
                        dve.tensor_scalar(row(EN[d])[:, TOK:], row(EN[d])[:, TOK:], -1.0, 88.0, ALU.mult, ALU.min)
                    dve.tensor_scalar(negm[:, 0, :], row(M[0])[:, TOK:], -1.0, None, ALU.mult)
                    dve.tensor_scalar(negm[:, 1, :], row(M[1])[:, 2 * TOK - 1:TOK - 1:-1], -1.0, None, ALU.mult)
                    dve.tensor_copy(row(13)[:, 0:TOK], row(X[1])[:, TOK - 1::-1])
                    dve.tensor_copy(row(13)[:, TOK:], row(X[1])[:, 2 * TOK - 1:TOK - 1:-1])
                elif name == "gate_back":
                    for b in range(3):
                        dve.wait_ge(pe_full, f0 + b + 1)
                        dve.tensor_copy(mcols[:, 4 * b:4 * b + 4, :], ps[:, b, :].rearrange("p (i n) -> p i n", i=4)[:, :, 0:P:32])
                elif name == "kv":
                    base = PAIR0["kv"]
                    for i in range(2):
                        for par in range(2):
                            dve.wait_ge(piece_used[par * 4 + 3], i + base + 1)
                            c0 = (2 * i + par) * CHUNK
                            for s in (1, 3):
                                dve.tensor_copy((zt if s < 2 else czt)[:, 1, c0:c0 + CHUNK], ps[:, par * 4 + s, :]).then_inc(evac[par], 1)
                elif name == "mvmk":
                    dve.wait_ge(piece_used[3], PAIR0[name] + 1)
                    for s in (1, 3):
                        dve.tensor_copy((zt if s < 2 else czt)[:, 1, 2048:2560], ps[:, s, :]).then_inc(evac[0], 1)
                    dve.wait_ge(piece_used[7], PAIR0[name] + 1)
                    for b in (1, 3):
                        dve.tensor_copy(raw_x[:, b, :], ps[:, 4 + b, 0:TOK])
                        dve.tensor_copy(raw_c[:, b, :], ps[:, 4 + b, TOK:]).then_inc(evac[1], 1)
                elif name == "mqrq":
                    dve.wait_ge(piece_used[3], PAIR0[name] + 1)
                    for b in (1, 3):
                        dve.tensor_copy(raw_x[:, 4 + b, :], ps[:, b, 0:TOK]).then_inc(evac[0], 1)
                    dve.wait_ge(piece_used[7], PAIR0[name] + 1)
                    for c in range(2):
                        dve.tensor_copy(zt[:, 1, RQ + c * 256:][:, 0:256], ps[:, 5, c * 256:(c + 1) * 256]).then_inc(evac[1], 1)
                elif name == "rgmo":
                    base = PAIR0["rgmo"]
                    for i in range(2):
                        for par in range(2):
                            dve.wait_ge(piece_used[par * 4 + 3], i + base + 1)
                            c0 = RG + (2 * i + par) * CHUNK
                            dve.tensor_copy(zt[:, 1, c0:c0 + CHUNK], ps[:, par * 2 + 1, :]).then_inc(evac[par], 1)
                elif name == "conv":
                    def tap(i, ch):
                        return cols[:, C_CONV + i * 8 + ch:C_CONV + i * 8 + ch + 1]
                    def parts(b):
                        return (raw_x[:, b, :], b + 4 if b < 4 else b - 4) if b < 8 else (raw_c[:, b - 8, :], b - 4)
                    for step in range(3):
                        for b in range(12):
                            x, ch = parts(b)
                            o = conv[:, b, :]
                            if step == 0:
                                a = dve.tensor_scalar(o, x, tap(1, ch), None, ALU.mult)
                            elif step == 1:
                                a = dve.scalar_tensor_tensor(o[:, 1:], x[:, 0:TOK - 1], tap(0, ch), o[:, 1:], ALU.mult, ALU.add)
                            else:
                                a = dve.scalar_tensor_tensor(o[:, 0:TOK - 1], x[:, 1:], tap(2, ch), o[:, 0:TOK - 1], ALU.mult, ALU.add)
                        chain(dve, "dve", a)
                    dve.wait_ge(aux, aux_at["trig2"])
                    def tmp2(i, w):
                        return act[:, 8192 + i * 512:][:, 0:w]
                    for c0 in (RQ, RK):
                        rope(dve, heads_of(c0, R_HEADS, R_DK, 0, 32), heads_of(c0, R_HEADS, R_DK, 32, 64), R_HEADS, 32, tmp2)
                elif name == "turn_r":
                    turn_evac(dve, "dve", f0, lambda k: rT[:, k, :], blocks=12)
                elif name == "retention":
                    def ready(u):
                        dve.wait_ge(re_exp, u + 1)
                        e, w = work[:, 2 * (u % 2), :], work[:, 2 * (u % 2) + 1, :]
                        chain(dve, "dve", dve.tensor_tensor(e, e, w, ALU.add))
                        dve.wait_ge(re_att, u + 1)
                        dve.scalar_tensor_tensor(w, ps[:, u % 2, :], R_DK ** -0.5, e, ALU.mult, ALU.mult).then_inc(re_ready, 1)

                    def done(hd):
                        dve.wait_ge(re_out, 2 * hd + 2)
                        for s in range(NT):
                            a = dve.tensor_copy(zt[:, s, RV + hd * R_DV:RV + (hd + 1) * R_DV], ps[:, 2 + 2 * (hd % 2) + s, 0:R_DV])
                        a.then_inc(re_done, 1)

                    for u in range(2 * R_HEADS):
                        ready(u)
                        if u >= 2 and u % 2 == 0:
                            done(u // 2 - 1)
                    done(R_HEADS - 1)
                elif name == "mlstm":
                    def arg(v):
                        hd, d = v // 2, v % 2
                        dve.wait_ge(ml_att, v + 1)
                        if v >= 2:
                            dve.wait_ge(ml_out, v - 1)
                        w = work[:, 2 * (v % 2):2 * (v % 2) + 2, :].rearrange("p b n -> p (b n)")
                        for i in range(4):
                            a = dve.tensor_scalar(w[:, i * TOK:(i + 1) * TOK], ps[:, 4 + v % 2, 0:TOK], mcols[:, 4 * d + i, hd:hd + 1], 0.0,
                                                  ALU.add, ALU.min)
                        a.then_inc(ml_arg, 1)

                    def ready(v):
                        hd, d = v // 2, v % 2
                        dve.wait_ge(ml_exp, v + 1)
                        lat = work[:, 2 * (v % 2) + 1, :]
                        chain(dve, "dve", dve.scalar_tensor_tensor(lat, dist[:, d, 2:4, :].rearrange("p i n -> p (i n)"), 1e29, lat,
                                                                   ALU.is_lt, ALU.mult))
                        for half in range(2):
                            w = work[:, 2 * (v % 2) + half, :]
                            a = dve.scalar_tensor_tensor(w, ps[:, 2 * (hd % 2) + half, :], M_DK ** -0.5, w, ALU.mult, ALU.mult)
                        a.then_inc(ml_ready, 1)

                    def done(v):
                        hd, d = v // 2, v % 2
                        dve.wait_ge(ml_out, v + 1)
                        y0 = (RK if hd < 2 else RQ) + (hd % 2) * M_DV
                        den = ps[:, 6:8, M_DV]
                        clamp = mcols[:, 8 + 2 * d:10 + 2 * d, hd]
                        a, b = st[:, 80:82], st[:, 82:84]
                        chain(dve, "dve", dve.tensor_copy(b, den))
                        chain(dve, "dve", dve.scalar_tensor_tensor(a, b, -1.0, b, ALU.mult, ALU.max))
                        chain(dve, "dve", dve.tensor_tensor(a, a, clamp, ALU.max))
                        chain(dve, "dve", dve.reciprocal(a, a))
                        for s in range(NT):
                            y = zt[:, s, y0:y0 + M_DV]
                            if d == 0:
                                m = dve.tensor_scalar(y, ps[:, 6 + s, 0:M_DV], a[:, s:s + 1], None, ALU.mult)
                            else:
                                m = dve.scalar_tensor_tensor(y, ps[:, 6 + s, 0:M_DV], a[:, s:s + 1], y, ALU.mult, ALU.add)
                        m.then_inc(ml_done, 1)

                    for v in range(2 * M_HEADS + 2):
                        if v < 2 * M_HEADS:
                            arg(v)
                        if 1 <= v <= 2 * M_HEADS:
                            ready(v - 1)
                        if v >= 2:
                            done(v - 2)
                elif name == "head_norm":
                    N = NT * 1024
                    yr = zt[:, :, RV:RV + 1024].rearrange("p t (h d) -> p t h d", h=R_HEADS)
                    ym = [zt[:, :, c0:c0 + 512].rearrange("p t (h d) -> p t h d", h=2) for c0 in (RK, RQ)]
                    groups = [(yr, R_HEADS, R_DV, 0)] + [(y, 2, M_DV, 16 + 4 * i) for i, y in enumerate(ym)]
                    mean = st[:, 0:24]
                    def stat(tile_, c0, heads):
                        return tile_[:, c0:c0 + NT * heads].rearrange("p (t h) -> p t h", t=NT)
                    for y, heads, dv, c0 in groups:
                        a = dve.tensor_reduce(stat(st, c0, heads), y, AX_X, ALU.add)
                    chain(dve, "dve", a)
                    dve.tensor_scalar(st[:, 0:16], st[:, 0:16], 1.0 / R_DV, None, ALU.mult)
                    chain(dve, "dve", dve.tensor_scalar(st[:, 16:24], st[:, 16:24], 1.0 / M_DV, None, ALU.mult))
                    for y, heads, dv, c0 in groups:
                        a = dve.tensor_tensor(y, y, stat(st, c0, heads).unsqueeze(3).to_broadcast([P, NT, heads, dv]), ALU.subtract)
                    chain(dve, "dve", a)
                    sq = [act[:, o:o + NT * heads * dv].rearrange("p (t h d) -> p t h d", t=NT, h=heads)
                          for o, (y, heads, dv, c0) in zip((4096, 6144, 7168), groups)]
                    for q, (y, heads, dv, c0) in zip(sq, groups):
                        a = dve.tensor_tensor(q, y, y, ALU.mult)
                    chain(dve, "dve", a)
                    for q, (y, heads, dv, c0) in zip(sq, groups):
                        a = dve.tensor_reduce(stat(rs, c0, heads), q, AX_X, ALU.add)
                    chain(dve, "dve", a)
                    dve.tensor_scalar(rs[:, 0:16], rs[:, 0:16], 1.0 / R_DV, None, ALU.mult)
                    chain(dve, "dve", dve.tensor_scalar(rs[:, 16:24], rs[:, 16:24], 1.0 / M_DV, None, ALU.mult))
                    rms_dve(dve, rms_k[n], 24)
                    for y, heads, dv, c0 in groups:
                        a = dve.tensor_tensor(y, y, stat(rs, 64 + c0, heads).unsqueeze(3).to_broadcast([P, NT, heads, dv]), ALU.mult)
                    chain(dve, "dve", a)
                    for s in range(NT):
                        dve.tensor_tensor(zt[:, s, RG:RG + 1024], zt[:, s, RG:RG + 1024], zt[:, s, RV:RV + 1024], ALU.mult)
                        for i, c0 in enumerate((RK, RQ)):
                            m0 = MO + i * 512
                            dve.tensor_tensor(zt[:, s, m0:m0 + 512], zt[:, s, m0:m0 + 512], zt[:, s, c0:c0 + 512], ALU.mult)
                elif name == "turn_y":
                    turn_evac(dve, "dve", f0, lambda k: yT[:, k, :])
                elif name == "merge":
                    for n4 in range(4):
                        c = 3 * n4 + 2
                        dve.wait_ge(mg_sig, 2 * n4 + 2)
                        dve.wait_ge(piece_used[(c % 2) * 4 + 3], PAIR0["merge"] + c // 2 + 1)
                        g = [r2[:, 2048 + i * 512:2560 + i * 512] for i in range(4)]
                        for i in range(4):
                            a = dve.tensor_tensor(g[i], g[i], ps[:, 4 + i, :], ALU.mult)
                        chain(dve, "dve", a)
                        for s in range(NT):
                            a = dve.tensor_tensor(ztiles(s)[:, n4 * CHUNK:(n4 + 1) * CHUNK], g[s], g[2 + s], ALU.add)
                        a.then_inc(mg_sum, 1)
                elif name == "turn_m":
                    turn_evac(dve, "dve", f0, lambda k: xT[:, k, :])
                elif name == "out2":
                    base = PAIR0["out2"]
                    dve.wait_ge(aux, aux_at["gt1"])
                    for i in range(2):
                        for par in range(2):
                            c = 2 * i + par
                            dve.wait_ge(piece_used[par * 4 + 3], i + base + 1)
                            for s in range(NT):
                                a = dve.tensor_tensor(ztiles(s)[:, c * CHUNK:(c + 1) * CHUNK], ps[:, par * 2 + s, :], gt[:, c * CHUNK:(c + 1) * CHUNK], ALU.mult)
                                a.then_inc(evac[par], 1)
                            dve.wait_ge(evac[par], EVAC0["out2"] + 2 * i + 2)
                            for s in range(NT):
                                hc = ht[:, s, c * CHUNK:(c + 1) * CHUNK]
                                dve.tensor_tensor(hc, hc, ztiles(s)[:, c * CHUNK:(c + 1) * CHUNK], ALU.add)
                elif name == "norm_2":
                    rms_dve(dve, rms_k[n], NT, sums=rms_s[n])
                    for s in range(NT):
                        dve.tensor_scalar(ztiles(s), ht[:, s, :], rs[:, 64 + s:65 + s], None, ALU.mult)
                elif name == "turn_2":
                    turn_evac(dve, "dve", f0, lambda k: xT[:, k, :], scale=lambda k: modc[:, 2, k:k + 1],
                              bias=lambda k: adac[:, 2 * KT + k, 0:1])
                elif name == "query":
                    for i in range(2):
                        for par in range(2):
                            dve.wait_ge(piece_used[par * 4 + 3], PAIR0[name] + i + 1)
                            for b in (1, 3):
                                dve.tensor_copy(qT[:, (2 * i + par) * 4 + b, :], ps[:, par * 4 + b, 0:TOK]).then_inc(evac[par], 1)
                elif name == "key_scores":
                    for b in range(4):
                        dve.wait_ge(pe_full, f0 + 5 + b)
                        dve.tensor_copy(S[:, 1, 4 * b:4 * b + 4, :], ps[:, 4 + b, :].rearrange("p (b n) -> p b n", b=4))
                elif name == "top_keys":
                    def top16(values_, vals, idx, rows):
                        for r in range(2):
                            for x in rows:
                                a = dve.max(vals(x)[:, 8 * r:8 * r + 8], values_(x))
                            chain(dve, "dve", a)
                            for x in rows:
                                a = dve.max_index(idx(x)[:, 8 * r:8 * r + 8], vals(x)[:, 8 * r:8 * r + 8], values_(x))
                            chain(dve, "dve", a)
                            if r == 0:
                                for x in rows:
                                    a = dve.match_replace(values_(x), vals(x)[:, 0:8], values_(x), -3e38)
                                chain(dve, "dve", a)
                    rows = [(s, b) for s in range(NT) for b in range(16)]
                    top16(lambda x: S[:, x[0], x[1], :], lambda x: sv[:, x[0], x[1], :], lambda x: si[:, x[0], x[1], :], rows)
                    dve.tensor_copy(z[:, 5120:5632], z[:, 4608:5120].bitcast(U32))
                    svp = z[:, 4096:4608].rearrange("p (s h f n) -> p s h f n", s=NT, h=P_HEADS, f=2)
                    for s in range(NT):
                        a = dve.tensor_tensor(cand[:, s].rearrange("p h (i j) -> p h i j", i=16),
                                              svp[:, s, :, 0, :].unsqueeze(3).to_broadcast([P, P_HEADS, 16, 16]),
                                              svp[:, s, :, 1, :].unsqueeze(2).to_broadcast([P, P_HEADS, 16, 16]), ALU.add)
                    chain(dve, "dve", a)
                    rows = [(s, b) for s in range(NT) for b in range(P_HEADS)]
                    top16(lambda x: cand[:, x[0], x[1], :], lambda x: bs[:, x[0], x[1], :], lambda x: bjv[:, x[0], x[1], :], rows)
                    for s in range(NT):
                        dve.tensor_tensor(sel[2][:, s, :].rearrange("p (h n) -> p h n", n=16), bs[:, s], bs[:, s, :, 0:1].to_broadcast([P, P_HEADS, 16]),
                                          ALU.subtract)
                elif name == "experts_of":
                    for s in range(NT):
                        a = dve.tensor_reduce(st[:, 8 * s:8 * s + 8], sel[2][:, s, :].rearrange("p (h n) -> p h n", n=16), AX_X, ALU.add)
                    chain(dve, "dve", a)
                    chain(dve, "dve", dve.reciprocal(st[:, 0:16], st[:, 0:16]))
                    for s in range(NT):
                        g = sel[2][:, s, :].rearrange("p (h n) -> p h n", n=16)
                        dve.tensor_tensor(g, g, st[:, 8 * s:8 * s + 8].unsqueeze(2).to_broadcast([P, P_HEADS, 16]), ALU.mult)
                    dve.tensor_scalar(j12[0], bj, 4, None, ALU.logical_shift_right)
                    chain(dve, "dve", dve.tensor_scalar(j12[1], bj, 15, None, ALU.bitwise_and))
                    for i in range(2):
                        a = dve.tensor_copy(z[:, 10752 + i * 256:11008 + i * 256], j12[i])
                    chain(dve, "dve", a)
                    sifp = z[:, 5120:5632].rearrange("p (s h f n) -> p s h f n", s=NT, h=P_HEADS, f=2)
                    pos16 = iota[:, 0:16].unsqueeze(1).to_broadcast([P, P, 16])
                    for s in range(NT):
                        for f in range(2):
                            chain(dve, "dve", dve.tensor_tensor(hot, j12f[f][:, s, :].unsqueeze(2).to_broadcast([P, P, 16]), pos16, ALU.is_equal))
                            h4 = hot.rearrange("p (h k) j -> p h k j", h=P_HEADS)
                            chain(dve, "dve", dve.tensor_tensor(h4, h4, sifp[:, s, :, f, :].unsqueeze(2).to_broadcast([P, P_HEADS, 16, 16]), ALU.mult))
                            chain(dve, "dve", dve.tensor_reduce(sel[f][:, s, :], hot, AX_X, ALU.add))
                elif name == "turn_sel":
                    for m in range(3):
                        dve.wait_ge(pe_full, f0 + m + 1)
                        dve.tensor_copy(selT[:, m, :], ps[:, m, 0:TOK])
                elif name == "spread":
                    def block_of_tokens(b, first):
                        for i in range(SB):
                            if i >= 8 or not first:
                                dve.wait_ge(hot_used, b * SB + (i - 7))
                            dve.tensor_scalar(hots[:, i % 8, 0, :], iota[:, :], selT[:, 0, bass.ds(b * SB + i, 1)],
                                              selT[:, 2, bass.ds(b * SB + i, 1)], ALU.is_equal, ALU.mult)
                            dve.tensor_scalar(hots[:, i % 8, 1, :], iota[:, :], selT[:, 1, bass.ds(b * SB + i, 1)], None,
                                              ALU.is_equal).then_inc(hot_made, 1)

                    block_of_tokens(0, True)
                    with dve.Fori(1, TOK // SB) as b:
                        block_of_tokens(b, False)
                elif name == "experts":
                    base = PAIR0["experts"]
                    dve.memset(z[:, 0:4096], 0.0).then_inc(yacc_zero, 1)
                    dve.wait_ge(yacc_zero, 1)
                    with dve.Fori(0, GROUPS // 2) as gg:
                        for par in range(2):
                            dve.wait_ge(slab_full[par], gg * 16 + 16)
                            for b in range(4):
                                dve.wait_ge(hid_act, gg * 8 + (4 * par + b + 1))
                                hb = hid[:, b, :].rearrange("p (b n) -> p b n", n=SB)
                                dve.tensor_tensor(hb, hb, slab[:, par, :, b, :], ALU.mult).then_inc(hid_done, 1)
                            for dc in range(4):
                                if dc < 3:
                                    dve.wait_ge(up_full, gg * 6 + (3 * par + dc + 1))
                                else:
                                    dve.wait_ge(piece_used[7], gg * 2 + (par + base + 1))
                                for s in range(NT):
                                    y = yacc[:, s, dc * CHUNK:(dc + 1) * CHUNK]
                                    a = dve.tensor_tensor(y, y, ps[:, 4 + 2 * (dc % 2) + s, :], ALU.add)
                                a.then_inc(up_read, 1)
                elif name == "final2":
                    dve.wait_ge(aux, aux_at["final2"])
                    for s in range(NT):
                        a = dve.tensor_tensor(yacc[:, s, :], yacc[:, s, :], gt, ALU.mult)
                    chain(dve, "dve", a)
                    for s in range(NT):
                        a = dve.tensor_tensor(ht[:, s, :], ht[:, s, :], yacc[:, s, :], ALU.add)
                    a.then_inc(h_sum, 1)
                    rms_dve(dve, rms_k[n], NT, sums=rms_s[n])
                    for s in range(NT):
                        dve.scalar_tensor_tensor(ht[:, s, :], ht[:, s, :], rs[:, 64 + s:65 + s], act[:, 4096:4096 + D], ALU.mult, ALU.mult)
                end(dve, "dve")


def pack_chunks(w):
    n = w.shape[1] // CHUNK
    return w.reshape(4, PIECE_KT, P, n, CHUNK).transpose(3, 0, 2, 1, 4).reshape(n, 4, P, PIECE)


def lay_out(i):
    f32 = np.float32
    w0 = KI0 + IDX_DIM
    order = np.concatenate([np.arange(w0), np.arange(w0 + IDX_HEADS, ZW), np.arange(w0, w0 + IDX_HEADS)])
    parts = []
    for l in range(DEPTH):
        parts += [pack_chunks(i["w_in"][l][:, order[:WI0]]), pack_chunks(i["w_o"][l]), pack_chunks(i["w_pg"][l])]
    parts.append(pack_chunks(i["w_ada_2"][0]))
    w2 = i["w_in_2"][0]
    rq, rk, rv, rg = w2[:, 0:512], w2[:, 512:1024], w2[:, 1024:2048], w2[:, 2048:3072]
    mq, mk, mv, mo = w2[:, 3072:3584], w2[:, 3584:4096], w2[:, 4096:5120], w2[:, 5120:6144]
    wg, gr, gm = w2[:, 6144:6160], w2[:, 6160:6160 + D], w2[:, 6160 + D:6160 + 2 * D]
    for w in (rk, rv, mv, mk, mq, rq, rg, mo):
        parts.append(pack_chunks(w))
    outs = np.concatenate([i["w_ret_out_2"][0], i["w_mlstm_out_2"][0]])
    merge = np.stack([pack_chunks(w) for w in (gr, gm, outs)], axis=1)
    parts += [merge.reshape(-1, 4, P, PIECE), pack_chunks(i["w_out_2"][0]), pack_chunks(i["peer_query_2"][0])]
    down = i["peer_down_2"][0].reshape(P_KEYS, GROUPS, 4, 4, PIECE_KT, P).transpose(1, 3, 5, 4, 2, 0)
    up = i["peer_up_2"][0].reshape(P_KEYS, GROUPS, 4, D).transpose(1, 2, 0, 3)
    experts = np.empty((GROUPS, 2, 4, P, PIECE), f32)
    experts[:, 0] = down.reshape(GROUPS, 4, P, PIECE)
    experts[:, 1] = up
    parts.append(experts.reshape(-1, 4, P, PIECE))
    stream = np.concatenate(parts).reshape(N_PAIRS, PIECES, P, PIECE)

    def columns(v):
        return v.reshape(-1, P).T

    cols = np.concatenate([columns(i["norm_g"]), columns(i["q_norm_g"]), columns(i["kv_norm_g"]), columns(i["norm1_g_2"]),
                           columns(i["norm2_g_2"]), columns(i["m_conv_2"][0]),
                           np.stack([columns(i["c_2"][0]), columns(i["c_ctx_2"])], axis=2).reshape(P, 2 * KT)], axis=1)
    bc = np.concatenate([i["subln_g"].reshape(-1), i["m_gate_bias_2"][0].reshape(-1), i["ret_decay_2"][0].reshape(-1)])
    tail = i["w_in"][:, :, w0:w0 + IDX_HEADS].reshape(DEPTH, KT, P, IDX_HEADS).transpose(2, 0, 1, 3).reshape(P, -1)
    wg = wg.reshape(KT, P, 16).transpose(1, 0, 2).reshape(P, -1)
    nope = [np.arange(h * (HD + A_ROPE), h * (HD + A_ROPE) + HD) for h in range(A_HEADS)]
    rot = [np.arange(h * (HD + A_ROPE) + HD, (h + 1) * (HD + A_ROPE)) for h in range(A_HEADS)]
    key = [np.arange(h * 2 * HD, h * 2 * HD + HD) for h in range(A_HEADS)]
    val = [np.arange(h * 2 * HD + HD, (h + 1) * 2 * HD) for h in range(A_HEADS)]
    inv_freq = (1.0 / (f32(500000.0) ** (np.arange(32, dtype=f32) * f32(2.0 / 64)))).astype(f32)
    freq = (f32(10000.0) ** (-np.arange(16, dtype=f32) / f32(16))).astype(f32)
    tok = np.arange(TOK)
    ang = np.concatenate([(tok // 64)[:, None].astype(f32) * freq, (tok % 64)[:, None].astype(f32) * freq], axis=1)
    trig2 = np.stack([np.cos(ang), np.sin(ang)]).reshape(2, NT, P, 32).transpose(2, 0, 1, 3).astype(f32)
    s, c = tok[:, None], tok[None, :]
    far = 1e30
    dist = np.stack([np.concatenate([TOK + c - s, np.where(c >= s, c - s, far)]),
                     np.concatenate([TOK - c + s, np.where(s >= c, s - c, far)])])
    dist = dist.reshape(2, 4, P, TOK).transpose(2, 0, 1, 3).reshape(P, -1).astype(f32)
    return dict(
        x=i["x"][0], positions=i["positions"][0].reshape(NT, P).T, cols=cols, bc=bc,
        wsmall=np.concatenate([tail, wg], axis=1), inv_freq=inv_freq,
        lam=np.concatenate([i[k].reshape(-1) for k in ("lam_q1", "lam_k1", "lam_q2", "lam_k2")]),
        w_uq=i["w_uq"][:, :, np.concatenate(nope + rot)], w_ukv=i["w_ukv"][:, :, np.concatenate(key + val)],
        w_ple=i["w_ple"], pT=i["p"][:, 0].transpose(0, 2, 1), final_g=i["final_g"], trig2=trig2,
        ctx=i["ctx_2"][0], wgates=wg.reshape(P, KT, 16), dist=dist, b_ada=i["b_ada_2"],
        keysT=i["peer_keys_2"][0].reshape(16, P_KEYS, P).transpose(2, 0, 1).reshape(P, -1), final_g2=i["final_g_2"],
        stream=stream)


def kernel(**inputs):
    import concourse.bacc as bacc
    from concourse.bass_utils import run_bass_kernel_spmd

    laid = {k: np.ascontiguousarray(v) for k, v in lay_out({k: np.asarray(v) for k, v in inputs.items()}).items()}
    nc = bacc.Bacc("TRN2", target_bir_lowering=False, num_devices=1)
    arrays, t = {}, {}
    for name, a in laid.items():
        arrays[f"in_{name}_dram"] = a
        t[name] = nc.dram_tensor(f"in_{name}_dram", a.shape, mybir.dt.from_np(a.dtype), kind="ExternalInput").ap()
    t["out"] = nc.dram_tensor("out_0_dram", (TOK, D), F32, kind="ExternalOutput").ap()
    build_program(nc, t)
    r = run_bass_kernel_spmd(nc, [arrays], core_ids=[0])
    return r.results[0]["out_0_dram"].reshape(1, TOK, D)
```

```python
from contextlib import ExitStack

import numpy as np

import concourse.bass as bass
from concourse import mybir

F32 = mybir.dt.float32
F32R = mybir.dt.float32r
I32 = mybir.dt.int32
U32 = mybir.dt.uint32
ALU = mybir.AluOpType
ACT = mybir.ActivationFunctionType
AX_X = mybir.AxisListType.X

P = 128
D = 2048
TOK = 256
NT = TOK // P
KT = D // P
PIECE_KT = 4
CHUNK = 512
PIECE = PIECE_KT * CHUNK
PIECES = 4
DEPTH = 2
EPS = 1e-6
NEG = -1e30
TWO_PI = 2 * np.pi

A_Q, A_KV, A_ROPE, A_HEADS, HD = 384, 256, 64, 6, 128
B_HEADS, C_HEADS, IDX_HEADS, IDX_DIM, C_QK = 5, 5, 8, 64, 64
CQ0 = 0
CKV0 = CQ0 + A_Q
KR0 = CKV0 + A_KV
GA0 = KR0 + A_ROPE
QB0 = GA0 + A_HEADS * HD
KB0 = QB0 + B_HEADS * HD
VB0 = KB0 + B_HEADS * HD
QI0 = VB0 + B_HEADS * HD
KI0 = QI0 + IDX_HEADS * IDX_DIM
GB0 = KI0 + IDX_DIM
QC0 = GB0 + B_HEADS * HD
KC0 = QC0 + C_HEADS * HD
VC0 = KC0 + C_HEADS * HD
GC0 = VC0 + C_HEADS * HD
WI0 = GC0 + C_HEADS * HD
ZW = WI0 + IDX_HEADS
N_SEL = 64
MIX0 = (GA0, GB0, GC0)
MIXW = (A_HEADS * HD, B_HEADS * HD, C_HEADS * HD)

R_HEADS, R_DK, R_DV = 8, 64, 128
M_HEADS, M_DK, M_DV = 4, 128, 256
P_HEADS, P_KEYS, P_TOPK = 8, 128, 16
GROUPS = 32

STREAM = []
for _l in range(DEPTH):
    STREAM += [(f"in{_l}", 7, 2), (f"out{_l}", 2, 2), (f"gate{_l}", 2, 2)]
STREAM += [("ada", 12, 1), ("kv", 2, 4), ("mvmk", 1, 4), ("mqrq", 1, 4), ("rgmo", 2, 2), ("merge", 6, 0),
           ("out2", 2, 2), ("query", 2, 4), ("experts", GROUPS, 0)]
PAIR0, EVAC0, _pair, _evac = {}, {}, 0, 0
for _n, _p, _e in STREAM:
    PAIR0[_n], EVAC0[_n] = _pair, _evac
    _pair += _p
    _evac += _p * _e
N_CHUNKS = 2 * _pair

C_NORM = 0
C_QN = C_NORM + DEPTH * KT
C_KVN = C_QN + DEPTH * 3
C_N1 = C_KVN + DEPTH * 2
C_N2 = C_N1 + KT
C_CONV = C_N2 + KT
C_SILU = C_CONV + 3 * 8
NCOLS = C_SILU + 2 * KT
B_SUB = 0
B_MGB = B_SUB + DEPTH * HD
B_RDEC = B_MGB + 16
NBC = B_RDEC + 16


def build_program(nc, t):
    ctx = ExitStack()
    with ctx:
        def sb(name, shape, dt=F32):
            return ctx.enter_context(nc.sbuf_tensor(name, shape, dt))

        def sem(name):
            return ctx.enter_context(nc.semaphore(name))

        def two_views(name, shape):
            with nc.sbuf_tensor(name, shape, F32) as plain:
                pass
            return plain, sb(name + "_r", shape, F32R)

        ring, ring_r = two_views("ring", [P, PIECES, PIECE])
        high = sb("high", [P, PIECES, PIECE], F32R)
        silu_high = sb("silu_high", [P, 2 * KT], F32R)
        h = sb("h", [P, NT * D])
        act, act_r = two_views("act", [P, 4096 + 6528])
        z, z_r = two_views("z", [P, NT * ZW])
        r2, r2_r = two_views("r2", [P, 5120])
        ident = sb("ident", [P, P])
        iota = sb("iota", [P, P])
        mask = sb("mask", [P, P + TOK])
        trig = sb("trig", [P, 2, NT, 32])
        cols, cols_r = two_views("cols", [P, NCOLS])
        bc = sb("bc", [P, NBC])
        wsmall = sb("wsmall", [P, 512])
        st = sb("st", [P, 128])
        rs = sb("rs", [P, 96])
        sti = sb("sti", [P, 2], I32)
        ones = sb("ones", [P, P])
        mcols = sb("mcols", [P, 12, M_HEADS])
        ps = ctx.enter_context(nc.psum_tensor("ps", [P, 8, 512], F32))

        xT = act[:, 0:KT * TOK].rearrange("p (k n) -> p k n", k=KT)
        xT_r = act_r[:, 0:KT * TOK].rearrange("p (k n) -> p k n", k=KT)
        W0 = KT * TOK
        wtail = wsmall[:, 0:256].rearrange("p (l k n) -> p l k n", l=DEPTH, k=KT)
        wgates = wsmall[:, 256:512].rearrange("p (k n) -> p k n", k=KT)
        zt = z[:, :].rearrange("p (t n) -> p t n", t=NT)
        ht = h[:, :].rearrange("p (t n) -> p t n", t=NT)

        piece_full = [sem(f"piece_full{j}") for j in range(PIECES)]
        piece_high = [sem(f"piece_high{j}") for j in range(PIECES)]
        piece_low = [sem(f"piece_low{j}") for j in range(PIECES)]
        x_high = sem("x_high")
        piece_used = [sem(f"piece_used{j}") for j in range(PIECES)]
        evac = [sem(f"evac{i}") for i in range(2)]
        stage_done = {e: sem(f"stage_done_{e}") for e in ("pe", "act", "dve", "pool")}
        pe_full = sem("pe_full")
        dve_step = sem("dve_step")
        act_step = sem("act_step")
        pool_step = sem("pool_step")
        rms_sums = sem("rms_sums")
        rms_inv = sem("rms_inv")
        rms_root = sem("rms_root")
        att_scores = sem("att_scores")
        att_logits = sem("att_logits")
        att_probs = sem("att_probs")
        att_mixed = sem("att_mixed")
        att_turned = sem("att_turned")
        att_pT = sem("att_pT")
        att_out = sem("att_out")
        att_done = sem("att_done")
        rel_done = sem("rel_done")
        gate_sig = sem("gate_sig")
        gate_used = sem("gate_used")
        consts = sem("consts")
        consts_p = sem("consts_p")
        aux = sem("aux")
        stored = sem("stored")
        made = sem("made")

        n_step = {"act": 0, "dve": 0, "pool": 0}
        step_sem = {"act": act_step, "dve": dve_step, "pool": pool_step}

        def chain(eng, who, ins):
            n_step[who] += 1
            ins.then_inc(step_sem[who], 1)
            eng.wait_ge(step_sem[who], n_step[who])

        ALL = ("pe", "act", "dve", "pool")

        def begin(eng, n, wait_for=ALL):
            if n >= 1:
                for who in wait_for:
                    eng.wait_ge(stage_done[who], n)

        def end(eng, who):
            eng.drain().then_inc(stage_done[who], 1)

        def count(c, mul, add):
            i, off = c
            return i * (2 * mul) + (off * mul + add)

        def weights(j, c0, n):
            return high[:, j, c0:c0 + n], ring_r[:, j, c0:c0 + n]

        def product(pe, out, lhs, rhs, start, stop):
            pe.matmul(out, lhs[0], rhs[0], start=start, stop=False)
            pe.matmul(out, lhs[0], rhs[1], start=False, stop=False)
            return pe.matmul(out, lhs[1], rhs[0], start=False, stop=stop)

        def split_act(sc, c, js):
            for j in js:
                sc.wait_ge(piece_full[j], count(c, 16, 16))
                sc.copy(high[:, j, :], ring[:, j, :]).then_inc(piece_high[j], 1)

        def split_dve(dve, c, js):
            for j in js:
                dve.wait_ge(piece_high[j], count(c, 1, 1))
                dve.tensor_tensor(ring_r[:, j, :], ring[:, j, :], high[:, j, :], ALU.subtract).then_inc(piece_low[j], 1)

        def stream_split(eng, split, name, n_pairs, evacuate=None, looped=True):
            def chunk(i, par):
                c = (i, 2 * PAIR0[name] + par)
                nxt = (i, c[1] + 1)
                split(eng, c, (3,))
                split(eng, nxt, range(3))
                if evacuate is not None:
                    eng.wait_ge(piece_used[3], count(c, 1, 1))
                    evacuate(i, par)
            if looped:
                with eng.Fori(0, n_pairs) as i:
                    for par in range(2):
                        chunk(i, par)
            else:
                for i in range(n_pairs):
                    for par in range(2):
                        chunk(i, par)

        def stream_pe(pe, name, n_pairs, evacs, lhs, M=P, tiles=NT):
            base, e0 = PAIR0[name], EVAC0[name]
            def body(i):
                for par in range(2):
                    if base > 0 or not isinstance(i, int) or i > 0:
                        pe.wait_ge(evac[par], i * evacs + e0)
                    for k in range(KT):
                        j = k // PIECE_KT
                        if k % PIECE_KT == 0:
                            pe.wait_ge(piece_low[j], count((i, 2 * base + par), 1, 1))
                        w = weights(j, (k % PIECE_KT) * CHUNK, CHUNK)
                        for s in range(tiles):
                            mm = product(pe, ps[0:M, par * tiles + s, :], lhs(s, k), w, k == 0, k == KT - 1)
                        if k % PIECE_KT == PIECE_KT - 1:
                            mm.then_inc(piece_used[j], 1)
            if base == 0 and e0 == 0:
                body(0)
                with pe.Fori(1, n_pairs) as i:
                    body(i)
            else:
                with pe.Fori(0, n_pairs) as i:
                    body(i)

        def turn_pe(pe, src, blocks=KT, tiles=NT):
            for j in range((blocks + 1) // 2):
                for k in range(2 * j, min(2 * j + 2, blocks)):
                    for s in range(tiles):
                        mm = pe.transpose(ps[:, j, (k % 2) * TOK + s * P:(k % 2) * TOK + (s + 1) * P], src(s, k), ident[:, :])
                mm.then_inc(pe_full, 1)

        def turn_evac(eng, who, base, dst, blocks=KT, scale=None, bias=None):
            for j in range((blocks + 1) // 2):
                if (j % 2 == 0) != (who == "dve"):
                    continue
                eng.wait_ge(pe_full, base + j + 1)
                for k in range(2 * j, min(2 * j + 2, blocks)):
                    src = ps[:, j, (k % 2) * TOK:(k % 2 + 1) * TOK]
                    s = None if scale is None else scale(k)
                    b = None if bias is None else bias(k)
                    if who == "dve":
                        if s is None:
                            eng.tensor_copy(dst(k), src)
                        elif b is None:
                            eng.tensor_scalar(dst(k), src, s, None, ALU.mult)
                        else:
                            eng.tensor_scalar(dst(k), src, s, b, ALU.mult, ALU.add)
                    elif s is None:
                        eng.copy(dst(k), src)
                    elif b is None:
                        eng.activation(dst(k), src, ACT.Copy, scale=s)
                    else:
                        eng.activation(dst(k), src, ACT.Identity, scale=s, bias=b)


        def rms_act(act_, k, sources, n, have_sums=False):
            if not have_sums:
                for c, (src, width, junk) in enumerate(sources):
                    last = act_.activation(junk, src, ACT.Square, scale=float(width) ** -0.5, accum_out=rs[:, c:c + 1])
                last.then_inc(rms_sums, 1)
            act_.wait_ge(rms_inv, k + 1)
            act_.activation(rs[:, 64:64 + n], rs[:, 32:32 + n], ACT.Sqrt).then_inc(rms_root, 1)

        def rms_dve(dve, k, n, sums=None):
            if sums is not None:
                dve.wait_ge(rms_sums, sums + 1)
            chain(dve, "dve", dve.tensor_scalar(rs[:, 32:32 + n], rs[:, 0:n], EPS, None, ALU.add))
            dve.reciprocal(rs[:, 32:32 + n], rs[:, 32:32 + n]).then_inc(rms_inv, 1)
            dve.wait_ge(rms_root, k + 1)

        def rope(dve, x1, x2, heads, half, tmp, out1=None, out2=None):
            cs, sn = (trig[:, f, :, 0:32:32 // half].unsqueeze(2).to_broadcast([P, NT, heads, half]) for f in range(2))
            a, b, c, d = (tmp(i, NT * heads * half).rearrange("p (t h d) -> p t h d", t=NT, h=heads) for i in range(4))
            dve.tensor_tensor(a, x1, cs, ALU.mult)
            dve.tensor_tensor(b, x2, sn, ALU.mult)
            dve.tensor_tensor(c, x2, cs, ALU.mult)
            chain(dve, "dve", dve.tensor_tensor(d, x1, sn, ALU.mult))
            dve.tensor_tensor(x1 if out1 is None else out1, a, b, ALU.subtract)
            chain(dve, "dve", dve.tensor_tensor(x2 if out2 is None else out2, c, d, ALU.add))

        def heads_of(col, heads, width, lo, hi):
            return zt[:, :, col:col + heads * width].rearrange("p t (h d) -> p t h d", h=heads)[:, :, :, lo:hi]

        va = r2[:, 0:1536].rearrange("p (t n) -> p t n", t=NT)
        qr = r2[:, 1536:2304].rearrange("p (t n) -> p t n", t=NT)
        qrT = r2[:, 2304:3072].rearrange("p (k n) -> p k n", k=3)
        kd = r2[:, 3072:3328].rearrange("p (t n) -> p t n", t=NT)
        kpeT = r2[:, 3328:3584]
        ckvT = r2[:, 3584:4096].rearrange("p (k n) -> p k n", k=2)
        qnT = act[:, 0:1536].rearrange("p (k n) -> p k n", k=6)
        knT = act[:, 1536:3072].rearrange("p (k n) -> p k n", k=6)
        cqT = act[:, 3072:3840].rearrange("p (k n) -> p k n", k=3)
        w_uq = act[:, W0:W0 + 3456].rearrange("p (k n) -> p k n", k=3)
        w_ukv = act[:, W0 + 3456:W0 + 6528].rearrange("p (k n) -> p k n", k=2)
        w_ple = act[:, W0:W0 + 4096].rearrange("p (k n) -> p k n", k=2)
        pT = act[:, W0 + 4096:W0 + 4608].rearrange("p (k n) -> p k n", k=2)
        hqT = act[:, 0:1280].rearrange("p (k n) -> p k n", k=5)
        hkT = act[:, 1280:2560].rearrange("p (k n) -> p k n", k=5)
        qiT = act[:, 2560:3584].rearrange("p (k n) -> p k n", k=4)
        kiT = act[:, 3584:3840]
        score = r2[:, 0:384]
        rel = r2[:, 384:3456].rearrange("p (h n) -> p h n", h=IDX_HEADS)
        kept = r2[:, 3456:3840]
        kid = r2[:, 3840:4096].rearrange("p (t n) -> p t n", t=NT)

        def keys(s):
            return (s + 1) * P, s * P

        def units(heads):
            return [(hd, s) for hd in range(heads) for s in range(NT)]

        UNITS = {"A": units(A_HEADS), "B": units(B_HEADS), "C": units(C_HEADS)}
        UNIT0 = {}
        nu = 0
        for l in range(DEPTH):
            for m in "ABC":
                UNIT0[m, l] = nu
                nu += len(UNITS[m])
        MIXED0 = {l: l * len(UNITS["C"]) for l in range(DEPTH)}
        SCALE = {"A": (A_ROPE + HD) ** -0.5, "B": HD ** -0.5, "C": C_QK ** -0.5}

        def scbuf(m, slot, sub=0):
            return r2[:, slot * 512 + sub * 256:][:, 0:256] if m == "C" else r2[:, 4096 + slot * 256:4352 + slot * 256]

        def prbuf(m, slot, sub=0):
            return r2[:, 1024 + slot * 512 + sub * 256:][:, 0:256] if m == "C" else r2[:, 4608 + slot * 256:4864 + slot * 256]

        def mixbuf(slot):
            return r2[:, 2048 + slot * 256:2304 + slot * 256]

        def pTbuf(m, slot):
            b = 2560 if m == "C" else 1536
            return r2[:, b + slot * 256:b + slot * 256 + 256]

        def values(m, j, hd):
            return va[:, j, hd * HD:(hd + 1) * HD] if m == "A" else zt[:, j, (VB0 if m == "B" else VC0) + hd * HD:][:, 0:HD]

        def attend_pe(pe, m, l):
            u0, us = UNIT0[m, l], UNITS[m]
            subs = 2 if m == "C" else 1

            def scores(u):
                hd, s = us[u]
                nk, _ = keys(s)
                if u >= 2:
                    pe.wait_ge(att_logits, u0 + u - 1)
                q0, q1 = s * P, (s + 1) * P
                b = u % 2
                if m == "A":
                    r = (hd % 2) * A_ROPE
                    pe.matmul(ps[:, b, 0:nk], qnT[:, hd, q0:q1], knT[:, hd, 0:nk], start=True, stop=False)
                    mm = pe.matmul(ps[:, b, 0:nk], qrT[r:r + A_ROPE, hd // 2, q0:q1], kpeT[r:r + A_ROPE, 0:nk],
                                   start=False, stop=True)
                elif m == "B":
                    mm = pe.matmul(ps[:, b, 0:nk], hqT[:, hd, q0:q1], hkT[:, hd, 0:nk], start=True, stop=True)
                else:
                    for c in range(2):
                        r = c * C_QK
                        mm = pe.matmul(ps[:, 2 * b + c, 0:nk], hqT[r:r + C_QK, hd, q0:q1], hkT[r:r + C_QK, hd, 0:nk],
                                       start=True, stop=True)
                mm.then_inc(att_scores, 1)

            def turn(u):
                _, s = us[u]
                if m == "C":
                    pe.wait_ge(att_mixed, MIXED0[l] + u + 1)
                else:
                    pe.wait_ge(att_probs, u0 + u + 1)
                if u >= 2:
                    pe.wait_ge(att_pT, u0 + u - 1)
                src = mixbuf(u % 2) if m == "C" else prbuf(m, u % 2)
                for j in range(s + 1):
                    mm = pe.transpose(ps[:, 4 + u % 2, j * P:(j + 1) * P], src[:, j * P:(j + 1) * P], ident[:, :])
                mm.then_inc(att_turned, 1)

            def out(u):
                hd, s = us[u]
                pe.wait_ge(att_pT, u0 + u + 1)
                if u >= 2:
                    pe.wait_ge(att_done, u0 + u - 1)
                for j in range(s + 1):
                    mm = pe.matmul(ps[:, 6 + u % 2, 0:HD], pTbuf(m, u % 2)[:, j * P:(j + 1) * P], values(m, j, hd),
                                   start=(j == 0), stop=(j == s))
                mm.then_inc(att_out, 1)

            n = len(us)
            for u in range(n + 2):
                if u < n:
                    scores(u)
                if 1 <= u <= n:
                    turn(u - 1)
                if u >= 2:
                    out(u - 2)

        def attend_act(act_, m, l):
            u0, us = UNIT0[m, l], UNITS[m]

            def probs(u):
                _, s = us[u]
                nk, _ = keys(s)
                act_.wait_ge(att_logits, u0 + u + 1)
                if u >= 2:
                    if m == "C":
                        act_.wait_ge(att_mixed, MIXED0[l] + u - 1)
                    else:
                        act_.wait_ge(att_turned, u0 + u - 1)
                for c in range(2 if m == "C" else 1):
                    k = 2 * (u % 2) + c
                    last = act_.activation(prbuf(m, u % 2, c)[:, 0:nk], scbuf(m, u % 2, c)[:, 0:nk], ACT.Exp,
                                           bias=st[:, 34 + k:35 + k], accum_out=st[:, 38 + k:39 + k])
                last.then_inc(att_probs, 1)

            def turned(u):
                _, s = us[u]
                act_.wait_ge(att_turned, u0 + u + 1)
                if u >= 2:
                    act_.wait_ge(att_out, u0 + u - 1)
                act_.copy(pTbuf(m, u % 2)[:, 0:(s + 1) * P], ps[:, 4 + u % 2, 0:(s + 1) * P]).then_inc(att_pT, 1)

            n = len(us)
            for u in range(n + 1):
                if u < n:
                    probs(u)
                if u >= 1:
                    turned(u - 1)

        def attend_dve(dve, m, l):
            u0, us = UNIT0[m, l], UNITS[m]
            subs = 2 if m == "C" else 1
            masks = score if m == "B" else mask

            def logits(u):
                _, s = us[u]
                nk, m0 = keys(s)
                dve.wait_ge(att_scores, u0 + u + 1)
                if u >= 2:
                    dve.wait_ge(att_probs, u0 + u - 1)
                for c in range(subs):
                    k = 2 * (u % 2) + c
                    bank = 2 * (u % 2) + c if m == "C" else u % 2
                    last = dve.tensor_tensor_reduce(scbuf(m, u % 2, c)[:, 0:nk], ps[:, bank, 0:nk], masks[:, m0:m0 + nk],
                                                    SCALE[m], NEG, ALU.add, ALU.max, st[:, 30 + k:31 + k])
                chain(dve, "dve", last)
                k = 2 * (u % 2)
                dve.tensor_scalar(st[:, 34 + k:34 + k + subs], st[:, 30 + k:30 + k + subs], -1.0, None, ALU.mult)\
                   .then_inc(att_logits, 1)

            def mix(u):
                _, s = us[u]
                nk, _ = keys(s)
                k = 2 * (u % 2)
                dve.wait_ge(att_probs, u0 + u + 1)
                chain(dve, "dve", dve.reciprocal(st[:, 42 + k:44 + k], st[:, 38 + k:40 + k]))
                if u >= 2:
                    dve.wait_ge(att_turned, u0 + u - 1)
                dve.tensor_scalar(prbuf(m, u % 2, 0)[:, 0:nk], prbuf(m, u % 2, 0)[:, 0:nk], st[:, 42 + k:43 + k], None, ALU.mult)
                chain(dve, "dve", dve.tensor_scalar(st[:, 43 + k:44 + k], st[:, 43 + k:44 + k], st[:, 60 + l:61 + l], None, ALU.mult))
                dve.scalar_tensor_tensor(mixbuf(u % 2)[:, 0:nk], prbuf(m, u % 2, 1)[:, 0:nk], st[:, 43 + k:44 + k],
                                         prbuf(m, u % 2, 0)[:, 0:nk], ALU.mult, ALU.add).then_inc(att_mixed, 1)

            def done(u):
                hd, s = us[u]
                dve.wait_ge(att_out, u0 + u + 1)
                src = ps[:, 6 + u % 2, 0:HD]
                if m == "C":
                    dve.tensor_copy(zt[:, s, QC0 + hd * HD:QC0 + (hd + 1) * HD], src).then_inc(att_done, 1)
                    return
                k = 2 * (u % 2)
                g = zt[:, s, (GA0 if m == "A" else GB0) + hd * HD:][:, 0:HD]
                dve.scalar_tensor_tensor(g, src, st[:, 46 + u % 2:47 + u % 2], g, ALU.mult, ALU.mult).then_inc(att_done, 1)

            def sums(u):
                dve.wait_ge(att_probs, u0 + u + 1)
                k = 2 * (u % 2)
                chain(dve, "dve", dve.reciprocal(st[:, 46 + u % 2:47 + u % 2], st[:, 38 + k:39 + k]))

            n = len(us)
            for u in range(n + 2):
                if m == "C" and 1 <= u <= n:
                    mix(u - 1)
                if u < n:
                    logits(u)
                if u >= 2:
                    done(u - 2)
                if m != "C" and 1 <= u <= n:
                    sums(u - 1)

        STAGES = [("setup", 0), ("angles", 0)]
        for l in range(DEPTH):
            STAGES += [("norm", l), ("turn_in", l), ("split_in", l), ("project", l), ("prep_a", l), ("turn_a", l), ("heads_a", l),
                       ("values_a", l), ("turn_ar", l), ("attend_a", l), ("prep_b", l), ("turn_b", l), ("turn_idx", l),
                       ("index", l), ("select", l), ("attend_b", l), ("prep_c", l), ("turn_c", l), ("attend_c", l),
                       ("norm_c", l), ("turn_mix", l), ("split_mix", l), ("project_out", l), ("turn_h", l), ("split_h", l),
                       ("embed", l), ("gate", l)]
        STAGES += [(name, 0) for name in (
            "final1", "silu_c", "split_c", "ada", "ada_cols", "mod_cols", "norm_x", "turn_x", "turn_ctx",
            "gates", "gates_exp", "gates_log", "gate_rows", "gate_clamp", "gate_back",
            "split_xc", "kv", "mvmk", "mqrq", "rgmo", "join", "conv", "conv_silu", "turn_r", "retention", "mlstm", "head_norm",
            "turn_y", "split_xy", "merge", "turn_m", "split_m", "out2", "norm_2", "turn_2", "split_2", "query", "key_scores", "top_keys",
            "soft", "experts_of", "turn_sel", "spread", "experts", "final2")]
        FULL_OF = {"turn_in": 8, "split_in": 2, "turn_a": 3, "heads_a": 8, "values_a": 4, "turn_ar": 2, "turn_b": 5,
                   "turn_idx": 3, "index": 6, "turn_c": 5, "turn_mix": 8, "turn_h": 8, "embed": 8,
                   "ada_cols": 1, "turn_x": 8, "turn_ctx": 8, "gates": 4, "gate_rows": 4, "gate_back": 3, "turn_r": 6,
                   "turn_y": 8, "turn_m": 8, "turn_2": 8, "key_scores": 8, "turn_sel": 3}
        full, _f = [], 0
        for name, _ in STAGES:
            full.append(_f)
            _f += FULL_OF.get(name, 0)
        RMS_OF = {"norm": (1, 1), "prep_a": (1, 1), "norm_c": (1, 0), "final1": (1, 1), "norm_x": (1, 1),
                  "head_norm": (1, 0), "norm_2": (1, 1), "final2": (1, 1)}
        rms_k, rms_s, _k, _s = [], [], 0, 0
        for name, _ in STAGES:
            rms_k.append(_k)
            rms_s.append(_s)
            _k += RMS_OF.get(name, (0, 0))[0]
            _s += RMS_OF.get(name, (0, 0))[1]

        def ztiles(s):
            return z[:, s * D:(s + 1) * D]

        def col(c):
            return cols[:, c:c + 1]

        MIX_COL = [MIX0[0] + i * HD for i in range(6)] + [MIX0[1] + i * HD for i in range(5)] + \
                  [MIX0[2] + i * HD for i in range(5)]
        norm_c_in = zt[:, :, QC0:QC0 + C_HEADS * HD].rearrange("p t (h d) -> p t h d", h=C_HEADS)
        norm_c_sq = r2[:, 0:NT * C_HEADS * HD].rearrange("p (t h d) -> p t h d", t=NT, h=C_HEADS)

        def turn_ab_src(m):
            q0, k0 = (QB0, KB0) if m == "B" else (QC0, KC0)
            return lambda s, k: zt[:, s, (q0 + k * HD if k < 5 else k0 + (k - 5) * HD):][:, 0:HD]

        def turn_ab_dst(k):
            return act[:, k * TOK:(k + 1) * TOK]

        def turn_a_src(s, k):
            return zt[:, s, CQ0 + k * P:][:, 0:P] if k < 5 else kd[:, s, :]

        def turn_a_dst(k):
            return cqT[:, k, :] if k < 3 else ckvT[:, k - 3, :] if k < 5 else kpeT

        def idx_src(s, k):
            return zt[:, s, QI0 + k * P:][:, 0:P] if k < 4 else kid[:, s, :]

        aux_at, _a = {}, 0
        for l in range(DEPTH):
            for what, n in (("a", 2), ("ple", 2)):
                _a += n * 16
                aux_at[what, l] = _a
        _a += 16
        aux_at["final"] = _a
        for what in ("trig2", "wgates", "ctx", "dist", "gt1", "keys", "gt2", "final2"):
            _a += 16
            aux_at[what] = _a

        def tiles_of(area):
            return lambda k: area[:, k * TOK:(k + 1) * TOK]

        high_in, high_mix, high_2 = tiles_of(r2_r), tiles_of(z_r[:, 8192:12288]), tiles_of(act_r[:, 4096:8192])
        zt_r = z_r[:, :].rearrange("p (t n) -> p t n", t=NT)

        def high_x(k):
            return (act_r[:, 8192 + k * TOK:] if k < 9 else zt_r[:, 1, 6144 + (k - 9) * TOK:] if k < 13
                    else zt_r[:, 1, 4096 + (k - 13) * TOK:])[:, 0:TOK]

        def high_xm(k):
            return high_x(k) if k < 13 else act_r[:, 4096 + (k - 13) * TOK:][:, 0:TOK]

        def high_c(k):
            return (zt_r[:, 0, 2560 + k * TOK:] if k < 10 else zt_r[:, 1, 2560 + (k - 10) * TOK:])[:, 0:TOK]

        def pair_of(high_, low_, s, k):
            return high_(k)[:, s * P:(s + 1) * P], low_[:, k, s * P:(s + 1) * P]

        cT = act[:, 4096:8192].rearrange("p (k n) -> p k n", k=KT)
        both = act[:, 0:8192].rearrange("p (s n) -> p s n", s=2)
        czt = r2[:, :].rearrange("p (t n) -> p t n", t=NT)
        RK, RV, MV, RQ, RG, MO, RAW = 0, 512, 1536, 2560, 3072, 4096, 5120
        raw_x = zt[:, 0, RAW:RAW + 2048].rearrange("p (b n) -> p b n", b=8)
        raw_c = zt[:, 1, RAW:RAW + 1024].rearrange("p (b n) -> p b n", b=4)
        conv = act[:, 4096:7168].rearrange("p (b n) -> p b n", b=12)
        rT = act[:, 7168:10240].rearrange("p (b n) -> p b n", b=12)
        dist = zt[:, 0, RAW:RAW + 2048].rearrange("p (d i n) -> p d i n", d=2, i=4)
        work = zt[:, 1, RAW:RAW + 2048].rearrange("p (b n) -> p b n", b=4)
        adac = mask[:, 0:128].rearrange("p (b r) -> p b r", r=2)
        modc = mask[:, 128:176].rearrange("p (m k) -> p m k", m=3)
        SEC = {"sh1": 0, "sc1": 1, "sh2": 3, "sc2": 4}
        SECS = ["sh1", "sc1", "sh2", "sc2"]
        gpad = z[:, 0:2048].rearrange("p (d s n) -> p d s n", d=4, s=4)

        def row(i):
            return z[:, 4096 + i * 512:4608 + i * 512]

        negm = wsmall[:, :].rearrange("p (d n) -> p d n", d=2)
        yT = act[:, 4096:8192].rearrange("p (k n) -> p k n", k=KT)
        cT_r = yT_r = act_r[:, 4096:8192].rearrange("p (k n) -> p k n", k=KT)
        qT = z[:, 8192:12288].rearrange("p (k n) -> p k n", k=KT)
        keysT = r2[:, 0:2048].rearrange("p (b n) -> p b n", b=16)
        gt = act[:, 8192:8192 + D]
        S = z[:, 0:4096].rearrange("p (s b n) -> p s b n", s=NT, b=16)
        sv = z[:, 4096:4608].rearrange("p (s b n) -> p s b n", s=NT, b=16)
        si = z[:, 4608:5120].bitcast(U32).rearrange("p (s b n) -> p s b n", s=NT, b=16)
        sif = z[:, 5120:5632].rearrange("p (s b n) -> p s b n", s=NT, b=16)
        cand = z[:, 5632:9728].rearrange("p (s b n) -> p s b n", s=NT, b=P_HEADS)
        bs = z[:, 9728:9984].rearrange("p (s b n) -> p s b n", s=NT, b=P_HEADS)
        bj = z[:, 9984:10240].bitcast(U32)
        bjv = bj.rearrange("p (s b n) -> p s b n", s=NT, b=P_HEADS)
        j12 = [z[:, 10240 + i * 256:10496 + i * 256].bitcast(U32) for i in range(2)]
        j12f = [z[:, 10752 + i * 256:11008 + i * 256].rearrange("p (s n) -> p s n", s=NT) for i in range(2)]
        sel = [z[:, 11264 + i * 256:11520 + i * 256].rearrange("p (s n) -> p s n", s=NT) for i in range(3)]
        hot = z[:, 12032:14080].rearrange("p (a n) -> p a n", n=P_TOPK)
        selT = r2[:, 4096:4864].rearrange("p (m n) -> p m n", m=3)
        hot1 = r2[:, 1024:2048].rearrange("p (b n) -> p b n", b=8)
        hot2 = r2[:, 2048:4096].rearrange("p (a b n) -> p a b n", a=2, b=8)
        SB = 32
        stage = z[:, 0:8192].rearrange("p (b i n) -> p b i n", b=2, n=SB)
        slab = r2[:, 0:2048].rearrange("p (a b i n) -> p a b i n", a=2, b=TOK // SB, i=4)
        hid = z[:, 4096:6144].rearrange("p (b i n) -> p b i n", b=2, i=4)
        hid_low = z_r[:, 4096:6144].rearrange("p (b i n) -> p b i n", b=2, i=4)
        hid_high = z_r[:, 6144:8192].rearrange("p (b i n) -> p b i n", b=2, i=4)
        yacc = z[:, 0:4096].rearrange("p (t n) -> p t n", t=NT)
        high_y = tiles_of(z_r[:, 4096:8192])
        SPLITS = {"split_in": [(xT, xT_r, high_in)], "split_mix": [(xT, xT_r, high_mix)], "split_h": [(xT, xT_r, high_mix)],
                  "split_xc": [(xT, xT_r, high_x), (cT, cT_r, high_c)], "split_xy": [(xT, xT_r, high_mix), (yT, yT_r, high_y)],
                  "split_m": [(xT, xT_r, high_2)], "split_2": [(xT, xT_r, high_2)]}
        high0, _h = [], 0
        for name, _ in STAGES:
            high0.append(_h)
            _h += KT * len(SPLITS.get(name, ())) + (name == "split_c")

        GT = nc.dram_tensor("gate_matrix", [TOK // SB, P, P, SB], F32).ap()
        GTROWS = nc.dram_tensor("gate_rows", [2, D], F32).ap()

        def expert_chunk(g, off, up):
            base = 2 * PAIR0["experts"]
            if not up:
                return (g * 2, base + 2 * off - 1) if not (isinstance(g, int) and 2 * g + off == 0) else (0, base)
            if isinstance(g, int) and 2 * g + off == GROUPS - 1:
                return (0, base + 2 * GROUPS - 1)
            return (g * 2, base + 2 * off + 2)

        re_att = sem("re_att")
        re_exp = sem("re_exp")
        re_ready = sem("re_ready")
        re_out = sem("re_out")
        re_done = sem("re_done")
        ml_att = sem("ml_att")
        ml_arg = sem("ml_arg")
        ml_exp = sem("ml_exp")
        ml_ready = sem("ml_ready")
        ml_out = sem("ml_out")
        ml_done = sem("ml_done")
        mg_sig = sem("mg_sig")
        mg_sum = sem("mg_sum")
        hot_made = sem("hot_made")
        hot_second = sem("hot_second")
        hot_used = sem("hot_used")
        sp_read = sem("sp_read")
        sp_stored = [sem(f"sp_stored{i}") for i in range(2)]
        slab_full = [sem(f"slab_full{i}") for i in range(2)]
        hid_act = sem("hid_act")
        hid_step = sem("hid_step")
        hid_done = sem("hid_done")
        up_read = sem("up_read")
        yacc_zero = sem("yacc_zero")
        h_sum = sem("h_sum")
        bias_in = sem("bias_in")
        stored_rows = sem("stored_rows")
        result = sem("result")

        block = ctx.enter_context(nc.Block())

        @block.sync
        def _(sp):
            sp.dma_start(ht, t["x"].rearrange("(t p) d -> p t d", p=P)).then_inc(consts, 16)
            sp.dma_start(cols[:, :], t["cols"]).then_inc(consts, 16)
            for j in range(PIECES):
                sp.dma_start(ring[:, j, :], t["stream"][0, j]).then_inc(piece_full[j], 16)
            with sp.Fori(1, N_CHUNKS) as c:
                for j in range(PIECES):
                    sp.wait_ge(piece_used[j], c)
                    sp.dma_start(ring[:, j, :], t["stream"][bass.ds(c, 1), j].rearrange("a p n -> p (a n)"))\
                      .then_inc(piece_full[j], 16)
            sp.wait_ge(stage_done["dve"], len(STAGES))
            sp.dma_start(t["out"].rearrange("(t p) d -> p t d", p=P), ht).then_inc(result, 16)
            sp.wait_ge(result, 16)

        @block.gpsimd
        def _(pool):
            for n, (name, l) in enumerate(STAGES):
                begin(pool, n)
                if name == "setup":
                    pool.dma_start(sti[:, 0:NT], t["positions"]).then_inc(consts_p, 16)
                    pool.dma_start(bc[:, :], t["bc"].partition_broadcast(P)).then_inc(consts_p, 16)
                    pool.dma_start(wsmall[:, :], t["wsmall"]).then_inc(consts_p, 16)
                    pool.dma_start(z[:, 0:32], t["inv_freq"].partition_broadcast(P)).then_inc(consts_p, 16)
                    pool.dma_start(z[:, 512:1024], t["lam"].partition_broadcast(P)).then_inc(consts_p, 16)
                    chain(pool, "pool", pool.memset(ident[:, :], 0.0))
                    pool.affine_select(out=ident[:, :], in_=ident[:, :], compare_op=ALU.not_equal, fill=1.0,
                                       base=0, pattern=[[-1, P]], channel_multiplier=1)
                    pool.memset(ones[:, :], 1.0)
                    pool.iota(iota[:, :], pattern=[[1, P]], base=0, channel_multiplier=0,
                              allow_small_or_imprecise_dtypes=True)
                elif name == "project" and l == 0:
                    pool.dma_start(w_uq, t["w_uq"][0].rearrange("(k p) n -> p k n", p=P)).then_inc(aux, 16)
                    pool.dma_start(w_ukv, t["w_ukv"][0].rearrange("(k p) n -> p k n", p=P)).then_inc(aux, 16)
                elif name == "attend_a":
                    pool.dma_start(w_ple, t["w_ple"][l].rearrange("(k p) n -> p k n", p=P)).then_inc(aux, 16)
                    pool.dma_start(pT, t["pT"][l].rearrange("(k p) n -> p k n", p=P)).then_inc(aux, 16)
                elif name == "gate" and l + 1 < DEPTH:
                    pool.dma_start(w_uq, t["w_uq"][l + 1].rearrange("(k p) n -> p k n", p=P)).then_inc(aux, 16)
                    pool.dma_start(w_ukv, t["w_ukv"][l + 1].rearrange("(k p) n -> p k n", p=P)).then_inc(aux, 16)
                elif name == "final1":
                    pool.dma_start(act[:, W0:W0 + D], t["final_g"].partition_broadcast(P)).then_inc(aux, 16)
                elif name == "silu_c":
                    for r in range(2):
                        pool.dma_start(z[r:r + 1, 0:6 * D], t["b_ada"]).then_inc(bias_in, 16)
                    pool.dma_start(trig[:, :, :, :], t["trig2"]).then_inc(aux, 16)
                    pool.dma_start(wgates, t["wgates"]).then_inc(aux, 16)
                    pool.dma_start(r2[:, 0:4096].rearrange("p (t n) -> p t n", t=NT),
                                   t["ctx"].rearrange("(t p) d -> p t d", p=P)).then_inc(aux, 16)
                elif name == "ada_cols":
                    pool.dma_start(GTROWS[0:1, :], z[0:1, 2 * D:3 * D]).then_inc(stored_rows, 16)
                    pool.dma_start(GTROWS[1:2, :], z[0:1, 5 * D:6 * D]).then_inc(stored_rows, 16)
                    pool.wait_ge(stored_rows, 32)
                elif name == "conv_silu":
                    pool.dma_start(dist.rearrange("p d i n -> p (d i n)"), t["dist"]).then_inc(aux, 16)
                elif name == "merge":
                    pool.dma_start(gt, GTROWS[0].partition_broadcast(P)).then_inc(aux, 16)
                elif name == "turn_m":
                    pool.dma_start(keysT.rearrange("p b n -> p (b n)"), t["keysT"]).then_inc(aux, 16)
                elif name == "spread":
                    for b in range(2):
                        pool.wait_ge(sp_stored[b], 8 * (TOK // SB))
                    pool.dma_start(gt, GTROWS[1].partition_broadcast(P)).then_inc(aux, 16)
                elif name == "experts":
                    def load_slab(g, b):
                        pool.dma_start(slab[:, b].rearrange("p b i n -> p b (i n)"),
                                       GT[:, :, bass.ds(g * 4, 4), :].rearrange("b p i n -> p b (i n)")).then_inc(slab_full[b], 16)
                    load_slab(0, 0)
                    load_slab(1, 1)
                    with pool.Fori(1, GROUPS // 2) as g:
                        for b in range(2):
                            pool.wait_ge(hid_done, g * 2 + (b - 1))
                            load_slab(g * 2 + b, b)
                elif name == "final2":
                    pool.dma_start(act[:, 4096:4096 + D], t["final_g2"].partition_broadcast(P)).then_inc(aux, 16)
                end(pool, "pool")

        @block.tensor
        def _(pe):
            def xTk(s, k):
                return xT[:, k, s * P:(s + 1) * P]

            for n, (name, l) in enumerate(STAGES):
                begin(pe, n)
                if name == "turn_in":
                    turn_pe(pe, lambda s, k: ztiles(s)[:, k * P:(k + 1) * P])
                elif name == "split_in":
                    for s in range(NT):
                        for k in range(KT):
                            mm = pe.matmul(ps[:, 6 + s, 0:IDX_HEADS], xTk(s, k), wtail[:, l, k, :],
                                           start=(k == 0), stop=(k == KT - 1))
                        mm.then_inc(pe_full, 1)
                elif name == "project":
                    stream_pe(pe, f"in{l}", 7, 2, lambda s, k: pair_of(high_in, xT_r, s, k))
                elif name == "turn_a":
                    turn_pe(pe, turn_a_src, blocks=6)
                elif name == "heads_a":
                    pe.wait_ge(aux, aux_at["a", l])
                    for j in range(3):
                        for hd in (2 * j, 2 * j + 1):
                            for k in range(3):
                                mm = pe.matmul(ps[:, j, (hd % 2) * TOK:(hd % 2 + 1) * TOK], w_uq[:, k, hd * HD:(hd + 1) * HD],
                                               cqT[:, k, :], start=(k == 0), stop=(k == 2))
                        mm.then_inc(pe_full, 1)
                    for j in range(3):
                        for hd in (2 * j, 2 * j + 1):
                            for k in range(2):
                                mm = pe.matmul(ps[:, 3 + j, (hd % 2) * TOK:(hd % 2 + 1) * TOK],
                                               w_ukv[:, k, hd * HD:(hd + 1) * HD], ckvT[:, k, :], start=(k == 0), stop=(k == 1))
                        mm.then_inc(pe_full, 1)
                    for s in range(NT):
                        for k in range(3):
                            mm = pe.matmul(ps[:, 6 + s, 0:A_HEADS * A_ROPE], cqT[:, k, s * P:(s + 1) * P],
                                           w_uq[:, k, A_HEADS * HD:], start=(k == 0), stop=(k == 2))
                        mm.then_inc(pe_full, 1)
                elif name == "values_a":
                    for j in range(2):
                        for s in range(NT):
                            for k in range(2):
                                mm = pe.matmul(ps[:, 2 * j + s, 0:384], ckvT[:, k, s * P:(s + 1) * P],
                                               w_ukv[:, k, 768 + j * 384:768 + (j + 1) * 384], start=(k == 0), stop=(k == 1))
                            mm.then_inc(pe_full, 1)
                elif name == "turn_ar":
                    turn_pe(pe, lambda s, k: qr[:, s, k * P:(k + 1) * P], blocks=3)
                elif name in ("attend_a", "attend_b", "attend_c"):
                    attend_pe(pe, name[-1].upper(), l)
                elif name == "turn_b":
                    turn_pe(pe, turn_ab_src("B"), blocks=10)
                elif name == "turn_c":
                    turn_pe(pe, turn_ab_src("C"), blocks=10)
                elif name == "turn_idx":
                    turn_pe(pe, idx_src, blocks=5)
                elif name == "index":
                    for c in range(2):
                        r = c * IDX_DIM
                        for j in range(4):
                            mm = pe.matmul(ps[:, c, j * P:(j + 1) * P], qiT[r:r + IDX_DIM, j, 0:P], kiT[r:r + IDX_DIM, 0:P],
                                           start=True, stop=True)
                        mm.then_inc(pe_full, 1)
                    for c in range(2):
                        r = c * IDX_DIM
                        for j in range(4):
                            mm = pe.matmul(ps[:, 2 + 2 * c + j // 2, (j % 2) * TOK:(j % 2 + 1) * TOK],
                                           qiT[r:r + IDX_DIM, j, P:2 * P], kiT[r:r + IDX_DIM, :], start=True, stop=True)
                            if j % 2:
                                mm.then_inc(pe_full, 1)
                elif name == "turn_mix":
                    turn_pe(pe, lambda s, k: zt[:, s, MIX_COL[k]:][:, 0:HD])
                elif name == "project_out":
                    stream_pe(pe, f"out{l}", 2, 2, lambda s, k: pair_of(high_mix, xT_r, s, k))
                elif name == "turn_h":
                    turn_pe(pe, lambda s, k: ht[:, s, k * P:(k + 1) * P])
                elif name == "embed":
                    pe.wait_ge(aux, aux_at["ple", l])
                    for c in range(4):
                        for s in range(NT):
                            for k in range(2):
                                mm = pe.matmul(ps[:, 2 * c + s, :], pT[:, k, s * P:(s + 1) * P],
                                               w_ple[:, k, c * CHUNK:(c + 1) * CHUNK], start=(k == 0), stop=(k == 1))
                            mm.then_inc(pe_full, 1)
                elif name == "gate":
                    stream_pe(pe, f"gate{l}", 2, 2, lambda s, k: pair_of(high_mix, xT_r, s, k))
                elif name == "ada":
                    stream_pe(pe, "ada", 12, 1, lambda s, k: (silu_high[:, 2 * k:2 * k + 2], cols_r[:, C_SILU + 2 * k:C_SILU + 2 * k + 2]), M=2, tiles=1)
                elif name == "ada_cols":
                    for b in range(4 * KT):
                        c0 = SEC[SECS[b // KT]] * D + (b % KT) * P
                        mm = pe.transpose(ps[:, 0, 2 * b:2 * b + 2], z[0:2, c0:c0 + P], ident[0:2, 0:2])
                    mm.then_inc(pe_full, 1)
                elif name == "turn_x":
                    turn_pe(pe, lambda s, k: ztiles(s)[:, k * P:(k + 1) * P])
                elif name == "turn_ctx":
                    turn_pe(pe, lambda s, k: r2[:, s * D + k * P:][:, 0:P])
                elif name == "gates":
                    for s in range(4):
                        src = (xT if s < 2 else cT)
                        for k in range(KT):
                            mm = pe.matmul(ps[:, s, 0:16], src[:, k, (s % 2) * P:(s % 2 + 1) * P], wgates[:, k, :],
                                           start=(k == 0), stop=(k == KT - 1))
                        mm.then_inc(pe_full, 1)
                elif name == "gate_rows":
                    for dk in range(4):
                        for i, s in enumerate((2, 3, 0, 1)):
                            mm = pe.transpose(ps[:, dk, i * P:(i + 1) * P], gpad[:, dk, s, :], ident[:, :])
                        mm.then_inc(pe_full, 1)
                elif name == "gate_back":
                    for d in range(2):
                        for i in range(4):
                            mm = pe.transpose(ps[:, d, i * P:(i + 1) * P], row((7, 13)[d])[:, i * P:(i + 1) * P], ident[:, :])
                        mm.then_inc(pe_full, 1)
                    for d in range(2):
                        for s in range(NT):
                            c0 = (TOK, 0)[d] + s * P
                            mm = pe.transpose(ps[:, 2, (2 * d + s) * P:(2 * d + s + 1) * P],
                                              row((11, 14)[d])[:, c0:c0 + P], ident[:, :])
                    mm.then_inc(pe_full, 1)
                elif name == "kv":
                    stream_pe(pe, "kv", 2, 4, lambda s, k: pair_of(high_x, xT_r, s, k) if s < 2 else pair_of(high_c, cT_r, s - 2, k), tiles=4)
                elif name in ("mvmk", "mqrq", "query"):
                    for i in range(2 if name == "query" else 1):
                        for par in range(2):
                            chunk = 2 * (PAIR0[name] + i) + par
                            pe.wait_ge(evac[par], EVAC0[name] + 4 * i)
                            if name == "mvmk" and par == 1:
                                pe.wait_ge(evac[0], EVAC0[name] + 4)
                            turned = name == "query" or (name == "mvmk") == (par == 1)
                            high_ = high_2 if name == "query" else high_x
                            for k in range(KT):
                                j = k // PIECE_KT
                                if k % PIECE_KT == 0:
                                    pe.wait_ge(piece_low[j], chunk + 1)
                                flags = (k == 0, k == KT - 1)
                                w0 = (k % PIECE_KT) * CHUNK
                                if turned:
                                    for b in range(4):
                                        wb = weights(j, w0 + b * P, P)
                                        mm = product(pe, ps[:, par * 4 + b, 0:TOK], wb, (high_(k), xT_r[:, k, :]), *flags)
                                        if name == "mvmk":
                                            mm = product(pe, ps[:, b, 0:TOK], wb, (high_c(k), cT_r[:, k, :]), *flags)
                                else:
                                    for s in range(4 if name == "mvmk" else 2):
                                        lhs = pair_of(high_, xT_r, s, k) if s < 2 else pair_of(high_c, cT_r, s - 2, k)
                                        mm = product(pe, ps[:, par * 4 + s, :], lhs, weights(j, w0, CHUNK), *flags)
                                if k % PIECE_KT == PIECE_KT - 1:
                                    mm.then_inc(piece_used[j], 1)
                elif name == "rgmo":
                    stream_pe(pe, "rgmo", 2, 2, lambda s, k: pair_of(high_xm, xT_r, s, k))
                elif name == "turn_r":
                    def src(s, k):
                        if k < 4:
                            return zt[:, s, RQ + k * P:][:, 0:P]
                        return zt[:, s, RK + (k - 4) * P:][:, 0:P] if k < 8 else czt[:, s, RK + (k - 8) * P:][:, 0:P]
                    turn_pe(pe, src, blocks=12)
                elif name == "retention":
                    def att(u):
                        hd, half = u // 2, u % 2
                        r, b = (hd % 2) * R_DK, hd // 2
                        if u >= 2:
                            pe.wait_ge(re_ready, u - 1)
                        keys_ = rT[:, (4 if half else 8) + b, :]
                        for i in range(2):
                            mm = pe.matmul(ps[:, u % 2, i * TOK:(i + 1) * TOK], keys_[r:r + R_DK, i * P:(i + 1) * P],
                                           rT[r:r + R_DK, b, :], start=True, stop=True)
                        mm.then_inc(re_att, 1)

                    def out(u):
                        hd, half = u // 2, u % 2
                        pe.wait_ge(re_ready, u + 1)
                        if half == 0 and hd >= 2:
                            pe.wait_ge(re_done, hd - 1)
                        v = zt if half else czt
                        for s in range(NT):
                            for i in range(2):
                                mm = pe.matmul(ps[:, 2 + 2 * (hd % 2) + s, 0:R_DV],
                                               work[:, 2 * (u % 2) + 1, i * TOK + s * P:i * TOK + (s + 1) * P],
                                               v[:, i, RV + hd * R_DV:RV + (hd + 1) * R_DV],
                                               start=(half == 0 and i == 0), stop=(half == 1 and i == 1))
                        mm.then_inc(re_out, 1)

                    for u in range(2 * R_HEADS + 1):
                        if u < 2 * R_HEADS:
                            att(u)
                        if u >= 1:
                            out(u - 1)
                elif name == "mlstm":
                    def att(v):
                        hd, d = v // 2, v % 2
                        if d == 0:
                            if hd >= 2:
                                pe.wait_ge(ml_ready, 2 * hd - 2)
                            for i in range(4):
                                kT = conv[:, 8 + hd, i * P:(i + 1) * P] if i < 2 else conv[:, hd, (i - 2) * P:(i - 1) * P]
                                pe.matmul(ps[:, 2 * (hd % 2) + i // 2, (i % 2) * TOK:(i % 2 + 1) * TOK], kT, conv[:, 4 + hd, :],
                                          start=True, stop=True)
                        if v >= 2:
                            pe.wait_ge(ml_arg, v - 1)
                        mm = pe.matmul(ps[:, 4 + v % 2, 0:TOK], ones[32 * hd:32 * hd + 1, :], negm[32 * hd:32 * hd + 1, d, :],
                                       start=True, stop=True, tile_position=(32 * hd, 0))
                        mm.then_inc(ml_att, 1)

                    def out(v):
                        hd, d = v // 2, v % 2
                        pe.wait_ge(ml_ready, v + 1)
                        if v >= 1:
                            pe.wait_ge(ml_done, v)
                        w = work[:, 2 * (v % 2):2 * (v % 2) + 2, :].rearrange("p b n -> p (b n)")
                        for s in range(NT):
                            see = [i for i in range(4) if i < 2 or (i - 2 <= s if d == 0 else i - 2 >= s)]
                            for what in range(2):
                                for i in see:
                                    vals = ones[:, 0:1] if what else (czt if i < 2 else zt)[:, i % 2, MV + hd * M_DV:MV + (hd + 1) * M_DV]
                                    dst = ps[:, 6 + s, M_DV:M_DV + 1] if what else ps[:, 6 + s, 0:M_DV]
                                    mm = pe.matmul(dst, w[:, i * TOK + s * P:i * TOK + (s + 1) * P], vals,
                                                   start=(i == see[0]), stop=(i == see[-1]))
                        mm.then_inc(ml_out, 1)

                    for v in range(2 * M_HEADS + 1):
                        if v < 2 * M_HEADS:
                            att(v)
                        if v >= 1:
                            out(v - 1)
                elif name == "turn_y":
                    turn_pe(pe, lambda s, k: zt[:, s, RG + k * P:][:, 0:P])
                elif name == "merge":
                    for n4 in range(4):
                        for which in range(3):
                            c = 3 * n4 + which
                            chunk = 2 * PAIR0["merge"] + c
                            if n4 >= 1 and which == 0:
                                pe.wait_ge(mg_sig, 2 * n4)
                            if n4 >= 1 and which == 2:
                                pe.wait_ge(mg_sum, n4)
                            for k in range(KT):
                                j = k // PIECE_KT
                                if k % PIECE_KT == 0:
                                    pe.wait_ge(piece_low[j], chunk + 1)
                                w = weights(j, (k % PIECE_KT) * CHUNK, CHUNK)
                                for s in range(NT):
                                    if which < 2:
                                        mm = product(pe, ps[:, 2 * which + s, :], pair_of(high_mix, xT_r, s, k), w, k == 0, k == KT - 1)
                                    else:
                                        mm = product(pe, ps[:, 4 + 2 * (k // 8) + s, :], pair_of(high_y, yT_r, s, k), w,
                                                     k % 8 == 0, k % 8 == 7)
                                if k % PIECE_KT == PIECE_KT - 1:
                                    mm.then_inc(piece_used[j], 1)
                elif name == "turn_m":
                    turn_pe(pe, lambda s, k: ztiles(s)[:, k * P:(k + 1) * P])
                elif name == "out2":
                    stream_pe(pe, "out2", 2, 2, lambda s, k: pair_of(high_2, xT_r, s, k))
                elif name == "turn_2":
                    turn_pe(pe, lambda s, k: ztiles(s)[:, k * P:(k + 1) * P])
                elif name == "key_scores":
                    for s in range(NT):
                        for b in range(16):
                            mm = pe.matmul(ps[:, 4 * s + b // 4, (b % 4) * P:(b % 4 + 1) * P], qT[:, b, s * P:(s + 1) * P],
                                           keysT[:, b, :], start=True, stop=True)
                            if b % 4 == 3:
                                mm.then_inc(pe_full, 1)
                elif name == "turn_sel":
                    for m in range(3):
                        for s in range(NT):
                            mm = pe.transpose(ps[:, m, s * P:(s + 1) * P], sel[m][:, s, :], ident[:, :])
                        mm.then_inc(pe_full, 1)
                elif name == "spread":
                    def block_of_tokens(b, first):
                        for i in range(SB):
                            pe.wait_ge(hot_made, b * SB + (i + 1))
                            if i % 8 == 0:
                                pe.wait_ge(hot_second, b * (SB // 8) + (i // 8 + 1))
                            if i % 4 == 0 and not first:
                                pe.wait_ge(sp_read, b * 8 + (i // 4 - 7))
                            mm = pe.matmul(ps[:, i // 4, (i % 4) * P:(i % 4 + 1) * P], hot1[:, i % 8, :], hot2[:, (i // 8) % 2, i % 8, :],
                                           start=True, stop=True)
                            mm.then_inc(hot_used, 1)

                    block_of_tokens(0, True)
                    with pe.Fori(1, TOK // SB) as b:
                        block_of_tokens(b, False)
                elif name == "experts":
                    def down(g, off):
                        c = expert_chunk(g, off, 0)
                        if not (isinstance(g, int) and 2 * g + off == 0):
                            pe.wait_ge(hid_act, g * 2 + off)
                        for k in range(KT):
                            j = k // PIECE_KT
                            if k % PIECE_KT == 0:
                                pe.wait_ge(piece_low[j], count(c, 1, 1))
                            for b in range(4):
                                mm = product(pe, ps[:, b, 0:TOK], weights(j, (k % PIECE_KT) * CHUNK + b * P, P),
                                             (high_2(k), xT_r[:, k, :]), k == 0, k == KT - 1)
                            if k % PIECE_KT == PIECE_KT - 1:
                                mm.then_inc(piece_used[j], 1)

                    def up(g, off):
                        c = expert_chunk(g, off, 1)
                        pe.wait_ge(hid_done, g * 2 + (off + 1))
                        for dc in range(4):
                            pe.wait_ge(piece_low[dc], count(c, 1, 1))
                            if dc >= 2 or not (isinstance(g, int) and 2 * g + off == 0):
                                pe.wait_ge(up_read, g * 8 + (4 * off + dc - 1))
                            for i in range(4):
                                for s in range(NT):
                                    tok = slice(s * P, (s + 1) * P)
                                    mm = product(pe, ps[:, 4 + 2 * (dc % 2) + s, :], (hid_high[:, off % 2, i, tok], hid_low[:, off % 2, i, tok]),
                                                 weights(dc, i * CHUNK, CHUNK), i == 0, i == 3)
                            mm.then_inc(piece_used[dc], 1)

                    down(0, 0)
                    down(0, 1)
                    up(0, 0)
                    down(0, 2)
                    up(0, 1)
                    with pe.Fori(1, GROUPS // 2 - 1) as g:
                        down(g, 1)
                        up(g, 0)
                        down(g, 2)
                        up(g, 1)
                    down(GROUPS // 2 - 1, 1)
                    up(GROUPS // 2 - 1, 0)
                    up(GROUPS // 2 - 1, 1)
                end(pe, "pe")

        @block.scalar
        def _(sc):
            for n, (name, l) in enumerate(STAGES):
                begin(sc, n)
                f0 = full[n]
                if name == "angles":
                    sc.activation(trig[:, 1, :, :], z[:, 128:192].rearrange("p (t n) -> p t n", t=NT), ACT.Sin)
                    sc.activation(trig[:, 0, :, :], z[:, 192:256].rearrange("p (t n) -> p t n", t=NT), ACT.Sin)
                    sc.activation(st[:, 64:68], st[:, 68:72], ACT.Exp)
                    split_act(sc, (0, 0), range(3))
                elif name == "norm":
                    rms_act(sc, rms_k[n], [(ht[:, s, :], D, z[:, 2 * D + s * D:][:, 0:D]) for s in range(NT)], NT)
                elif name == "turn_in":
                    turn_evac(sc, "act", f0, lambda k: xT[:, k, :], scale=lambda k: col(C_NORM + l * KT + k))
                elif name in SPLITS:
                    for x, x_r, high_ in SPLITS[name]:
                        for k in range(KT):
                            sc.copy(high_(k), x[:, k, :]).then_inc(x_high, 1)
                elif name == "project":
                    stream_split(sc, split_act, f"in{l}", 7, lambda i, par:
                                 sc.copy(zt[:, 0, bass.ds(i * 1024 + par * CHUNK, CHUNK)], ps[:, par * 2, :]).then_inc(evac[par], 1))
                elif name == "prep_a":
                    junk = [act[:, 0:A_Q], act[:, A_Q:2 * A_Q], act[:, 1024:1024 + A_KV], act[:, 1536:1536 + A_KV]]
                    rms_act(sc, rms_k[n], [(zt[:, s, CQ0:CQ0 + A_Q], A_Q, junk[s]) for s in range(NT)] +
                            [(zt[:, s, CKV0:CKV0 + A_KV], A_KV, junk[2 + s]) for s in range(NT)], 4)
                    for g0, w in zip(MIX0, MIXW):
                        sc.activation(zt[:, :, g0:g0 + w], zt[:, :, g0:g0 + w], ACT.Silu)
                elif name == "turn_a":
                    turn_evac(sc, "act", f0, turn_a_dst, blocks=6,
                              scale=lambda k: col(C_QN + l * 3 + k if k < 3 else C_KVN + l * 2 + k - 3))
                elif name == "heads_a":
                    for j in (3, 4, 5):
                        sc.wait_ge(pe_full, f0 + j + 1)
                        sc.copy(knT[:, 2 * j - 6:2 * j - 4, :], ps[:, j, :].rearrange("p (h n) -> p h n", h=2))
                    sc.wait_ge(pe_full, f0 + 8)
                    sc.copy(qr[:, 1, :], ps[:, 7, 0:384])
                elif name == "values_a":
                    for j in range(2):
                        sc.wait_ge(pe_full, f0 + 2 * j + 2)
                        sc.copy(va[:, 1, j * 384:(j + 1) * 384], ps[:, 2 * j + 1, 0:384])
                        sc.copy(va[:, 0, j * 384:(j + 1) * 384], ps[:, 2 * j, 0:384])
                elif name == "turn_ar":
                    turn_evac(sc, "act", f0, lambda k: qrT[:, k, :], blocks=3)
                elif name in ("attend_a", "attend_b", "attend_c"):
                    attend_act(sc, name[-1].upper(), l)
                elif name in ("turn_b", "turn_c"):
                    turn_evac(sc, "act", f0, turn_ab_dst, blocks=10)
                elif name == "turn_idx":
                    turn_evac(sc, "act", f0, lambda k: act[:, 2560 + k * TOK:][:, 0:TOK], blocks=5)
                elif name == "index":
                    for c in range(2):
                        sc.wait_ge(pe_full, f0 + c + 1)
                        sc.activation(rel[:, c:8:2, 0:P], ps[:, c, :].rearrange("p (h n) -> p h n", h=4), ACT.Relu)\
                          .then_inc(rel_done, 1)
                    for c in range(2):
                        for j in range(2):
                            b = 2 + 2 * c + j
                            sc.wait_ge(pe_full, f0 + b + 1)
                            sc.activation(rel[:, 4 * j + c:4 * j + c + 3:2, P:], ps[:, b, :].rearrange("p (h n) -> p h n", h=2), ACT.Relu)\
                              .then_inc(rel_done, 1)
                elif name == "norm_c":
                    rms_act(sc, rms_k[n], None, NT * C_HEADS, have_sums=True)
                elif name == "turn_mix":
                    turn_evac(sc, "act", f0, lambda k: xT[:, k, :])
                elif name == "turn_h":
                    turn_evac(sc, "act", f0, lambda k: xT[:, k, :])
                elif name == "embed":
                    for c in range(4):
                        sc.wait_ge(pe_full, f0 + 2 * c + 1)
                        sc.copy(z[:, c * CHUNK:(c + 1) * CHUNK], ps[:, 2 * c, :])
                elif name == "project_out":
                    stream_split(sc, split_act, f"out{l}", 2)
                elif name == "gate":
                    def sigmoids(i, par):
                        c = 2 * i + par
                        if c >= 2:
                            sc.wait_ge(gate_used, l * 4 + c - 1)
                        for s in range(NT):
                            sc.activation(r2[:, (par * 2 + s) * 512:][:, 0:512], ps[:, par * 2 + s, :], ACT.Sigmoid).then_inc(evac[par], 1)
                    stream_split(sc, split_act, f"gate{l}", 2, sigmoids, looped=False)
                elif name == "final1":
                    rms_act(sc, rms_k[n], [(ht[:, s, :], D, z[:, 2 * D + s * D:][:, 0:D]) for s in range(NT)], NT)
                elif name == "silu_c":
                    sc.activation(cols[:, C_SILU:C_SILU + 2 * KT], cols[:, C_SILU:C_SILU + 2 * KT], ACT.Silu)
                elif name == "split_c":
                    sc.copy(silu_high[:, :], cols[:, C_SILU:C_SILU + 2 * KT]).then_inc(x_high, 1)
                elif name == "ada":
                    stream_split(sc, split_act, "ada", 12)
                elif name == "norm_x":
                    sc.wait_ge(aux, aux_at["ctx"])
                    rms_act(sc, rms_k[n], [(ht[:, s, :], D, z[:, 2 * D + s * D:][:, 0:D]) for s in range(NT)] +
                            [(r2[:, s * D:(s + 1) * D], D, z[:, 4 * D + s * D:][:, 0:D]) for s in range(NT)], 4)
                elif name == "turn_x":
                    turn_evac(sc, "act", f0, lambda k: xT[:, k, :], scale=lambda k: modc[:, 0, k:k + 1],
                              bias=lambda k: adac[:, k, 0:1])
                elif name == "turn_ctx":
                    turn_evac(sc, "act", f0, lambda k: cT[:, k, :], scale=lambda k: modc[:, 1, k:k + 1],
                              bias=lambda k: adac[:, k, 1:2])
                elif name == "gates_exp":
                    chain(sc, "act", sc.activation(z[:, 2304:2352], z[:, 2304:2352], ACT.Exp, scale=-1.0))
                    sc.activation(z[:, 2304:2352], z[:, 2304:2352], ACT.Ln, bias=1.0)
                elif name == "gate_clamp":
                    sc.activation(row(11)[:, TOK:], row(11)[:, TOK:], ACT.Exp)
                    sc.activation(row(14)[:, 0:TOK], row(12)[:, 2 * TOK - 1:TOK - 1:-1], ACT.Exp)
                elif name == "kv":
                    def out_kv(i, par):
                        for s in (0, 2):
                            sc.copy((zt if s < 2 else czt)[:, 0, (2 * i + par) * CHUNK:][:, 0:CHUNK], ps[:, par * 4 + s, :]).then_inc(evac[par], 1)
                    stream_split(sc, split_act, "kv", 2, out_kv, looped=False)
                elif name == "mvmk":
                    def out_m(i, par):
                        if par == 0:
                            for s in (0, 2):
                                sc.copy((zt if s < 2 else czt)[:, 0, 2048:2560], ps[:, s, :]).then_inc(evac[0], 1)
                        else:
                            for b in (0, 2):
                                sc.copy(raw_x[:, b, :], ps[:, 4 + b, 0:TOK])
                                sc.copy(raw_c[:, b, :], ps[:, b, 0:TOK]).then_inc(evac[1], 1)
                    stream_split(sc, split_act, "mvmk", 1, out_m, looped=False)
                elif name == "mqrq":
                    def out_q(i, par):
                        if par == 0:
                            for b in (0, 2):
                                sc.copy(raw_x[:, 4 + b, :], ps[:, b, 0:TOK]).then_inc(evac[0], 1)
                        else:
                            for c in range(2):
                                sc.copy(zt[:, 0, RQ + c * 256:][:, 0:256], ps[:, 4, c * 256:(c + 1) * 256]).then_inc(evac[1], 1)
                    for k in range(13, 16):
                        sc.copy(high_xm(k), high_x(k))
                    stream_split(sc, split_act, "mqrq", 1, out_q, looped=False)
                elif name == "rgmo":
                    def out_g(i, par):
                        c0 = RG + (2 * i + par) * CHUNK
                        sc.activation(zt[:, 0, c0:c0 + CHUNK], ps[:, par * 2, :], ACT.Silu if i == 0 else ACT.Sigmoid).then_inc(evac[par], 1)
                    stream_split(sc, split_act, "rgmo", 2, out_g, looped=False)
                elif name == "conv":
                    for f, c0 in ((ACT.Silu, RG), (ACT.Sigmoid, MO)):
                        sc.activation(zt[:, 1, c0:c0 + 1024], zt[:, 1, c0:c0 + 1024], f)
                elif name == "conv_silu":
                    sc.activation(act[:, 4096:7168], act[:, 4096:7168], ACT.Silu)
                elif name == "turn_r":
                    turn_evac(sc, "act", f0, lambda k: rT[:, k, :], blocks=12)
                elif name == "retention":
                    sc.wait_ge(aux, aux_at["dist"])
                    for u in range(2 * R_HEADS):
                        hd, half = u // 2, u % 2
                        if u >= 2:
                            sc.wait_ge(re_out, u - 1)
                        for d in range(2):
                            last = sc.activation(work[:, 2 * (u % 2) + d, :].rearrange("p (i n) -> p i n", i=2), dist[:, d, 2 * half:2 * half + 2, :],
                                                 ACT.Exp, scale=st[:, 112 + 8 * d + hd:113 + 8 * d + hd])
                        last.then_inc(re_exp, 1)
                elif name == "mlstm":
                    for v in range(2 * M_HEADS):
                        sc.wait_ge(ml_arg, v + 1)
                        w = work[:, 2 * (v % 2):2 * (v % 2) + 2, :]
                        sc.activation(w, w, ACT.Exp).then_inc(ml_exp, 1)
                elif name == "head_norm":
                    rms_act(sc, rms_k[n], None, 24, have_sums=True)
                elif name == "turn_y":
                    turn_evac(sc, "act", f0, lambda k: yT[:, k, :])
                elif name == "merge":
                    for n4 in range(4):
                        for which in range(3):
                            c = 2 * PAIR0["merge"] + 3 * n4 + which
                            split_act(sc, (0, c), (3,))
                            split_act(sc, (0, c + 1), range(3))
                            if which == 0 and n4 >= 1:
                                sc.wait_ge(mg_sum, n4)
                            if which < 2:
                                sc.wait_ge(piece_used[3], c + 1)
                                for s in range(NT):
                                    a = sc.activation(r2[:, 2048 + (2 * which + s) * 512:][:, 0:512], ps[:, 2 * which + s, :], ACT.Sigmoid)
                                a.then_inc(mg_sig, 1)
                elif name == "turn_m":
                    turn_evac(sc, "act", f0, lambda k: xT[:, k, :])
                elif name == "norm_2":
                    rms_act(sc, rms_k[n], [(ht[:, s, :], D, z[:, 2 * D + s * D:][:, 0:D]) for s in range(NT)], NT)
                elif name == "turn_2":
                    turn_evac(sc, "act", f0, lambda k: xT[:, k, :], scale=lambda k: modc[:, 2, k:k + 1],
                              bias=lambda k: adac[:, 2 * KT + k, 0:1])
                elif name == "out2":
                    stream_split(sc, split_act, "out2", 2)
                elif name == "query":
                    def out_query(i, par):
                        for b in (0, 2):
                            sc.copy(qT[:, (2 * i + par) * 4 + b, :], ps[:, par * 4 + b, 0:TOK]).then_inc(evac[par], 1)
                    stream_split(sc, split_act, "query", 2, out_query, looped=False)
                elif name == "key_scores":
                    for b in range(4):
                        sc.wait_ge(pe_full, f0 + b + 1)
                        sc.copy(S[:, 0, 4 * b:4 * b + 4, :], ps[:, b, :].rearrange("p (b n) -> p b n", b=4))
                elif name == "soft":
                    for s in range(NT):
                        sc.activation(sel[2][:, s, :], sel[2][:, s, :], ACT.Exp)
                elif name == "spread":
                    def two_blocks(bb, first):
                        for half in range(2):
                            if not first:
                                sc.wait_ge(sp_stored[half], bb * 16)
                            for i in range(SB // 4):
                                sc.wait_ge(hot_used, bb * 64 + (half * SB + 4 * i + 4))
                                sc.copy(stage[:, half, :, 4 * i:4 * i + 4].rearrange("p i n -> p n i"),
                                        ps[:, i, :].rearrange("p (n i) -> p n i", n=4)).then_inc(sp_read, 1)
                            sc.wait_ge(sp_read, bb * (2 * SB // 4) + (half + 1) * (SB // 4))
                            sc.dma_start(GT[bass.ds(bb * 2 + half, 1)].rearrange("b p n i -> p (b n i)"),
                                         stage[:, half].rearrange("p n i -> p (n i)")).then_inc(sp_stored[half], 16)

                    two_blocks(0, True)
                    with sc.Fori(1, TOK // (2 * SB)) as bb:
                        two_blocks(bb, False)
                elif name == "experts":
                    def next_down(g, off):
                        split_act(sc, expert_chunk(g, off - 1, 1), range(3))
                        gelu(g, off)
                        split_act(sc, expert_chunk(g, off - 1, 1), (3,))

                    def gelu(g, off):
                        sc.wait_ge(piece_used[3], count(expert_chunk(g, off, 0), 1, 1))
                        if not (isinstance(g, int) and 2 * g + off < 2):
                            sc.wait_ge(piece_used[3], count(expert_chunk(g, off - 2, 1), 1, 1))
                        sc.activation(hid[:, off % 2], ps[:, 0:4, 0:TOK], ACT.Gelu).then_inc(hid_act, 1)

                    split_act(sc, expert_chunk(0, 0, 0), (3,))
                    split_act(sc, expert_chunk(0, 1, 0), range(3))
                    gelu(0, 0)
                    split_act(sc, expert_chunk(0, 1, 0), (3,))
                    next_down(0, 1)
                    split_act(sc, expert_chunk(0, 2, 0), range(4))
                    next_down(0, 2)
                    split_act(sc, expert_chunk(1, 1, 0), range(4))
                    with sc.Fori(1, GROUPS // 2 - 1) as g:
                        next_down(g, 1)
                        split_act(sc, expert_chunk(g, 2, 0), range(4))
                        next_down(g, 2)
                        split_act(sc, expert_chunk(g, 3, 0), range(4))
                    next_down(GROUPS // 2 - 1, 1)
                    split_act(sc, expert_chunk(GROUPS // 2 - 1, 1, 1), range(4))
                elif name == "final2":
                    sc.wait_ge(h_sum, 1)
                    rms_act(sc, rms_k[n], [(ht[:, s, :], D, z[:, 2 * D + s * D:][:, 0:D]) for s in range(NT)], NT)
                end(sc, "act")

        @block.vector
        def _(dve):
            for n, (name, l) in enumerate(STAGES):
                begin(dve, n)
                f0 = full[n]
                if name == "setup":
                    chain(dve, "dve", dve.memset(mask[:, :], 0.0))
                    dve.memset(mask[0:64, 64:128], NEG)
                    dve.memset(mask[0:64, 128 + 192:], NEG)
                    dve.wait_ge(consts, 16 * 2)
                    dve.wait_ge(consts_p, 16 * 5)
                    pos, inv = st[:, 80:82], z[:, 0:32]
                    chain(dve, "dve", dve.tensor_copy(pos, sti[:, 0:NT]))
                    for s in range(NT):
                        a = dve.tensor_scalar(z[:, 32 + s * 32:64 + s * 32], inv, pos[:, s:s + 1], None, ALU.mult)
                    chain(dve, "dve", a)
                    ang, turns, r = z[:, 32:96], z[:, 96:160], z[:, 128:192]
                    turns = z[:, 256:320]
                    chain(dve, "dve", dve.tensor_scalar(turns, ang, float(np.float32(1 / TWO_PI)), 12582912.0, ALU.mult, ALU.add))
                    chain(dve, "dve", dve.tensor_scalar(turns, turns, 12582912.0, None, ALU.subtract))
                    c1 = 6.28125
                    c2 = float(np.float32(np.round((TWO_PI - c1) * 2 ** 20) / 2 ** 20))
                    c3 = float(np.float32(TWO_PI - c1 - c2))
                    prev = ang
                    for cc in (c1, c2, c3):
                        chain(dve, "dve", dve.scalar_tensor_tensor(r, turns, -cc, prev, ALU.mult, ALU.add))
                        prev = r
                    pi = float(np.nextafter(np.float32(np.pi), np.float32(0)))
                    chain(dve, "dve", dve.tensor_scalar(r, r, pi, -pi, ALU.min, ALU.max))
                    c = z[:, 192:256]
                    chain(dve, "dve", dve.scalar_tensor_tensor(c, r, -1.0, r, ALU.mult, ALU.max))
                    dve.tensor_scalar(c, c, -1.0, float(np.float32(np.pi / 2)), ALU.mult, ALU.add)
                    lam = z[:, 512:1024].rearrange("p (k l n) -> p k l n", k=4, l=DEPTH)
                    for ly in range(DEPTH):
                        for pr in range(2):
                            k = 2 * ly + pr
                            dve.tensor_tensor_reduce(z[:, 1024 + k * 64:][:, 0:64], lam[:, 2 * pr, ly, :], lam[:, 2 * pr + 1, ly, :],
                                                     1.0, 0.0, ALU.mult, ALU.add, st[:, 68 + k:69 + k])
                elif name == "angles":
                    split_dve(dve, (0, 0), range(3))
                elif name == "norm":
                    if l == 0:
                        e = st[:, 64:68].rearrange("p (l k) -> p l k", k=2)
                        chain(dve, "dve", dve.tensor_tensor(st[:, 60:62], e[:, :, 1], e[:, :, 0], ALU.subtract))
                        for ly in range(DEPTH):
                            init = 0.8 - 0.6 * float(np.exp(-0.3 * ly))
                            dve.tensor_scalar(st[:, 60 + ly:61 + ly], st[:, 60 + ly:61 + ly], -init, None, ALU.add)
                            dve.tensor_scalar(bc[:, B_SUB + ly * HD:][:, 0:HD], bc[:, B_SUB + ly * HD:][:, 0:HD], 1.0 - init, None, ALU.mult)
                    rms_dve(dve, rms_k[n], NT, sums=rms_s[n])
                    for s in range(NT):
                        dve.tensor_scalar(ztiles(s), ht[:, s, :], rs[:, 64 + s:65 + s], None, ALU.mult)
                elif name == "turn_in":
                    turn_evac(dve, "dve", f0, lambda k: xT[:, k, :], scale=lambda k: col(C_NORM + l * KT + k))
                elif name == "split_c":
                    dve.wait_ge(x_high, high0[n] + 1)
                    c = cols[:, C_SILU:C_SILU + 2 * KT]
                    dve.tensor_tensor(cols_r[:, C_SILU:C_SILU + 2 * KT], c, silu_high[:, :], ALU.subtract)
                elif name in SPLITS:
                    if name == "split_in":
                        for s in range(NT):
                            dve.wait_ge(pe_full, f0 + s + 1)
                            dve.tensor_copy(zt[:, s, WI0:WI0 + IDX_HEADS], ps[:, 6 + s, 0:IDX_HEADS])
                    made_ = high0[n]
                    for x, x_r, high_ in SPLITS[name]:
                        for k in range(KT):
                            made_ += 1
                            dve.wait_ge(x_high, made_)
                            dve.tensor_tensor(x_r[:, k, :], x[:, k, :], high_(k), ALU.subtract)
                elif name == "join":
                    for k in range(KT):
                        dve.tensor_tensor(xT[:, k, :], xT_r[:, k, :], high_xm(k), ALU.add)
                elif name == "project":
                    stream_split(dve, split_dve, f"in{l}", 7, lambda i, par:
                                 dve.tensor_copy(zt[:, 1, bass.ds(i * 1024 + par * CHUNK, CHUNK)], ps[:, par * 2 + 1, :]).then_inc(evac[par], 1))
                elif name == "prep_a":
                    kr = zt[:, :, KR0:KR0 + A_ROPE].unsqueeze(2)
                    kd1 = kd[:, :, 0:64].unsqueeze(2)
                    rope(dve, kr[:, :, :, 0:32], kr[:, :, :, 32:64], 1, 32, lambda i, w: r2[:, i * 384:][:, 0:w],
                         kd1[:, :, :, 0:32], kd1[:, :, :, 32:64])
                    dve.tensor_copy(kd[:, :, 64:128], kd[:, :, 0:64])
                    rms_dve(dve, rms_k[n], 4, sums=rms_s[n])
                    for s in range(NT):
                        dve.tensor_scalar(zt[:, s, CQ0:CQ0 + A_Q], zt[:, s, CQ0:CQ0 + A_Q], rs[:, 64 + s:65 + s], None, ALU.mult)
                        dve.tensor_scalar(zt[:, s, CKV0:CKV0 + A_KV], zt[:, s, CKV0:CKV0 + A_KV], rs[:, 66 + s:67 + s], None, ALU.mult)
                elif name == "turn_a":
                    for j in (0, 2):
                        dve.wait_ge(pe_full, f0 + j + 1)
                        for k in (2 * j, 2 * j + 1):
                            src = ps[:, j, (k % 2) * TOK:(k % 2 + 1) * TOK]
                            if k == 5:
                                dve.tensor_copy(kpeT, src)
                            else:
                                dve.tensor_scalar(turn_a_dst(k), src, col(C_QN + l * 3 + k if k < 3 else C_KVN + l * 2 + k - 3),
                                                  None, ALU.mult)
                elif name == "heads_a":
                    for j in range(3):
                        dve.wait_ge(pe_full, f0 + j + 1)
                        dve.tensor_copy(qnT[:, 2 * j:2 * j + 2, :], ps[:, j, :].rearrange("p (h n) -> p h n", h=2))
                    dve.wait_ge(pe_full, f0 + 7)
                    dve.tensor_copy(qr[:, 0, :], ps[:, 6, 0:384])
                elif name == "values_a":
                    q = qr.rearrange("p t (h d) -> p t h d", h=A_HEADS)
                    rope(dve, q[:, :, :, 0:32], q[:, :, :, 32:64], A_HEADS, 32,
                         lambda i, w: (act[:, 3072 + i * 384:] if i < 2 else r2[:, 4096 + (i - 2) * 384:])[:, 0:w])
                elif name == "turn_ar":
                    turn_evac(dve, "dve", f0, lambda k: qrT[:, k, :], blocks=3)
                elif name in ("attend_a", "attend_b", "attend_c"):
                    attend_dve(dve, name[-1].upper(), l)
                elif name == "prep_b":
                    def tmp(i, w):
                        return r2[:, i * 160:][:, 0:w]
                    for c0 in (QB0, KB0):
                        rope(dve, heads_of(c0, B_HEADS, HD, 0, 16), heads_of(c0, B_HEADS, HD, 16, 32), B_HEADS, 16, tmp)
                    rope(dve, heads_of(QI0, IDX_HEADS, IDX_DIM, 0, 8), heads_of(QI0, IDX_HEADS, IDX_DIM, 8, 16), IDX_HEADS, 8, tmp)
                    rope(dve, heads_of(KI0, 1, IDX_DIM, 0, 8), heads_of(KI0, 1, IDX_DIM, 8, 16), 1, 8, tmp)
                    dve.tensor_copy(kid[:, :, 0:64], zt[:, :, KI0:KI0 + IDX_DIM])
                    dve.tensor_copy(kid[:, :, 64:128], zt[:, :, KI0:KI0 + IDX_DIM])
                elif name in ("turn_b", "turn_c"):
                    turn_evac(dve, "dve", f0, turn_ab_dst, blocks=10)
                elif name == "turn_idx":
                    turn_evac(dve, "dve", f0, lambda k: act[:, 2560 + k * TOK:][:, 0:TOK], blocks=5)
                elif name == "index":
                    dve.wait_ge(rel_done, l * 6 + 6)
                    for hd in range(IDX_HEADS):
                        for s in range(NT):
                            nk, m0 = keys(s)
                            wi = zt[:, s, WI0 + hd:WI0 + hd + 1]
                            o = score[:, m0:m0 + nk]
                            if hd == 0:
                                a = dve.tensor_scalar(o, rel[:, hd, m0:m0 + nk], wi, None, ALU.mult)
                            else:
                                a = dve.scalar_tensor_tensor(o, rel[:, hd, m0:m0 + nk], wi, o, ALU.mult, ALU.add)
                        chain(dve, "dve", a)
                elif name == "select":
                    TAKEN = -3e38
                    chain(dve, "dve", dve.tensor_tensor(kept, score, mask[:, :], ALU.add))
                    for r in range(N_SEL // 8):
                        for s in range(NT):
                            nk, m0 = keys(s)
                            a = dve.max(st[:, 90 + 8 * s:98 + 8 * s], kept[:, m0:m0 + nk])
                        chain(dve, "dve", a)
                        for s in range(NT):
                            nk, m0 = keys(s)
                            a = dve.match_replace(kept[:, m0:m0 + nk], st[:, 90 + 8 * s:98 + 8 * s], kept[:, m0:m0 + nk], TAKEN)
                        chain(dve, "dve", a)
                    chain(dve, "dve", dve.tensor_scalar(kept, kept, -2e38, NEG, ALU.is_gt, ALU.mult))
                    dve.tensor_tensor(score, kept, mask[:, :], ALU.add)
                elif name == "prep_c":
                    for c0 in (QC0, KC0):
                        rope(dve, heads_of(c0, 2 * C_HEADS, C_QK, 0, 8), heads_of(c0, 2 * C_HEADS, C_QK, 8, 16), 2 * C_HEADS, 8,
                             lambda i, w: r2[:, 4096 + i * 160:][:, 0:w])
                elif name == "norm_c":
                    for s in range(NT):
                        a = dve.tensor_tensor(norm_c_sq[:, s], norm_c_in[:, s], norm_c_in[:, s], ALU.mult)
                    chain(dve, "dve", a)
                    chain(dve, "dve", dve.tensor_reduce(rs[:, 0:10], r2[:, 0:1280].rearrange("p (h d) -> p h d", d=HD), AX_X, ALU.add))
                    chain(dve, "dve", dve.tensor_scalar(rs[:, 0:10], rs[:, 0:10], 1.0 / HD, None, ALU.mult))
                    rms_dve(dve, rms_k[n], 10)
                    for s in range(NT):
                        for hd in range(C_HEADS):
                            g0 = GC0 + hd * HD
                            a = dve.scalar_tensor_tensor(norm_c_sq[:, s, hd], norm_c_in[:, s, hd], rs[:, 64 + s * 5 + hd:65 + s * 5 + hd],
                                                         bc[:, B_SUB + l * HD:][:, 0:HD], ALU.mult, ALU.mult)
                        chain(dve, "dve", a)
                        dve.tensor_tensor(zt[:, s, GC0:GC0 + 640], r2[:, s * 640:(s + 1) * 640], zt[:, s, GC0:GC0 + 640], ALU.mult)
                elif name in ("turn_mix", "turn_h"):
                    turn_evac(dve, "dve", f0, lambda k: xT[:, k, :])
                elif name == "project_out":
                    def add_out(i, par):
                        for s in range(NT):
                            hc = ht[:, s, bass.ds(i * 1024 + par * CHUNK, CHUNK)]
                            dve.tensor_tensor(hc, ps[:, par * 2 + s, :], hc, ALU.add).then_inc(evac[par], 1)
                    stream_split(dve, split_dve, f"out{l}", 2, add_out)
                elif name == "embed":
                    for c in range(4):
                        dve.wait_ge(pe_full, f0 + 2 * c + 2)
                        dve.tensor_copy(z[:, D + c * CHUNK:][:, 0:CHUNK], ps[:, 2 * c + 1, :])
                elif name == "gate":
                    e0 = EVAC0[f"gate{l}"]
                    def apply(i, par):
                        c = 2 * i + par
                        dve.wait_ge(evac[par], e0 + 2 * i + 2)
                        for s in range(NT):
                            g = r2[:, (par * 2 + s) * 512:][:, 0:512]
                            a = dve.tensor_tensor(g, g, ztiles(s)[:, c * CHUNK:(c + 1) * CHUNK], ALU.mult)
                        chain(dve, "dve", a)
                        for s in range(NT):
                            g = r2[:, (par * 2 + s) * 512:][:, 0:512]
                            hc = ht[:, s, c * CHUNK:(c + 1) * CHUNK]
                            a = dve.tensor_tensor(hc, hc, g, ALU.add)
                        a.then_inc(gate_used, 1)
                    stream_split(dve, split_dve, f"gate{l}", 2, apply, looped=False)
                elif name == "final1":
                    rms_dve(dve, rms_k[n], NT, sums=rms_s[n])
                    dve.wait_ge(aux, aux_at["final"])
                    for s in range(NT):
                        dve.scalar_tensor_tensor(ht[:, s, :], ht[:, s, :], rs[:, 64 + s:65 + s], act[:, W0:W0 + D], ALU.mult, ALU.mult)
                elif name == "ada":
                    dve.wait_ge(bias_in, 32)
                    def add_bias(i, par):
                        zc = z[0:2, bass.ds(i * 1024 + par * CHUNK, CHUNK)]
                        dve.tensor_tensor(zc, ps[0:2, par, :], zc, ALU.add).then_inc(evac[par], 1)
                    stream_split(dve, split_dve, "ada", 12, add_bias)
                elif name == "ada_cols":
                    dve.wait_ge(pe_full, f0 + 1)
                    dve.tensor_copy(mask[:, 0:128], ps[:, 0, 0:128])
                elif name == "mod_cols":
                    for m, (g0, sec, r) in enumerate(((C_N1, 1, 0), (C_N1, 1, 1), (C_N2, 3, 0))):
                        chain(dve, "dve", dve.tensor_scalar(modc[:, m, :], adac[:, sec * KT:(sec + 1) * KT, r], 1.0, None, ALU.add))
                        dve.tensor_tensor(modc[:, m, :], modc[:, m, :], cols[:, g0:g0 + KT], ALU.mult)
                elif name == "norm_x":
                    dve.wait_ge(aux, aux_at["ctx"])
                    rms_dve(dve, rms_k[n], 4, sums=rms_s[n])
                    for s in range(NT):
                        dve.tensor_scalar(ztiles(s), ht[:, s, :], rs[:, 64 + s:65 + s], None, ALU.mult)
                        dve.tensor_scalar(r2[:, s * D:(s + 1) * D], r2[:, s * D:(s + 1) * D], rs[:, 66 + s:67 + s], None, ALU.mult)
                elif name == "turn_x":
                    turn_evac(dve, "dve", f0, lambda k: xT[:, k, :], scale=lambda k: modc[:, 0, k:k + 1],
                              bias=lambda k: adac[:, k, 0:1])
                elif name == "turn_ctx":
                    turn_evac(dve, "dve", f0, lambda k: cT[:, k, :], scale=lambda k: modc[:, 1, k:k + 1],
                              bias=lambda k: adac[:, k, 1:2])
                elif name == "gates":
                    chain(dve, "dve", dve.memset(z[:, 0:2048], 0.0))
                    bias = bc[:, B_MGB:B_MGB + 16].rearrange("p (d h) -> p d h", h=M_HEADS)
                    for s in range(4):
                        dve.wait_ge(pe_full, f0 + s + 1)
                        a = dve.tensor_tensor(gpad[:, :, s, 0:P:32], ps[:, s, 0:16].rearrange("p (d h) -> p d h", h=M_HEADS), bias, ALU.add)
                    chain(dve, "dve", a)
                    for d in range(2):
                        dve.scalar_tensor_tensor(z[:, 2304 + 16 * d:2320 + 16 * d].rearrange("p (s h) -> p s h", s=4),
                                                 gpad[:, 2 * d + 1, :, 0:P:32], -1.0, gpad[:, 2 * d + 1, :, 0:P:32], ALU.mult, ALU.max)
                    rd = bc[:, B_RDEC:B_RDEC + 16]
                    dve.scalar_tensor_tensor(z[:, 2336:2352], rd, -1.0, rd, ALU.mult, ALU.max)
                elif name == "gates_log":
                    for d in range(2):
                        f = gpad[:, 2 * d + 1, :, 0:P:32]
                        dve.scalar_tensor_tensor(f, f, 0.0, z[:, 2304 + 16 * d:2320 + 16 * d].rearrange("p (s h) -> p s h", s=4),
                                                 ALU.min, ALU.subtract)
                    rd = bc[:, B_RDEC:B_RDEC + 16]
                    chain(dve, "dve", dve.scalar_tensor_tensor(st[:, 112:128], rd, 0.0, z[:, 2336:2352], ALU.min, ALU.subtract))
                    dve.tensor_scalar(st[:, 112:128], st[:, 112:128], -1e-20, None, ALU.min)
                elif name == "gate_rows":
                    F, I, B, X, M, EN = (0, 1), (2, 3), (5, 6), (7, 8), (9, 10), (11, 12)
                    for dk in range(4):
                        d, kind = dk // 2, dk % 2
                        dst = row((I, F)[kind][d])
                        dve.wait_ge(pe_full, f0 + dk + 1)
                        if d == 0:
                            dve.tensor_copy(dst, ps[:, dk, :])
                        else:
                            dve.tensor_copy(dst[:, 0:TOK], ps[:, dk, TOK - 1::-1])
                            dve.tensor_copy(dst[:, TOK:], ps[:, dk, 2 * TOK - 1:TOK - 1:-1])
                    chain(dve, "dve", dve.memset(row(4), 0.0))
                    for d in range(2):
                        chain(dve, "dve", dve.tensor_tensor_scan(row(B[d]), row(F[d]), row(4), 0.0, ALU.add, ALU.add))
                    for d in range(2):
                        a = dve.tensor_tensor(row(X[d]), row(I[d]), row(B[d]), ALU.subtract)
                    chain(dve, "dve", a)
                    for d in range(2):
                        chain(dve, "dve", dve.tensor_tensor_scan(row(M[d]), row(X[d]), row(X[d]), 0.0, ALU.max, ALU.max))
                    for d in range(2):
                        chain(dve, "dve", dve.tensor_tensor(row(EN[d])[:, TOK:], row(B[d])[:, TOK:], row(M[d])[:, TOK:], ALU.add))
                        dve.tensor_scalar(row(EN[d])[:, TOK:], row(EN[d])[:, TOK:], -1.0, 88.0, ALU.mult, ALU.min)
                    dve.tensor_scalar(negm[:, 0, :], row(M[0])[:, TOK:], -1.0, None, ALU.mult)
                    dve.tensor_scalar(negm[:, 1, :], row(M[1])[:, 2 * TOK - 1:TOK - 1:-1], -1.0, None, ALU.mult)
                    dve.tensor_copy(row(13)[:, 0:TOK], row(X[1])[:, TOK - 1::-1])
                    dve.tensor_copy(row(13)[:, TOK:], row(X[1])[:, 2 * TOK - 1:TOK - 1:-1])
                elif name == "gate_back":
                    for b in range(3):
                        dve.wait_ge(pe_full, f0 + b + 1)
                        dve.tensor_copy(mcols[:, 4 * b:4 * b + 4, :], ps[:, b, :].rearrange("p (i n) -> p i n", i=4)[:, :, 0:P:32])
                elif name == "kv":
                    def out_kv(i, par):
                        for s in (1, 3):
                            dve.tensor_copy((zt if s < 2 else czt)[:, 1, (2 * i + par) * CHUNK:][:, 0:CHUNK], ps[:, par * 4 + s, :])\
                               .then_inc(evac[par], 1)
                    stream_split(dve, split_dve, "kv", 2, out_kv, looped=False)
                elif name == "mvmk":
                    def out_m(i, par):
                        if par == 0:
                            for s in (1, 3):
                                dve.tensor_copy((zt if s < 2 else czt)[:, 1, 2048:2560], ps[:, s, :]).then_inc(evac[0], 1)
                        else:
                            for b in (1, 3):
                                dve.tensor_copy(raw_x[:, b, :], ps[:, 4 + b, 0:TOK])
                                dve.tensor_copy(raw_c[:, b, :], ps[:, b, 0:TOK]).then_inc(evac[1], 1)
                    stream_split(dve, split_dve, "mvmk", 1, out_m, looped=False)
                elif name == "mqrq":
                    def out_q(i, par):
                        if par == 0:
                            for b in (1, 3):
                                dve.tensor_copy(raw_x[:, 4 + b, :], ps[:, b, 0:TOK]).then_inc(evac[0], 1)
                        else:
                            for c in range(2):
                                dve.tensor_copy(zt[:, 1, RQ + c * 256:][:, 0:256], ps[:, 5, c * 256:(c + 1) * 256]).then_inc(evac[1], 1)
                    stream_split(dve, split_dve, "mqrq", 1, out_q, looped=False)
                elif name == "rgmo":
                    def out_g(i, par):
                        c0 = RG + (2 * i + par) * CHUNK
                        dve.tensor_copy(zt[:, 1, c0:c0 + CHUNK], ps[:, par * 2 + 1, :]).then_inc(evac[par], 1)
                    stream_split(dve, split_dve, "rgmo", 2, out_g, looped=False)
                elif name == "conv":
                    def tap(i, ch):
                        return cols[:, C_CONV + i * 8 + ch:C_CONV + i * 8 + ch + 1]
                    def parts(b):
                        return (raw_x[:, b, :], b + 4 if b < 4 else b - 4) if b < 8 else (raw_c[:, b - 8, :], b - 4)
                    for step in range(3):
                        for b in range(12):
                            x, ch = parts(b)
                            o = conv[:, b, :]
                            if step == 0:
                                a = dve.tensor_scalar(o, x, tap(1, ch), None, ALU.mult)
                            elif step == 1:
                                a = dve.scalar_tensor_tensor(o[:, 1:], x[:, 0:TOK - 1], tap(0, ch), o[:, 1:], ALU.mult, ALU.add)
                            else:
                                a = dve.scalar_tensor_tensor(o[:, 0:TOK - 1], x[:, 1:], tap(2, ch), o[:, 0:TOK - 1], ALU.mult, ALU.add)
                        chain(dve, "dve", a)
                    dve.wait_ge(aux, aux_at["trig2"])
                    def tmp2(i, w):
                        return act[:, 8192 + i * 512:][:, 0:w]
                    for c0 in (RQ, RK):
                        rope(dve, heads_of(c0, R_HEADS, R_DK, 0, 32), heads_of(c0, R_HEADS, R_DK, 32, 64), R_HEADS, 32, tmp2)
                elif name == "turn_r":
                    turn_evac(dve, "dve", f0, lambda k: rT[:, k, :], blocks=12)
                elif name == "retention":
                    def ready(u):
                        dve.wait_ge(re_exp, u + 1)
                        e, w = work[:, 2 * (u % 2), :], work[:, 2 * (u % 2) + 1, :]
                        chain(dve, "dve", dve.tensor_tensor(e, e, w, ALU.add))
                        dve.wait_ge(re_att, u + 1)
                        dve.scalar_tensor_tensor(w, ps[:, u % 2, :], R_DK ** -0.5, e, ALU.mult, ALU.mult).then_inc(re_ready, 1)

                    def done(hd):
                        dve.wait_ge(re_out, 2 * hd + 2)
                        for s in range(NT):
                            a = dve.tensor_copy(zt[:, s, RV + hd * R_DV:RV + (hd + 1) * R_DV], ps[:, 2 + 2 * (hd % 2) + s, 0:R_DV])
                        a.then_inc(re_done, 1)

                    for u in range(2 * R_HEADS):
                        ready(u)
                        if u >= 2 and u % 2 == 0:
                            done(u // 2 - 1)
                    done(R_HEADS - 1)
                elif name == "mlstm":
                    def arg(v):
                        hd, d = v // 2, v % 2
                        dve.wait_ge(ml_att, v + 1)
                        if v >= 2:
                            dve.wait_ge(ml_out, v - 1)
                        w = work[:, 2 * (v % 2):2 * (v % 2) + 2, :].rearrange("p b n -> p (b n)")
                        for i in range(4):
                            a = dve.tensor_scalar(w[:, i * TOK:(i + 1) * TOK], ps[:, 4 + v % 2, 0:TOK], mcols[:, 4 * d + i, hd:hd + 1], 0.0,
                                                  ALU.add, ALU.min)
                        a.then_inc(ml_arg, 1)

                    def ready(v):
                        hd, d = v // 2, v % 2
                        dve.wait_ge(ml_exp, v + 1)
                        lat = work[:, 2 * (v % 2) + 1, :]
                        chain(dve, "dve", dve.scalar_tensor_tensor(lat, dist[:, d, 2:4, :].rearrange("p i n -> p (i n)"), 1e29, lat,
                                                                   ALU.is_lt, ALU.mult))
                        for half in range(2):
                            w = work[:, 2 * (v % 2) + half, :]
                            a = dve.scalar_tensor_tensor(w, ps[:, 2 * (hd % 2) + half, :], M_DK ** -0.5, w, ALU.mult, ALU.mult)
                        a.then_inc(ml_ready, 1)

                    def done(v):
                        hd, d = v // 2, v % 2
                        dve.wait_ge(ml_out, v + 1)
                        y0 = (RK if hd < 2 else RQ) + (hd % 2) * M_DV
                        den = ps[:, 6:8, M_DV]
                        clamp = mcols[:, 8 + 2 * d:10 + 2 * d, hd]
                        a, b = st[:, 80:82], st[:, 82:84]
                        chain(dve, "dve", dve.tensor_copy(b, den))
                        chain(dve, "dve", dve.scalar_tensor_tensor(a, b, -1.0, b, ALU.mult, ALU.max))
                        chain(dve, "dve", dve.tensor_tensor(a, a, clamp, ALU.max))
                        chain(dve, "dve", dve.reciprocal(a, a))
                        for s in range(NT):
                            y = zt[:, s, y0:y0 + M_DV]
                            if d == 0:
                                m = dve.tensor_scalar(y, ps[:, 6 + s, 0:M_DV], a[:, s:s + 1], None, ALU.mult)
                            else:
                                m = dve.scalar_tensor_tensor(y, ps[:, 6 + s, 0:M_DV], a[:, s:s + 1], y, ALU.mult, ALU.add)
                        m.then_inc(ml_done, 1)

                    for v in range(2 * M_HEADS + 2):
                        if 1 <= v <= 2 * M_HEADS:
                            ready(v - 1)
                        if v >= 2:
                            done(v - 2)
                        if v < 2 * M_HEADS:
                            arg(v)
                elif name == "head_norm":
                    N = NT * 1024
                    yr = zt[:, :, RV:RV + 1024].rearrange("p t (h d) -> p t h d", h=R_HEADS)
                    ym = [zt[:, :, c0:c0 + 512].rearrange("p t (h d) -> p t h d", h=2) for c0 in (RK, RQ)]
                    groups = [(yr, R_HEADS, R_DV, 0)] + [(y, 2, M_DV, 16 + 4 * i) for i, y in enumerate(ym)]
                    mean = st[:, 0:24]
                    def stat(tile_, c0, heads):
                        return tile_[:, c0:c0 + NT * heads].rearrange("p (t h) -> p t h", t=NT)
                    for y, heads, dv, c0 in groups:
                        a = dve.tensor_reduce(stat(st, c0, heads), y, AX_X, ALU.add)
                    chain(dve, "dve", a)
                    dve.tensor_scalar(st[:, 0:16], st[:, 0:16], 1.0 / R_DV, None, ALU.mult)
                    chain(dve, "dve", dve.tensor_scalar(st[:, 16:24], st[:, 16:24], 1.0 / M_DV, None, ALU.mult))
                    for y, heads, dv, c0 in groups:
                        a = dve.tensor_tensor(y, y, stat(st, c0, heads).unsqueeze(3).to_broadcast([P, NT, heads, dv]), ALU.subtract)
                    chain(dve, "dve", a)
                    sq = [act[:, o:o + NT * heads * dv].rearrange("p (t h d) -> p t h d", t=NT, h=heads)
                          for o, (y, heads, dv, c0) in zip((4096, 6144, 7168), groups)]
                    for q, (y, heads, dv, c0) in zip(sq, groups):
                        a = dve.tensor_tensor(q, y, y, ALU.mult)
                    chain(dve, "dve", a)
                    for q, (y, heads, dv, c0) in zip(sq, groups):
                        a = dve.tensor_reduce(stat(rs, c0, heads), q, AX_X, ALU.add)
                    chain(dve, "dve", a)
                    dve.tensor_scalar(rs[:, 0:16], rs[:, 0:16], 1.0 / R_DV, None, ALU.mult)
                    chain(dve, "dve", dve.tensor_scalar(rs[:, 16:24], rs[:, 16:24], 1.0 / M_DV, None, ALU.mult))
                    rms_dve(dve, rms_k[n], 24)
                    for y, heads, dv, c0 in groups:
                        a = dve.tensor_tensor(y, y, stat(rs, 64 + c0, heads).unsqueeze(3).to_broadcast([P, NT, heads, dv]), ALU.mult)
                    chain(dve, "dve", a)
                    for s in range(NT):
                        dve.tensor_tensor(zt[:, s, RG:RG + 1024], zt[:, s, RG:RG + 1024], zt[:, s, RV:RV + 1024], ALU.mult)
                        for i, c0 in enumerate((RK, RQ)):
                            m0 = MO + i * 512
                            dve.tensor_tensor(zt[:, s, m0:m0 + 512], zt[:, s, m0:m0 + 512], zt[:, s, c0:c0 + 512], ALU.mult)
                elif name == "turn_y":
                    turn_evac(dve, "dve", f0, lambda k: yT[:, k, :])
                elif name == "merge":
                    for n4 in range(4):
                        for which in range(3):
                            c = 2 * PAIR0["merge"] + 3 * n4 + which
                            split_dve(dve, (0, c), (3,))
                            split_dve(dve, (0, c + 1), range(3))
                            if which == 2:
                                dve.wait_ge(mg_sig, 2 * n4 + 2)
                                dve.wait_ge(piece_used[3], c + 1)
                                g = [r2[:, 2048 + i * 512:2560 + i * 512] for i in range(4)]
                                for i in range(4):
                                    a = dve.tensor_tensor(g[i], g[i], ps[:, 4 + i, :], ALU.mult)
                                chain(dve, "dve", a)
                                for s in range(NT):
                                    a = dve.tensor_tensor(ztiles(s)[:, n4 * CHUNK:(n4 + 1) * CHUNK], g[s], g[2 + s], ALU.add)
                                a.then_inc(mg_sum, 1)
                elif name == "turn_m":
                    turn_evac(dve, "dve", f0, lambda k: xT[:, k, :])
                elif name == "out2":
                    dve.wait_ge(aux, aux_at["gt1"])
                    def add_gated(i, par):
                        c = 2 * i + par
                        for s in range(NT):
                            a = dve.tensor_tensor(ztiles(s)[:, c * CHUNK:(c + 1) * CHUNK], ps[:, par * 2 + s, :], gt[:, c * CHUNK:(c + 1) * CHUNK], ALU.mult)
                            a.then_inc(evac[par], 1)
                        dve.wait_ge(evac[par], EVAC0["out2"] + 2 * i + 2)
                        for s in range(NT):
                            hc = ht[:, s, c * CHUNK:(c + 1) * CHUNK]
                            dve.tensor_tensor(hc, hc, ztiles(s)[:, c * CHUNK:(c + 1) * CHUNK], ALU.add)
                    stream_split(dve, split_dve, "out2", 2, add_gated, looped=False)
                elif name == "norm_2":
                    rms_dve(dve, rms_k[n], NT, sums=rms_s[n])
                    for s in range(NT):
                        dve.tensor_scalar(ztiles(s), ht[:, s, :], rs[:, 64 + s:65 + s], None, ALU.mult)
                elif name == "turn_2":
                    turn_evac(dve, "dve", f0, lambda k: xT[:, k, :], scale=lambda k: modc[:, 2, k:k + 1],
                              bias=lambda k: adac[:, 2 * KT + k, 0:1])
                elif name == "query":
                    def out_query(i, par):
                        for b in (1, 3):
                            dve.tensor_copy(qT[:, (2 * i + par) * 4 + b, :], ps[:, par * 4 + b, 0:TOK]).then_inc(evac[par], 1)
                    stream_split(dve, split_dve, "query", 2, out_query, looped=False)
                elif name == "key_scores":
                    for b in range(4):
                        dve.wait_ge(pe_full, f0 + 5 + b)
                        dve.tensor_copy(S[:, 1, 4 * b:4 * b + 4, :], ps[:, 4 + b, :].rearrange("p (b n) -> p b n", b=4))
                elif name == "top_keys":
                    def top16(values_, vals, idx, rows):
                        for r in range(2):
                            for x in rows:
                                a = dve.max(vals(x)[:, 8 * r:8 * r + 8], values_(x))
                            chain(dve, "dve", a)
                            for x in rows:
                                a = dve.max_index(idx(x)[:, 8 * r:8 * r + 8], vals(x)[:, 8 * r:8 * r + 8], values_(x))
                            chain(dve, "dve", a)
                            if r == 0:
                                for x in rows:
                                    a = dve.match_replace(values_(x), vals(x)[:, 0:8], values_(x), -3e38)
                                chain(dve, "dve", a)
                    rows = [(s, b) for s in range(NT) for b in range(16)]
                    top16(lambda x: S[:, x[0], x[1], :], lambda x: sv[:, x[0], x[1], :], lambda x: si[:, x[0], x[1], :], rows)
                    dve.tensor_copy(z[:, 5120:5632], z[:, 4608:5120].bitcast(U32))
                    svp = z[:, 4096:4608].rearrange("p (s h f n) -> p s h f n", s=NT, h=P_HEADS, f=2)
                    for s in range(NT):
                        a = dve.tensor_tensor(cand[:, s].rearrange("p h (i j) -> p h i j", i=16),
                                              svp[:, s, :, 0, :].unsqueeze(3).to_broadcast([P, P_HEADS, 16, 16]),
                                              svp[:, s, :, 1, :].unsqueeze(2).to_broadcast([P, P_HEADS, 16, 16]), ALU.add)
                    chain(dve, "dve", a)
                    rows = [(s, b) for s in range(NT) for b in range(P_HEADS)]
                    top16(lambda x: cand[:, x[0], x[1], :], lambda x: bs[:, x[0], x[1], :], lambda x: bjv[:, x[0], x[1], :], rows)
                    for s in range(NT):
                        dve.tensor_tensor(sel[2][:, s, :].rearrange("p (h n) -> p h n", n=16), bs[:, s], bs[:, s, :, 0:1].to_broadcast([P, P_HEADS, 16]),
                                          ALU.subtract)
                elif name == "experts_of":
                    for s in range(NT):
                        a = dve.tensor_reduce(st[:, 8 * s:8 * s + 8], sel[2][:, s, :].rearrange("p (h n) -> p h n", n=16), AX_X, ALU.add)
                    chain(dve, "dve", a)
                    chain(dve, "dve", dve.reciprocal(st[:, 0:16], st[:, 0:16]))
                    for s in range(NT):
                        g = sel[2][:, s, :].rearrange("p (h n) -> p h n", n=16)
                        dve.tensor_tensor(g, g, st[:, 8 * s:8 * s + 8].unsqueeze(2).to_broadcast([P, P_HEADS, 16]), ALU.mult)
                    dve.tensor_scalar(j12[0], bj, 4, None, ALU.logical_shift_right)
                    chain(dve, "dve", dve.tensor_scalar(j12[1], bj, 15, None, ALU.bitwise_and))
                    for i in range(2):
                        a = dve.tensor_copy(z[:, 10752 + i * 256:11008 + i * 256], j12[i])
                    chain(dve, "dve", a)
                    sifp = z[:, 5120:5632].rearrange("p (s h f n) -> p s h f n", s=NT, h=P_HEADS, f=2)
                    pos16 = iota[:, 0:16].unsqueeze(1).to_broadcast([P, P, 16])
                    for s in range(NT):
                        for f in range(2):
                            chain(dve, "dve", dve.tensor_tensor(hot, j12f[f][:, s, :].unsqueeze(2).to_broadcast([P, P, 16]), pos16, ALU.is_equal))
                            h4 = hot.rearrange("p (h k) j -> p h k j", h=P_HEADS)
                            chain(dve, "dve", dve.tensor_tensor(h4, h4, sifp[:, s, :, f, :].unsqueeze(2).to_broadcast([P, P_HEADS, 16, 16]), ALU.mult))
                            chain(dve, "dve", dve.tensor_reduce(sel[f][:, s, :], hot, AX_X, ALU.add))
                elif name == "turn_sel":
                    for m in range(3):
                        dve.wait_ge(pe_full, f0 + m + 1)
                        dve.tensor_copy(selT[:, m, :], ps[:, m, 0:TOK])
                elif name == "spread":
                    def block_of_tokens(b, first):
                        for i in range(SB):
                            if i % 8 == 0:
                                if i >= 8 or not first:
                                    dve.wait_ge(hot_used, b * SB + (i - 8))
                                half = (i // 8) % 2
                                dve.tensor_tensor(hot2[:, half], iota[:, :].unsqueeze(1).to_broadcast([P, 8, P]),
                                                  selT[:, 1, bass.ds(b * SB + i, 8)].unsqueeze(2).to_broadcast([P, 8, P]),
                                                  ALU.is_equal).then_inc(hot_second, 1)
                            if i >= 8 or not first:
                                dve.wait_ge(hot_used, b * SB + (i - 7))
                            dve.tensor_scalar(hot1[:, i % 8, :], iota[:, :], selT[:, 0, bass.ds(b * SB + i, 1)],
                                              selT[:, 2, bass.ds(b * SB + i, 1)], ALU.is_equal, ALU.mult).then_inc(hot_made, 1)

                    block_of_tokens(0, True)
                    with dve.Fori(1, TOK // SB) as b:
                        block_of_tokens(b, False)
                elif name == "experts":
                    dve.memset(z[:, 0:4096], 0.0).then_inc(yacc_zero, 1)
                    dve.wait_ge(yacc_zero, 1)

                    def gates(g, off):
                        b = off % 2
                        dve.wait_ge(slab_full[b], g * 16 + (16 * (off // 2) + 16))
                        dve.wait_ge(hid_act, g * 2 + (off + 1))
                        hb = hid[:, b].rearrange("p i (b n) -> p i b n", n=SB)
                        dve.tensor_tensor(hb, hb, slab[:, b].rearrange("p b i n -> p i b n"), ALU.mult).then_inc(hid_step, 1)
                        dve.wait_ge(hid_step, g * 4 + (2 * off + 1))
                        dve.tensor_copy(hid_high[:, b], hid[:, b]).then_inc(hid_step, 1)
                        dve.wait_ge(hid_step, g * 4 + (2 * off + 2))
                        dve.tensor_tensor(hid_low[:, b], hid[:, b], hid_high[:, b], ALU.subtract).then_inc(hid_done, 1)

                    def next_down(g, off):
                        split_dve(dve, expert_chunk(g, off - 1, 1), range(3))
                        gates(g, off)
                        split_dve(dve, expert_chunk(g, off - 1, 1), (3,))

                    def this_up(g, off, nxt):
                        c = expert_chunk(g, off, 1)
                        for dc in range(4):
                            dve.wait_ge(piece_used[dc], count(c, 1, 1))
                            for s in range(NT):
                                y = yacc[:, s, dc * CHUNK:(dc + 1) * CHUNK]
                                a = dve.tensor_tensor(y, y, ps[:, 4 + 2 * (dc % 2) + s, :], ALU.add)
                            a.then_inc(up_read, 1)
                            if nxt is not None and dc >= 1:
                                split_dve(dve, nxt, (dc - 1,))
                        if nxt is not None:
                            split_dve(dve, nxt, (3,))

                    split_dve(dve, expert_chunk(0, 0, 0), (3,))
                    split_dve(dve, expert_chunk(0, 1, 0), range(3))
                    gates(0, 0)
                    split_dve(dve, expert_chunk(0, 1, 0), (3,))
                    next_down(0, 1)
                    this_up(0, 0, expert_chunk(0, 2, 0))
                    next_down(0, 2)
                    this_up(0, 1, expert_chunk(1, 1, 0))
                    last = GROUPS // 2 - 1
                    with dve.Fori(1, last) as g:
                        next_down(g, 1)
                        this_up(g, 0, expert_chunk(g, 2, 0))
                        next_down(g, 2)
                        this_up(g, 1, expert_chunk(g, 3, 0))
                    next_down(last, 1)
                    this_up(last, 0, expert_chunk(last, 1, 1))
                    this_up(last, 1, None)
                elif name == "final2":
                    dve.wait_ge(aux, aux_at["final2"])
                    for s in range(NT):
                        a = dve.tensor_tensor(yacc[:, s, :], yacc[:, s, :], gt, ALU.mult)
                    chain(dve, "dve", a)
                    for s in range(NT):
                        a = dve.tensor_tensor(ht[:, s, :], ht[:, s, :], yacc[:, s, :], ALU.add)
                    a.then_inc(h_sum, 1)
                    rms_dve(dve, rms_k[n], NT, sums=rms_s[n])
                    for s in range(NT):
                        dve.scalar_tensor_tensor(ht[:, s, :], ht[:, s, :], rs[:, 64 + s:65 + s], act[:, 4096:4096 + D], ALU.mult, ALU.mult)
                end(dve, "dve")


def pack_chunks(w):
    n = w.shape[1] // CHUNK
    return w.reshape(4, PIECE_KT, P, n, CHUNK).transpose(3, 0, 2, 1, 4).reshape(n, 4, P, PIECE)


def lay_out(i):
    f32 = np.float32
    w0 = KI0 + IDX_DIM
    order = np.concatenate([np.arange(w0), np.arange(w0 + IDX_HEADS, ZW), np.arange(w0, w0 + IDX_HEADS)])
    parts = []
    for l in range(DEPTH):
        parts += [pack_chunks(i["w_in"][l][:, order[:WI0]]), pack_chunks(i["w_o"][l]), pack_chunks(i["w_pg"][l])]
    parts.append(pack_chunks(i["w_ada_2"][0]))
    w2 = i["w_in_2"][0]
    rq, rk, rv, rg = w2[:, 0:512], w2[:, 512:1024], w2[:, 1024:2048], w2[:, 2048:3072]
    mq, mk, mv, mo = w2[:, 3072:3584], w2[:, 3584:4096], w2[:, 4096:5120], w2[:, 5120:6144]
    wg, gr, gm = w2[:, 6144:6160], w2[:, 6160:6160 + D], w2[:, 6160 + D:6160 + 2 * D]
    for w in (rk, rv, mv, mk, mq, rq, rg, mo):
        parts.append(pack_chunks(w))
    outs = np.concatenate([i["w_ret_out_2"][0], i["w_mlstm_out_2"][0]])
    merge = np.stack([pack_chunks(w) for w in (gr, gm, outs)], axis=1)
    parts += [merge.reshape(-1, 4, P, PIECE), pack_chunks(i["w_out_2"][0]), pack_chunks(i["peer_query_2"][0])]
    down = i["peer_down_2"][0].reshape(P_KEYS, GROUPS, 4, 4, PIECE_KT, P).transpose(1, 3, 5, 4, 2, 0)
    up = i["peer_up_2"][0].reshape(P_KEYS, GROUPS, 4, 4, CHUNK).transpose(1, 3, 0, 2, 4).reshape(GROUPS, 4, P, PIECE)
    experts = np.empty((GROUPS, 2, 4, P, PIECE), f32)
    experts[:, 0] = down.reshape(GROUPS, 4, P, PIECE)
    experts[:, 1] = up
    parts += [experts[0:1, 0], np.stack([experts[1:, 0], experts[:-1, 1]], axis=1).reshape(-1, 4, P, PIECE), experts[-1:, 1]]
    stream = np.concatenate(parts)

    def columns(v):
        return v.reshape(-1, P).T

    cols = np.concatenate([columns(i["norm_g"]), columns(i["q_norm_g"]), columns(i["kv_norm_g"]), columns(i["norm1_g_2"]),
                           columns(i["norm2_g_2"]), columns(i["m_conv_2"][0]),
                           np.stack([columns(i["c_2"][0]), columns(i["c_ctx_2"])], axis=2).reshape(P, 2 * KT)], axis=1)
    bc = np.concatenate([i["subln_g"].reshape(-1), i["m_gate_bias_2"][0].reshape(-1), i["ret_decay_2"][0].reshape(-1)])
    tail = i["w_in"][:, :, w0:w0 + IDX_HEADS].reshape(DEPTH, KT, P, IDX_HEADS).transpose(2, 0, 1, 3).reshape(P, -1)
    wg = wg.reshape(KT, P, 16).transpose(1, 0, 2).reshape(P, -1)
    nope = [np.arange(h * (HD + A_ROPE), h * (HD + A_ROPE) + HD) for h in range(A_HEADS)]
    rot = [np.arange(h * (HD + A_ROPE) + HD, (h + 1) * (HD + A_ROPE)) for h in range(A_HEADS)]
    key = [np.arange(h * 2 * HD, h * 2 * HD + HD) for h in range(A_HEADS)]
    val = [np.arange(h * 2 * HD + HD, (h + 1) * 2 * HD) for h in range(A_HEADS)]
    inv_freq = (1.0 / (f32(500000.0) ** (np.arange(32, dtype=f32) * f32(2.0 / 64)))).astype(f32)
    freq = (f32(10000.0) ** (-np.arange(16, dtype=f32) / f32(16))).astype(f32)
    tok = np.arange(TOK)
    ang = np.concatenate([(tok // 64)[:, None].astype(f32) * freq, (tok % 64)[:, None].astype(f32) * freq], axis=1)
    trig2 = np.stack([np.cos(ang), np.sin(ang)]).reshape(2, NT, P, 32).transpose(2, 0, 1, 3).astype(f32)
    s, c = tok[:, None], tok[None, :]
    far = 1e30
    dist = np.stack([np.concatenate([TOK + c - s, np.where(c >= s, c - s, far)]),
                     np.concatenate([TOK - c + s, np.where(s >= c, s - c, far)])])
    dist = dist.reshape(2, 4, P, TOK).transpose(2, 0, 1, 3).reshape(P, -1).astype(f32)
    return dict(
        x=i["x"][0], positions=i["positions"][0].reshape(NT, P).T, cols=cols, bc=bc,
        wsmall=np.concatenate([tail, wg], axis=1), inv_freq=inv_freq,
        lam=np.concatenate([i[k].reshape(-1) for k in ("lam_q1", "lam_k1", "lam_q2", "lam_k2")]),
        w_uq=i["w_uq"][:, :, np.concatenate(nope + rot)], w_ukv=i["w_ukv"][:, :, np.concatenate(key + val)],
        w_ple=i["w_ple"], pT=i["p"][:, 0].transpose(0, 2, 1), final_g=i["final_g"], trig2=trig2,
        ctx=i["ctx_2"][0], wgates=wg.reshape(P, KT, 16), dist=dist, b_ada=i["b_ada_2"],
        keysT=i["peer_keys_2"][0].reshape(16, P_KEYS, P).transpose(2, 0, 1).reshape(P, -1), final_g2=i["final_g_2"],
        stream=stream)


def kernel(**inputs):
    import concourse.bacc as bacc
    from concourse.bass_utils import run_bass_kernel_spmd

    laid = {k: np.ascontiguousarray(v) for k, v in lay_out({k: np.asarray(v) for k, v in inputs.items()}).items()}
    nc = bacc.Bacc("TRN2", target_bir_lowering=False, num_devices=1)
    arrays, t = {}, {}
    for name, a in laid.items():
        arrays[f"in_{name}_dram"] = a
        t[name] = nc.dram_tensor(f"in_{name}_dram", a.shape, mybir.dt.from_np(a.dtype), kind="ExternalInput").ap()
    t["out"] = nc.dram_tensor("out_0_dram", (TOK, D), F32, kind="ExternalOutput").ap()
    build_program(nc, t)
    r = run_bass_kernel_spmd(nc, [arrays], core_ids=[0])
    return r.results[0]["out_0_dram"].reshape(1, TOK, D)
```

```python
from contextlib import ExitStack

import numpy as np

import concourse.bass as bass
from concourse import mybir

F32 = mybir.dt.float32
F32R = mybir.dt.float32r
I32 = mybir.dt.int32
U32 = mybir.dt.uint32
ALU = mybir.AluOpType
ACT = mybir.ActivationFunctionType
AX_X = mybir.AxisListType.X

P = 128
D = 2048
TOK = 256
NT = TOK // P
KT = D // P
PIECE_KT = 4
CHUNK = 512
PIECE = PIECE_KT * CHUNK
PIECES = 4
DEPTH = 2
EPS = 1e-6
NEG = -1e30
TWO_PI = 2 * np.pi

A_Q, A_KV, A_ROPE, A_HEADS, HD = 384, 256, 64, 6, 128
B_HEADS, C_HEADS, IDX_HEADS, IDX_DIM, C_QK = 5, 5, 8, 64, 64
CQ0 = 0
CKV0 = CQ0 + A_Q
KR0 = CKV0 + A_KV
GA0 = KR0 + A_ROPE
QB0 = GA0 + A_HEADS * HD
KB0 = QB0 + B_HEADS * HD
VB0 = KB0 + B_HEADS * HD
QI0 = VB0 + B_HEADS * HD
KI0 = QI0 + IDX_HEADS * IDX_DIM
GB0 = KI0 + IDX_DIM
QC0 = GB0 + B_HEADS * HD
KC0 = QC0 + C_HEADS * HD
VC0 = KC0 + C_HEADS * HD
GC0 = VC0 + C_HEADS * HD
WI0 = GC0 + C_HEADS * HD
ZW = WI0 + IDX_HEADS
N_SEL = 64
MIX0 = (GA0, GB0, GC0)
MIXW = (A_HEADS * HD, B_HEADS * HD, C_HEADS * HD)

R_HEADS, R_DK, R_DV = 8, 64, 128
M_HEADS, M_DK, M_DV = 4, 128, 256
P_HEADS, P_KEYS, P_TOPK = 8, 128, 16
GROUPS = 32

ADA_AT = []
for _l in range(DEPTH):
    ADA_AT += [("norm", _l, f"in{_l}")] * (_l > 0)
    ADA_AT += [(_n, _l, f"out{_l}") for _n in
               ("prep_a", "values_a", "attend_a", "prep_b", "index", "select", "attend_b", "prep_c", "norm_c")]
    ADA_AT += [("split_h", _l, f"gate{_l}")]
ADA_AT += [("final1", 0, "kv"), ("norm_x", 0, "kv")]
ADA_CHUNKS = 6 * D // CHUNK
ADA_LEFT = ADA_CHUNKS - len(ADA_AT)
ADA_NEXT = [n for _, _, n in ADA_AT] + ["kv"] * ADA_LEFT
ADA_OF = {(n, _l): a for a, (n, _l, _) in enumerate(ADA_AT)}

STREAM = []
for _l in range(DEPTH):
    STREAM += [(f"in{_l}", 7, 2), (f"out{_l}", 2, 2), (f"gate{_l}", 2, 2)]
STREAM += [("kv", 2, 4), ("mvmk", 1, 4), ("mqrq", 1, 4), ("rgmo", 2, 2), ("merge", 6, 0),
           ("out2", 2, 2), ("query", 2, 4), ("experts", GROUPS, 0)]
PAIR0, EVAC0, _pair, _evac = {}, {}, 0, 0
for _n, _p, _e in STREAM:
    PAIR0[_n], EVAC0[_n] = _pair, _evac
    _pair += _p
    _evac += _p * _e
N_CHUNKS = 2 * _pair + ADA_CHUNKS
ADA_BEFORE = {n: sum(PAIR0[m] <= PAIR0[n] for m in ADA_NEXT) for n in PAIR0}


def ada_place(a):
    return 2 * PAIR0[ADA_NEXT[a]] + a


C_NORM = 0
C_QN = C_NORM + DEPTH * KT
C_KVN = C_QN + DEPTH * 3
C_N1 = C_KVN + DEPTH * 2
C_N2 = C_N1 + KT
C_CONV = C_N2 + KT
C_SILU = C_CONV + 3 * 8
NCOLS = C_SILU + 2 * KT
B_SUB = 0
B_MGB = B_SUB + DEPTH * HD
B_RDEC = B_MGB + 16
NBC = B_RDEC + 16


def build_program(nc, t):
    ctx = ExitStack()
    with ctx:
        def sb(name, shape, dt=F32):
            return ctx.enter_context(nc.sbuf_tensor(name, shape, dt))

        def sem(name):
            return ctx.enter_context(nc.semaphore(name))

        def two_views(name, shape):
            with nc.sbuf_tensor(name, shape, F32) as plain:
                pass
            return plain, sb(name + "_r", shape, F32R)

        ring, ring_r = two_views("ring", [P, PIECES, PIECE])
        high = sb("high", [P, PIECES, PIECE], F32R)
        h = sb("h", [P, NT * D])
        act, act_r = two_views("act", [P, 4096 + 6528])
        z, z_r = two_views("z", [P, NT * ZW])
        r2, r2_r = two_views("r2", [P, 5120])
        ident = sb("ident", [P, P])
        iota = sb("iota", [P, P])
        mask = sb("mask", [P, P + TOK])
        trig = sb("trig", [P, 2, NT, 32])
        cols, cols_r = two_views("cols", [P, NCOLS])
        bc = sb("bc", [P, NBC])
        wsmall = sb("wsmall", [P, 768])
        adac = sb("adac", [P, 6 * KT, 2])
        sel16 = sb("sel16", [P, 16])
        st = sb("st", [P, 128])
        rs = sb("rs", [P, 96])
        sti = sb("sti", [P, 2], I32)
        ones = sb("ones", [P, P])
        mcols = sb("mcols", [P, 12, M_HEADS])
        ps = ctx.enter_context(nc.psum_tensor("ps", [P, 8, 512], F32))

        xT = act[:, 0:KT * TOK].rearrange("p (k n) -> p k n", k=KT)
        xT_r = act_r[:, 0:KT * TOK].rearrange("p (k n) -> p k n", k=KT)
        W0 = KT * TOK
        wtail = wsmall[:, 0:256].rearrange("p (l k n) -> p l k n", l=DEPTH, k=KT)
        mod_rows = wsmall[:, 256:768]
        wgates = wsmall[:, 256:512].rearrange("p (k n) -> p k n", k=KT)
        zt = z[:, :].rearrange("p (t n) -> p t n", t=NT)
        part_rows = z[:, 4096:4608]
        zs = z[:, 8192:10240]
        ht = h[:, :].rearrange("p (t n) -> p t n", t=NT)

        piece_full = [sem(f"piece_full{j}") for j in range(PIECES)]
        piece_high = [sem(f"piece_high{j}") for j in range(PIECES)]
        piece_low = [sem(f"piece_low{j}") for j in range(PIECES)]
        x_high = sem("x_high")
        piece_used = [sem(f"piece_used{j}") for j in range(PIECES)]
        evac = [sem(f"evac{i}") for i in range(2)]
        stage_done = {e: sem(f"stage_done_{e}") for e in ("pe", "act", "dve", "pool")}
        pe_full = sem("pe_full")
        ada_rows = sem("ada_rows")
        ada_turned = sem("ada_turned")
        ada_done = sem("ada_done")
        part_done = sem("part_done")
        dve_step = sem("dve_step")
        act_step = sem("act_step")
        pool_step = sem("pool_step")
        rms_sums = sem("rms_sums")
        rms_inv = sem("rms_inv")
        rms_root = sem("rms_root")
        att_scores = sem("att_scores")
        att_logits = sem("att_logits")
        att_probs = sem("att_probs")
        att_mixed = sem("att_mixed")
        att_turned = sem("att_turned")
        att_pT = sem("att_pT")
        att_out = sem("att_out")
        att_done = sem("att_done")
        rel_done = sem("rel_done")
        gate_used = sem("gate_used")
        consts = sem("consts")
        small = sem("small")
        consts_p = sem("consts_p")
        aux = sem("aux")

        n_step = {"act": 0, "dve": 0, "pool": 0}
        step_sem = {"act": act_step, "dve": dve_step, "pool": pool_step}

        def chain(eng, who, ins):
            n_step[who] += 1
            ins.then_inc(step_sem[who], 1)
            eng.wait_ge(step_sem[who], n_step[who])

        ALL = ("pe", "act", "dve", "pool")

        def begin(eng, n, wait_for=ALL):
            if n >= 1:
                for who in wait_for:
                    eng.wait_ge(stage_done[who], n)

        def end(eng, who):
            eng.drain().then_inc(stage_done[who], 1)

        def count(c, mul, add):
            return c[0] * (2 * mul) + (c[1] * mul + add)

        def place(c, mul, add):
            return c[0] * (2 * mul) + ((c[1] + c[2]) * mul + add)

        def weights(j, c0, n):
            return high[:, j, c0:c0 + n], ring_r[:, j, c0:c0 + n]

        def product(pe, out, lhs, rhs, start, stop):
            pe.matmul(out, lhs[0], rhs[0], start=start, stop=False)
            pe.matmul(out, lhs[0], rhs[1], start=False, stop=False)
            return pe.matmul(out, lhs[1], rhs[0], start=False, stop=stop)

        def split_act(sc, c, js):
            for j in js:
                sc.wait_ge(piece_full[j], place(c, 16, 16))
                sc.copy(high[:, j, :], ring[:, j, :]).then_inc(piece_high[j], 1)

        def split_dve(dve, c, js):
            for j in js:
                dve.wait_ge(piece_high[j], count(c, 1, 1))
                dve.tensor_tensor(ring_r[:, j, :], ring[:, j, :], high[:, j, :], ALU.subtract).then_inc(piece_low[j], 1)

        def stream_split(eng, split, name, n_pairs, evacuate=None, looped=True, ends=False):
            def chunk(i, par):
                c = (i, 2 * PAIR0[name] + par, ADA_BEFORE[name])
                nxt = (i, c[1] + 1, c[2])
                split(eng, c, (3,))
                if not (ends and par == 1 and isinstance(i, int) and i == n_pairs - 1):
                    split(eng, nxt, range(3))
                if evacuate is not None:
                    eng.wait_ge(piece_used[3], place(c, 1, 1))
                    evacuate(i, par)
            if looped:
                with eng.Fori(0, n_pairs - ends) as i:
                    for par in range(2):
                        chunk(i, par)
                if ends:
                    for par in range(2):
                        chunk(n_pairs - 1, par)
            else:
                for i in range(n_pairs):
                    for par in range(2):
                        chunk(i, par)

        def stream_pe(pe, name, n_pairs, evacs, lhs, M=P, tiles=NT):
            base, e0 = PAIR0[name], EVAC0[name]
            def body(i):
                for par in range(2):
                    if base > 0 or not isinstance(i, int) or i > 0:
                        pe.wait_ge(evac[par], i * evacs + e0)
                    for k in range(KT):
                        j = k // PIECE_KT
                        if k % PIECE_KT == 0:
                            pe.wait_ge(piece_low[j], count((i, 2 * base + par, 0), 1, 1))
                        w = weights(j, (k % PIECE_KT) * CHUNK, CHUNK)
                        for s in range(tiles):
                            mm = product(pe, ps[0:M, par * tiles + s, :], lhs(s, k), w, k == 0, k == KT - 1)
                        if k % PIECE_KT == PIECE_KT - 1:
                            mm.then_inc(piece_used[j], 1)
            if base == 0 and e0 == 0:
                body(0)
                with pe.Fori(1, n_pairs) as i:
                    body(i)
            else:
                with pe.Fori(0, n_pairs) as i:
                    body(i)

        def ada_bank(name):
            return (3, 2) if name.startswith("attend") else (6, 7)

        def ada_pe(pe, a, bank, js=range(4)):
            for j in js:
                if a >= 1 and j == 0:
                    pe.wait_ge(ada_rows, a)
                pe.wait_ge(piece_full[j], 16 * (ada_place(a) + 1))
                for q in range(PIECE_KT):
                    k = PIECE_KT * j + q
                    mm = pe.matmul(ps[32 * q:32 * q + 2, bank, :], cols[:, C_SILU + 2 * k:C_SILU + 2 * k + 2],
                                   ring[:, j, q * CHUNK:(q + 1) * CHUNK], start=(j == 0), stop=(j == 3), tile_position=(0, 32 * q))
                mm.then_inc(piece_used[j], 1)

        def ada_turn(pe, a, bank):
            pe.wait_ge(ada_rows, a + 1)
            if a >= 1:
                pe.wait_ge(ada_done, a)
            for b in range(4):
                mm = pe.matmul(ps[:, bank, 2 * b:2 * b + 2], mod_rows[:, b * P:(b + 1) * P], sel16[:, 0:2], start=True, stop=True)
            mm.then_inc(ada_turned, 1)

        def ada_act(sc, a, bank):
            sc.wait_ge(piece_used[3], ada_place(a) + 1)
            if a >= 1:
                sc.wait_ge(ada_turned, a)
            for q in range(4):
                c = sc.copy(mod_rows[32 * q:32 * q + 2, :], ps[32 * q:32 * q + 2, bank, :])
            c.then_inc(ada_rows, 1)

        def ada_dve(dve, a, bank):
            dve.wait_ge(ada_turned, a + 1)
            dve.tensor_copy(adac[:, 4 * a:4 * a + 4, :], ps[:, bank, 0:8].rearrange("p (b r) -> p b r", r=2)).then_inc(ada_done, 1)

        def turn_pe(pe, src, blocks=KT, tiles=NT):
            for j in range((blocks + 1) // 2):
                for k in range(2 * j, min(2 * j + 2, blocks)):
                    for s in range(tiles):
                        mm = pe.transpose(ps[:, j, (k % 2) * TOK + s * P:(k % 2) * TOK + (s + 1) * P], src(s, k), ident[:, :])
                mm.then_inc(pe_full, 1)

        def turn_evac(eng, who, base, dst, blocks=KT, scale=None, bias=None):
            for j in range((blocks + 1) // 2):
                if (j % 2 == 0) != (who == "dve"):
                    continue
                eng.wait_ge(pe_full, base + j + 1)
                for k in range(2 * j, min(2 * j + 2, blocks)):
                    src = ps[:, j, (k % 2) * TOK:(k % 2 + 1) * TOK]
                    s = None if scale is None else scale(k)
                    b = None if bias is None else bias(k)
                    if who == "dve":
                        if s is None:
                            eng.tensor_copy(dst(k), src)
                        elif b is None:
                            eng.tensor_scalar(dst(k), src, s, None, ALU.mult)
                        else:
                            eng.tensor_scalar(dst(k), src, s, b, ALU.mult, ALU.add)
                    elif s is None:
                        eng.copy(dst(k), src)
                    elif b is None:
                        eng.activation(dst(k), src, ACT.Copy, scale=s)
                    else:
                        eng.activation(dst(k), src, ACT.Identity, scale=s, bias=b)


        def rms_act(act_, k, sources, n, have_sums=False):
            if not have_sums:
                for c, (src, width, junk) in enumerate(sources):
                    last = act_.activation(junk, src, ACT.Square, scale=float(width) ** -0.5, accum_out=rs[:, c:c + 1])
                last.then_inc(rms_sums, 1)
            act_.wait_ge(rms_inv, k + 1)
            act_.activation(rs[:, 64:64 + n], rs[:, 32:32 + n], ACT.Sqrt).then_inc(rms_root, 1)

        def rms_dve(dve, k, n, sums=None):
            if sums is not None:
                dve.wait_ge(rms_sums, sums + 1)
            chain(dve, "dve", dve.tensor_scalar(rs[:, 32:32 + n], rs[:, 0:n], EPS, None, ALU.add))
            dve.reciprocal(rs[:, 32:32 + n], rs[:, 32:32 + n]).then_inc(rms_inv, 1)
            dve.wait_ge(rms_root, k + 1)

        def rope(dve, x1, x2, heads, half, tmp, out1=None, out2=None):
            cs, sn = (trig[:, f, :, 0:32:32 // half].unsqueeze(2).to_broadcast([P, NT, heads, half]) for f in range(2))
            a, b, c, d = (tmp(i, NT * heads * half).rearrange("p (t h d) -> p t h d", t=NT, h=heads) for i in range(4))
            dve.tensor_tensor(a, x1, cs, ALU.mult)
            dve.tensor_tensor(b, x2, sn, ALU.mult)
            dve.tensor_tensor(c, x2, cs, ALU.mult)
            chain(dve, "dve", dve.tensor_tensor(d, x1, sn, ALU.mult))
            dve.tensor_tensor(x1 if out1 is None else out1, a, b, ALU.subtract)
            chain(dve, "dve", dve.tensor_tensor(x2 if out2 is None else out2, c, d, ALU.add))

        def heads_of(col, heads, width, lo, hi):
            return zt[:, :, col:col + heads * width].rearrange("p t (h d) -> p t h d", h=heads)[:, :, :, lo:hi]

        va = r2[:, 0:1536].rearrange("p (t n) -> p t n", t=NT)
        qr = r2[:, 1536:2304].rearrange("p (t n) -> p t n", t=NT)
        qrT = r2[:, 2304:3072].rearrange("p (k n) -> p k n", k=3)
        kd = r2[:, 3072:3328].rearrange("p (t n) -> p t n", t=NT)
        kpeT = r2[:, 3328:3584]
        ckvT = r2[:, 3584:4096].rearrange("p (k n) -> p k n", k=2)
        qnT = act[:, 0:1536].rearrange("p (k n) -> p k n", k=6)
        knT = act[:, 1536:3072].rearrange("p (k n) -> p k n", k=6)
        cqT = act[:, 3072:3840].rearrange("p (k n) -> p k n", k=3)
        w_uq = act[:, W0:W0 + 3456].rearrange("p (k n) -> p k n", k=3)
        w_ukv = act[:, W0 + 3456:W0 + 6528].rearrange("p (k n) -> p k n", k=2)
        w_ple = act[:, W0:W0 + 4096].rearrange("p (k n) -> p k n", k=2)
        pT = act[:, W0 + 4096:W0 + 4608].rearrange("p (k n) -> p k n", k=2)
        hqT = act[:, 0:1280].rearrange("p (k n) -> p k n", k=5)
        hkT = act[:, 1280:2560].rearrange("p (k n) -> p k n", k=5)
        qiT = act[:, 2560:3584].rearrange("p (k n) -> p k n", k=4)
        kiT = act[:, 3584:3840]
        score = r2[:, 0:384]
        rel = r2[:, 384:3456].rearrange("p (h n) -> p h n", h=IDX_HEADS)
        kept = r2[:, 3456:3840]
        kid = r2[:, 3840:4096].rearrange("p (t n) -> p t n", t=NT)

        def keys(s):
            return (s + 1) * P, s * P

        def units(heads):
            return [(hd, s) for hd in range(heads) for s in range(NT)]

        UNITS = {"A": units(A_HEADS), "B": units(B_HEADS), "C": units(C_HEADS)}
        UNIT0 = {}
        nu = 0
        for l in range(DEPTH):
            for m in "ABC":
                UNIT0[m, l] = nu
                nu += len(UNITS[m])
        MIXED0 = {l: l * len(UNITS["C"]) for l in range(DEPTH)}
        SCALE = {"A": (A_ROPE + HD) ** -0.5, "B": HD ** -0.5, "C": C_QK ** -0.5}

        def scbuf(m, slot, sub=0):
            return r2[:, slot * 512 + sub * 256:][:, 0:256] if m == "C" else r2[:, 4096 + slot * 256:4352 + slot * 256]

        def prbuf(m, slot, sub=0):
            return r2[:, 1024 + slot * 512 + sub * 256:][:, 0:256] if m == "C" else r2[:, 4608 + slot * 256:4864 + slot * 256]

        def mixbuf(slot):
            return r2[:, 2048 + slot * 256:2304 + slot * 256]

        def pTbuf(m, slot):
            b = 2560 if m == "C" else 1536
            return r2[:, b + slot * 256:b + slot * 256 + 256]

        def values(m, j, hd):
            return va[:, j, hd * HD:(hd + 1) * HD] if m == "A" else zt[:, j, (VB0 if m == "B" else VC0) + hd * HD:][:, 0:HD]

        def attend_pe(pe, m, l, between=()):
            u0, us = UNIT0[m, l], UNITS[m]
            subs = 2 if m == "C" else 1

            def scores(u):
                hd, s = us[u]
                nk, _ = keys(s)
                if u >= 2:
                    pe.wait_ge(att_logits, u0 + u - 1)
                q0, q1 = s * P, (s + 1) * P
                b = u % 2
                if m == "A":
                    r = (hd % 2) * A_ROPE
                    pe.matmul(ps[:, b, 0:nk], qnT[:, hd, q0:q1], knT[:, hd, 0:nk], start=True, stop=False)
                    mm = pe.matmul(ps[:, b, 0:nk], qrT[r:r + A_ROPE, hd // 2, q0:q1], kpeT[r:r + A_ROPE, 0:nk],
                                   start=False, stop=True)
                elif m == "B":
                    mm = pe.matmul(ps[:, b, 0:nk], hqT[:, hd, q0:q1], hkT[:, hd, 0:nk], start=True, stop=True)
                else:
                    for c in range(2):
                        r = c * C_QK
                        mm = pe.matmul(ps[:, 2 * b + c, 0:nk], hqT[r:r + C_QK, hd, q0:q1], hkT[r:r + C_QK, hd, 0:nk],
                                       start=True, stop=True)
                mm.then_inc(att_scores, 1)

            def turn(u):
                _, s = us[u]
                if m == "C":
                    pe.wait_ge(att_mixed, MIXED0[l] + u + 1)
                else:
                    pe.wait_ge(att_probs, u0 + u + 1)
                if u >= 2:
                    pe.wait_ge(att_pT, u0 + u - 1)
                src = mixbuf(u % 2) if m == "C" else prbuf(m, u % 2)
                for j in range(s + 1):
                    mm = pe.transpose(ps[:, 4 + u % 2, j * P:(j + 1) * P], src[:, j * P:(j + 1) * P], ident[:, :])
                mm.then_inc(att_turned, 1)

            def out(u):
                hd, s = us[u]
                pe.wait_ge(att_pT, u0 + u + 1)
                if u >= 2:
                    pe.wait_ge(att_done, u0 + u - 1)
                for j in range(s + 1):
                    mm = pe.matmul(ps[:, 6 + u % 2, 0:HD], pTbuf(m, u % 2)[:, j * P:(j + 1) * P], values(m, j, hd),
                                   start=(j == 0), stop=(j == s))
                mm.then_inc(att_out, 1)

            n = len(us)
            for u in range(n + 2):
                if u < n:
                    scores(u)
                if 1 <= u <= n:
                    turn(u - 1)
                if u >= 2:
                    out(u - 2)
                if u < len(between):
                    between[u]()

        def attend_act(act_, m, l):
            u0, us = UNIT0[m, l], UNITS[m]

            def probs(u):
                _, s = us[u]
                nk, _ = keys(s)
                act_.wait_ge(att_logits, u0 + u + 1)
                if u >= 2:
                    if m == "C":
                        act_.wait_ge(att_mixed, MIXED0[l] + u - 1)
                    else:
                        act_.wait_ge(att_turned, u0 + u - 1)
                for c in range(2 if m == "C" else 1):
                    k = 2 * (u % 2) + c
                    last = act_.activation(prbuf(m, u % 2, c)[:, 0:nk], scbuf(m, u % 2, c)[:, 0:nk], ACT.Exp,
                                           bias=st[:, 34 + k:35 + k], accum_out=st[:, 38 + k:39 + k])
                last.then_inc(att_probs, 1)

            def turned(u):
                _, s = us[u]
                act_.wait_ge(att_turned, u0 + u + 1)
                if u >= 2:
                    act_.wait_ge(att_out, u0 + u - 1)
                act_.copy(pTbuf(m, u % 2)[:, 0:(s + 1) * P], ps[:, 4 + u % 2, 0:(s + 1) * P]).then_inc(att_pT, 1)

            n = len(us)
            for u in range(n + 1):
                if u < n:
                    probs(u)
                if u >= 1:
                    turned(u - 1)

        def attend_dve(dve, m, l):
            u0, us = UNIT0[m, l], UNITS[m]
            subs = 2 if m == "C" else 1
            masks = score if m == "B" else mask

            def logits(u):
                _, s = us[u]
                nk, m0 = keys(s)
                dve.wait_ge(att_scores, u0 + u + 1)
                if u >= 2:
                    dve.wait_ge(att_probs, u0 + u - 1)
                for c in range(subs):
                    k = 2 * (u % 2) + c
                    bank = 2 * (u % 2) + c if m == "C" else u % 2
                    last = dve.tensor_tensor_reduce(scbuf(m, u % 2, c)[:, 0:nk], ps[:, bank, 0:nk], masks[:, m0:m0 + nk],
                                                    SCALE[m], NEG, ALU.add, ALU.max, st[:, 30 + k:31 + k])
                chain(dve, "dve", last)
                k = 2 * (u % 2)
                dve.tensor_scalar(st[:, 34 + k:34 + k + subs], st[:, 30 + k:30 + k + subs], -1.0, None, ALU.mult)\
                   .then_inc(att_logits, 1)

            def mix(u):
                _, s = us[u]
                nk, _ = keys(s)
                k = 2 * (u % 2)
                dve.wait_ge(att_probs, u0 + u + 1)
                chain(dve, "dve", dve.reciprocal(st[:, 42 + k:44 + k], st[:, 38 + k:40 + k]))
                if u >= 2:
                    dve.wait_ge(att_turned, u0 + u - 1)
                dve.tensor_scalar(prbuf(m, u % 2, 0)[:, 0:nk], prbuf(m, u % 2, 0)[:, 0:nk], st[:, 42 + k:43 + k], None, ALU.mult)
                chain(dve, "dve", dve.tensor_scalar(st[:, 43 + k:44 + k], st[:, 43 + k:44 + k], st[:, 60 + l:61 + l], None, ALU.mult))
                dve.scalar_tensor_tensor(mixbuf(u % 2)[:, 0:nk], prbuf(m, u % 2, 1)[:, 0:nk], st[:, 43 + k:44 + k],
                                         prbuf(m, u % 2, 0)[:, 0:nk], ALU.mult, ALU.add).then_inc(att_mixed, 1)

            def done(u):
                hd, s = us[u]
                dve.wait_ge(att_out, u0 + u + 1)
                src = ps[:, 6 + u % 2, 0:HD]
                if m == "C":
                    dve.tensor_copy(zt[:, s, QC0 + hd * HD:QC0 + (hd + 1) * HD], src).then_inc(att_done, 1)
                    return
                k = 2 * (u % 2)
                g = zt[:, s, (GA0 if m == "A" else GB0) + hd * HD:][:, 0:HD]
                dve.scalar_tensor_tensor(g, src, st[:, 46 + u % 2:47 + u % 2], g, ALU.mult, ALU.mult).then_inc(att_done, 1)

            def sums(u):
                dve.wait_ge(att_probs, u0 + u + 1)
                k = 2 * (u % 2)
                chain(dve, "dve", dve.reciprocal(st[:, 46 + u % 2:47 + u % 2], st[:, 38 + k:39 + k]))

            n = len(us)
            for u in range(n + 2):
                if m == "C" and 1 <= u <= n:
                    mix(u - 1)
                if u < n:
                    logits(u)
                if u >= 2:
                    done(u - 2)
                if m != "C" and 1 <= u <= n:
                    sums(u - 1)

        STAGES = [("setup", 0)]
        for l in range(DEPTH):
            STAGES += [("norm", l), ("turn_in", l), ("split_in", l), ("project", l), ("prep_a", l), ("turn_a", l), ("heads_a", l),
                       ("values_a", l), ("turn_ar", l), ("attend_a", l), ("prep_b", l), ("turn_b", l), ("turn_idx", l),
                       ("index", l), ("select", l), ("attend_b", l), ("prep_c", l), ("turn_c", l), ("attend_c", l),
                       ("norm_c", l), ("turn_mix", l), ("split_mix", l), ("project_out", l), ("turn_h", l), ("split_h", l),
                       ("embed", l), ("gate", l)]
        STAGES += [(name, 0) for name in (
            "final1", "norm_x", "ada", "mod_cols", "turn_x", "turn_ctx",
            "gates", "gates_exp", "gates_log", "gate_rows", "gate_clamp", "gate_back",
            "split_xc", "kv", "mvmk", "mqrq", "rgmo", "join", "conv", "conv_silu", "turn_r", "retention", "mlstm", "head_norm",
            "turn_y", "split_xy", "merge", "turn_m", "split_m", "out2", "norm_2", "turn_2", "split_2", "query", "top_keys",
            "soft", "experts_of", "turn_sel", "spread", "experts", "final2")]
        FULL_OF = {"turn_in": 8, "split_in": 3, "turn_a": 3, "heads_a": 8, "values_a": 4, "turn_ar": 2, "turn_b": 5,
                   "turn_idx": 3, "index": 6, "turn_c": 5, "turn_mix": 8, "turn_h": 8, "embed": 8,
                   "head_norm": 4, "experts_of": 4, "turn_x": 8, "turn_ctx": 8, "gates": 6, "gate_rows": 4, "gate_back": 3, "turn_r": 6,
                   "turn_y": 8, "turn_m": 8, "turn_2": 8, "turn_sel": 3}
        PRE_SPLIT = {("turn_in", 0): "in0", ("split_in", 1): "in1", ("split_xc", 0): "kv"}
        for l in range(DEPTH):
            PRE_SPLIT |= {("split_mix", l): f"out{l}", ("embed", l): f"gate{l}"}
        full, _f = [], 0
        for name, _ in STAGES:
            full.append(_f)
            _f += FULL_OF.get(name, 0)
        RMS_OF = {"norm": (1, 1), "prep_a": (1, 1), "norm_c": (1, 0), "final1": (1, 1), "norm_x": (1, 1),
                  "head_norm": (1, 0), "norm_2": (1, 1), "final2": (1, 1)}
        rms_k, rms_s, _k, _s = [], [], 0, 0
        for name, _ in STAGES:
            rms_k.append(_k)
            rms_s.append(_s)
            _k += RMS_OF.get(name, (0, 0))[0]
            _s += RMS_OF.get(name, (0, 0))[1]

        def ztiles(s):
            return z[:, s * D:(s + 1) * D]

        def col(c):
            return cols[:, c:c + 1]

        MIX_COL = [MIX0[0] + i * HD for i in range(6)] + [MIX0[1] + i * HD for i in range(5)] + \
                  [MIX0[2] + i * HD for i in range(5)]
        norm_c_in = zt[:, :, QC0:QC0 + C_HEADS * HD].rearrange("p t (h d) -> p t h d", h=C_HEADS)
        norm_c_sq = r2[:, 0:NT * C_HEADS * HD].rearrange("p (t h d) -> p t h d", t=NT, h=C_HEADS)

        def turn_ab_src(m):
            q0, k0 = (QB0, KB0) if m == "B" else (QC0, KC0)
            return lambda s, k: zt[:, s, (q0 + k * HD if k < 5 else k0 + (k - 5) * HD):][:, 0:HD]

        def turn_ab_dst(k):
            return act[:, k * TOK:(k + 1) * TOK]

        def turn_a_src(s, k):
            return zt[:, s, CQ0 + k * P:][:, 0:P] if k < 5 else kd[:, s, :]

        def turn_a_dst(k):
            return cqT[:, k, :] if k < 3 else ckvT[:, k - 3, :] if k < 5 else kpeT

        def idx_src(s, k):
            return zt[:, s, QI0 + k * P:][:, 0:P] if k < 4 else kid[:, s, :]

        aux_at, _a = {}, 0
        for l in range(DEPTH):
            for what, n in (("a", 2), ("ple", 2)):
                _a += n * 16
                aux_at[what, l] = _a
        _a += 16
        aux_at["final"] = _a
        for what in ("wgates", "dist", "keys", "final2"):
            _a += 16
            aux_at[what] = _a

        def tiles_of(area):
            return lambda k: area[:, k * TOK:(k + 1) * TOK]

        high_in, high_mix, high_2 = tiles_of(r2_r), tiles_of(z_r[:, 8192:12288]), tiles_of(act_r[:, 4096:8192])
        zt_r = z_r[:, :].rearrange("p (t n) -> p t n", t=NT)

        def high_x(k):
            return (act_r[:, 8192 + k * TOK:] if k < 9 else zt_r[:, 1, 6144 + (k - 9) * TOK:] if k < 13
                    else zt_r[:, 1, 4096 + (k - 13) * TOK:])[:, 0:TOK]

        def high_xm(k):
            return high_x(k) if k < 13 else act_r[:, 4096 + (k - 13) * TOK:][:, 0:TOK]

        def high_c(k):
            return (zt_r[:, 0, 2560 + k * TOK:] if k < 10 else zt_r[:, 1, 2560 + (k - 10) * TOK:])[:, 0:TOK]

        def pair_of(high_, low_, s, k):
            return high_(k)[:, s * P:(s + 1) * P], low_[:, k, s * P:(s + 1) * P]

        cT = act[:, 4096:8192].rearrange("p (k n) -> p k n", k=KT)
        both = act[:, 0:8192].rearrange("p (s n) -> p s n", s=2)
        czt = r2[:, :].rearrange("p (t n) -> p t n", t=NT)
        RK, RV, MV, RQ, RG, MO, RAW = 0, 512, 1536, 2560, 3072, 4096, 5120
        raw_x = zt[:, 0, RAW:RAW + 2048].rearrange("p (b n) -> p b n", b=8)
        raw_c = zt[:, 1, RAW:RAW + 1024].rearrange("p (b n) -> p b n", b=4)
        conv = act[:, 4096:7168].rearrange("p (b n) -> p b n", b=12)
        rT = act[:, 7168:10240].rearrange("p (b n) -> p b n", b=12)
        dist = zt[:, 0, RAW:RAW + 2048].rearrange("p (d i n) -> p d i n", d=2, i=4)
        work = zt[:, 1, RAW:RAW + 2048].rearrange("p (b n) -> p b n", b=4)
        modc = mask[:, 128:176].rearrange("p (m k) -> p m k", m=3)
        SH1, SC1, GT1, SH2, SC2, GT2 = (i * KT for i in range(6))
        b_ada = r2[:, 4096:4096 + 6 * KT]
        diag = {"head_norm": zt[:, 0, RAW:RAW + D].rearrange("p (k n) -> p k n", k=KT),
                "experts_of": r2[:, 0:D].rearrange("p (k n) -> p k n", k=KT)}
        gpad = z[:, 0:2048].rearrange("p (d s n) -> p d s n", d=4, s=4)

        def row(i):
            return z[:, 4096 + i * 512:4608 + i * 512]

        negm = wsmall[:, 0:512].rearrange("p (d n) -> p d n", d=2)
        yT = act[:, 4096:8192].rearrange("p (k n) -> p k n", k=KT)
        cT_r = yT_r = act_r[:, 4096:8192].rearrange("p (k n) -> p k n", k=KT)
        qT = z[:, 8192:12288].rearrange("p (k n) -> p k n", k=KT)
        keysT = r2[:, 0:2048].rearrange("p (b n) -> p b n", b=16)
        gt = act[:, 8192:8192 + D]
        S = z[:, 0:4096].rearrange("p (s b n) -> p s b n", s=NT, b=16)
        sv = z[:, 4096:4608].rearrange("p (s b n) -> p s b n", s=NT, b=16)
        si = z[:, 4608:5120].bitcast(U32).rearrange("p (s b n) -> p s b n", s=NT, b=16)
        sif = z[:, 5120:5632].rearrange("p (s b n) -> p s b n", s=NT, b=16)
        cand = z[:, 5632:9728].rearrange("p (s b n) -> p s b n", s=NT, b=P_HEADS)
        bs = z[:, 9728:9984].rearrange("p (s b n) -> p s b n", s=NT, b=P_HEADS)
        bj = z[:, 9984:10240].bitcast(U32)
        bjv = bj.rearrange("p (s b n) -> p s b n", s=NT, b=P_HEADS)
        j12 = [z[:, 10240 + i * 256:10496 + i * 256].bitcast(U32) for i in range(2)]
        j12f = [z[:, 10752 + i * 256:11008 + i * 256].rearrange("p (s n) -> p s n", s=NT) for i in range(2)]
        sel = [z[:, 11264 + i * 256:11520 + i * 256].rearrange("p (s n) -> p s n", s=NT) for i in range(3)]
        hot = z[:, 12032:14080].rearrange("p (a n) -> p a n", n=P_TOPK)
        selT = r2[:, 4096:4864].rearrange("p (m n) -> p m n", m=3)
        hot1 = r2[:, 1024:2048].rearrange("p (b n) -> p b n", b=8)
        hot2 = r2[:, 2048:4096].rearrange("p (a b n) -> p a b n", a=2, b=8)
        SB = 32
        stage = z[:, 0:8192].rearrange("p (b i n) -> p b i n", b=2, n=SB)
        slab = r2[:, 0:2048].rearrange("p (a b i n) -> p a b i n", a=2, b=TOK // SB, i=4)
        hid = z[:, 4096:6144].rearrange("p (b i n) -> p b i n", b=2, i=4)
        hid_low = z_r[:, 4096:6144].rearrange("p (b i n) -> p b i n", b=2, i=4)
        hid_high = z_r[:, 6144:8192].rearrange("p (b i n) -> p b i n", b=2, i=4)
        yacc = z[:, 0:4096].rearrange("p (t n) -> p t n", t=NT)
        high_y = tiles_of(z_r[:, 4096:8192])
        SPLITS = {"split_in": [(xT, xT_r, high_in)], "split_mix": [(xT, xT_r, high_mix)], "split_h": [(xT, xT_r, high_mix)],
                  "split_xc": [(xT, xT_r, high_x), (cT, cT_r, high_c)], "split_xy": [(xT, xT_r, high_mix), (yT, yT_r, high_y)],
                  "split_m": [(xT, xT_r, high_2)], "split_2": [(xT, xT_r, high_2)]}
        high0, _h = [], 0
        for name, _ in STAGES:
            high0.append(_h)
            _h += KT * len(SPLITS.get(name, ()))

        GT = nc.dram_tensor("gate_matrix", [TOK // SB, P, P, SB], F32).ap()

        def spread_gate_dve(dve, name):
            sec = GT1 if name == "head_norm" else GT2
            dve.tensor_tensor(diag[name], ident[:, :].unsqueeze(1).to_broadcast([P, KT, P]),
                              adac[:, sec:sec + KT, 0].unsqueeze(2).to_broadcast([P, KT, P]), ALU.mult).then_inc(diag_made, 1)

        def spread_gate_pe(pe, name):
            pe.wait_ge(diag_made, 1 if name == "head_norm" else 2)
            for k in range(KT):
                mm = pe.matmul(ps[:, k // 4, (k % 4) * P:(k % 4 + 1) * P], ones[:, :], diag[name][:, k, :], start=True, stop=True)
                if k % 4 == 3:
                    mm.then_inc(pe_full, 1)

        def spread_gate_act(sc, f0):
            for b in range(4):
                sc.wait_ge(pe_full, f0 + b + 1)
                sc.copy(gt[:, b * CHUNK:(b + 1) * CHUNK], ps[:, b, :])

        def expert_chunk(g, off, up):
            base = 2 * PAIR0["experts"]
            if not up:
                return (g * 2, base + 2 * off - 1, ADA_CHUNKS) if not (isinstance(g, int) and 2 * g + off == 0) else (0, base, ADA_CHUNKS)
            if isinstance(g, int) and 2 * g + off == GROUPS - 1:
                return (0, base + 2 * GROUPS - 1, ADA_CHUNKS)
            return (g * 2, base + 2 * off + 2, ADA_CHUNKS)

        re_att = sem("re_att")
        re_exp = sem("re_exp")
        re_ready = sem("re_ready")
        re_out = sem("re_out")
        re_done = sem("re_done")
        ml_att = sem("ml_att")
        ml_arg = sem("ml_arg")
        ml_exp = sem("ml_exp")
        ml_ready = sem("ml_ready")
        ml_out = sem("ml_out")
        ml_done = sem("ml_done")
        key_full = sem("key_full")
        key_read = sem("key_read")
        out_ready = sem("out_ready")
        mg_sig = sem("mg_sig")
        mg_sum = sem("mg_sum")
        hot_made = sem("hot_made")
        hot_second = sem("hot_second")
        hot_used = sem("hot_used")
        sp_read = sem("sp_read")
        sp_stored = [sem(f"sp_stored{i}") for i in range(2)]
        slab_full = [sem(f"slab_full{i}") for i in range(2)]
        hid_act = sem("hid_act")
        hid_step = sem("hid_step")
        hid_done = sem("hid_done")
        up_read = sem("up_read")
        yacc_zero = sem("yacc_zero")
        h_sum = sem("h_sum")
        diag_made = sem("diag_made")
        result = sem("result")

        block = ctx.enter_context(nc.Block())

        @block.sync
        def _(sp):
            sp.dma_start(ht, t["x"].rearrange("(t p) d -> p t d", p=P)).then_inc(consts, 16)
            sp.dma_start(cols[:, :], t["cols"]).then_inc(consts, 16)
            sp.dma_start(sti[:, 0:NT], t["positions"]).then_inc(small, 16)
            sp.dma_start(bc[:, :], t["bc"].partition_broadcast(P)).then_inc(small, 16)
            sp.dma_start(wsmall[:, 0:256], t["wtail"]).then_inc(small, 16)
            sp.dma_start(zs[:, 0:32], t["inv_freq"].partition_broadcast(P)).then_inc(small, 16)
            sp.dma_start(zs[:, 512:1024], t["lam"].partition_broadcast(P)).then_inc(small, 16)
            for j in range(PIECES):
                sp.dma_start(ring[:, j, :], t["stream"][0, j]).then_inc(piece_full[j], 16)
            with sp.Fori(1, N_CHUNKS) as c:
                for j in range(PIECES):
                    sp.wait_ge(piece_used[j], c)
                    sp.dma_start(ring[:, j, :], t["stream"][bass.ds(c, 1), j].rearrange("a p n -> p (a n)"))\
                      .then_inc(piece_full[j], 16)
            for s in range(NT):
                sp.wait_ge(out_ready, s + 1)
                sp.dma_start(t["out"][s * P:(s + 1) * P, :], ht[:, s, :]).then_inc(result, 16)
            sp.wait_ge(result, 16 * NT)

        @block.gpsimd
        def _(pool):
            for n, (name, l) in enumerate(STAGES):
                begin(pool, n)
                if name == "setup":
                    chain(pool, "pool", pool.memset(ident[:, :], 0.0))
                    pool.affine_select(out=ident[:, :], in_=ident[:, :], compare_op=ALU.not_equal, fill=1.0,
                                       base=0, pattern=[[-1, P]], channel_multiplier=1)
                    pool.memset(ones[:, :], 1.0)
                    pool.iota(iota[:, :], pattern=[[1, P]], base=0, channel_multiplier=0,
                              allow_small_or_imprecise_dtypes=True)
                elif name == "project" and l == 0:
                    pool.dma_start(w_uq, t["w_uq"][0].rearrange("(k p) n -> p k n", p=P)).then_inc(aux, 16)
                    pool.dma_start(w_ukv, t["w_ukv"][0].rearrange("(k p) n -> p k n", p=P)).then_inc(aux, 16)
                elif name == "attend_a":
                    pool.dma_start(w_ple, t["w_ple"][l].rearrange("(k p) n -> p k n", p=P)).then_inc(aux, 16)
                    pool.dma_start(pT, t["pT"][l].rearrange("(k p) n -> p k n", p=P)).then_inc(aux, 16)
                elif name == "gate" and l + 1 < DEPTH:
                    pool.dma_start(w_uq, t["w_uq"][l + 1].rearrange("(k p) n -> p k n", p=P)).then_inc(aux, 16)
                    pool.dma_start(w_ukv, t["w_ukv"][l + 1].rearrange("(k p) n -> p k n", p=P)).then_inc(aux, 16)
                elif name == "final1":
                    pool.dma_start(act[:, W0:W0 + D], t["final_g"].partition_broadcast(P)).then_inc(aux, 16)
                    pool.dma_start(trig[:, :, :, :], t["trig2"]).then_inc(consts_p, 16)
                    pool.dma_start(r2[:, 0:4096].rearrange("p (t n) -> p t n", t=NT),
                                   t["ctx"].rearrange("(t p) d -> p t d", p=P)).then_inc(consts_p, 16)
                    pool.dma_start(b_ada, t["b_ada"]).then_inc(consts_p, 16)
                elif name == "mod_cols":
                    pool.dma_start(wgates, t["wgates"]).then_inc(aux, 16)
                elif name == "conv_silu":
                    pool.dma_start(dist.rearrange("p d i n -> p (d i n)"), t["dist"]).then_inc(aux, 16)
                elif name == "turn_m":
                    pool.dma_start(keysT.rearrange("p b n -> p (b n)"), t["keysT"]).then_inc(aux, 16)
                elif name == "spread":
                    for b in range(2):
                        pool.wait_ge(sp_stored[b], 8 * (TOK // SB))
                elif name == "experts":
                    def load_slab(g, b):
                        pool.dma_start(slab[:, b].rearrange("p b i n -> p b (i n)"),
                                       GT[:, :, bass.ds(g * 4, 4), :].rearrange("b p i n -> p b (i n)")).then_inc(slab_full[b], 16)
                    load_slab(0, 0)
                    load_slab(1, 1)
                    with pool.Fori(1, GROUPS // 2) as g:
                        for b in range(2):
                            pool.wait_ge(hid_done, g * 2 + (b - 1))
                            load_slab(g * 2 + b, b)
                elif name == "final2":
                    pool.dma_start(act[:, 4096:4096 + D], t["final_g2"].partition_broadcast(P)).then_inc(aux, 16)
                end(pool, "pool")

        @block.tensor
        def _(pe):
            def xTk(s, k):
                return xT[:, k, s * P:(s + 1) * P]

            for n, (name, l) in enumerate(STAGES):
                begin(pe, n)
                if name == "turn_in":
                    turn_pe(pe, lambda s, k: ztiles(s)[:, k * P:(k + 1) * P])
                elif name == "split_in":
                    for k in range(KT):
                        q = k % 4
                        mm = pe.matmul(ps[32 * q:32 * q + IDX_HEADS, 5, 0:TOK], wtail[:, l, k, :], xT[:, k, :],
                                       start=(k < 4), stop=(k >= KT - 4), tile_position=(0, 32 * q))
                    mm.then_inc(pe_full, 1)
                    pe.wait_ge(part_done, l + 1)
                    for s in range(NT):
                        pe.matmul(ps[:, 6 + s, 0:IDX_HEADS], part_rows[:, s * P:(s + 1) * P], sel16[:, 0:IDX_HEADS],
                                  start=True, stop=True).then_inc(pe_full, 1)
                elif name == "project":
                    stream_pe(pe, f"in{l}", 7, 2, lambda s, k: pair_of(high_in, xT_r, s, k))
                elif name == "turn_a":
                    turn_pe(pe, turn_a_src, blocks=6)
                elif name == "heads_a":
                    pe.wait_ge(aux, aux_at["a", l])
                    for j in range(3):
                        for hd in (2 * j, 2 * j + 1):
                            for k in range(3):
                                mm = pe.matmul(ps[:, j, (hd % 2) * TOK:(hd % 2 + 1) * TOK], w_uq[:, k, hd * HD:(hd + 1) * HD],
                                               cqT[:, k, :], start=(k == 0), stop=(k == 2))
                        mm.then_inc(pe_full, 1)
                    for j in range(3):
                        for hd in (2 * j, 2 * j + 1):
                            for k in range(2):
                                mm = pe.matmul(ps[:, 3 + j, (hd % 2) * TOK:(hd % 2 + 1) * TOK],
                                               w_ukv[:, k, hd * HD:(hd + 1) * HD], ckvT[:, k, :], start=(k == 0), stop=(k == 1))
                        mm.then_inc(pe_full, 1)
                    for s in range(NT):
                        for k in range(3):
                            mm = pe.matmul(ps[:, 6 + s, 0:A_HEADS * A_ROPE], cqT[:, k, s * P:(s + 1) * P],
                                           w_uq[:, k, A_HEADS * HD:], start=(k == 0), stop=(k == 2))
                        mm.then_inc(pe_full, 1)
                elif name == "values_a":
                    for j in range(2):
                        for s in range(NT):
                            for k in range(2):
                                mm = pe.matmul(ps[:, 2 * j + s, 0:384], ckvT[:, k, s * P:(s + 1) * P],
                                               w_ukv[:, k, 768 + j * 384:768 + (j + 1) * 384], start=(k == 0), stop=(k == 1))
                            mm.then_inc(pe_full, 1)
                elif name == "turn_ar":
                    turn_pe(pe, lambda s, k: qr[:, s, k * P:(k + 1) * P], blocks=3)
                elif name in ("attend_a", "attend_b", "attend_c"):
                    between = []
                    if (name, l) in ADA_OF:
                        a, (b, b2) = ADA_OF[name, l], ada_bank(name)
                        between = [lambda: ada_turn(pe, a - 1, b2)] + [lambda j=j: ada_pe(pe, a, b, (j,)) for j in range(4)]
                    attend_pe(pe, name[-1].upper(), l, between)
                elif name == "turn_b":
                    turn_pe(pe, turn_ab_src("B"), blocks=10)
                elif name == "turn_c":
                    turn_pe(pe, turn_ab_src("C"), blocks=10)
                elif name == "turn_idx":
                    turn_pe(pe, idx_src, blocks=5)
                elif name == "index":
                    for c in range(2):
                        r = c * IDX_DIM
                        for j in range(4):
                            mm = pe.matmul(ps[:, c, j * P:(j + 1) * P], qiT[r:r + IDX_DIM, j, 0:P], kiT[r:r + IDX_DIM, 0:P],
                                           start=True, stop=True)
                        mm.then_inc(pe_full, 1)
                    for c in range(2):
                        r = c * IDX_DIM
                        for j in range(4):
                            mm = pe.matmul(ps[:, 2 + 2 * c + j // 2, (j % 2) * TOK:(j % 2 + 1) * TOK],
                                           qiT[r:r + IDX_DIM, j, P:2 * P], kiT[r:r + IDX_DIM, :], start=True, stop=True)
                            if j % 2:
                                mm.then_inc(pe_full, 1)
                elif name == "turn_mix":
                    turn_pe(pe, lambda s, k: zt[:, s, MIX_COL[k]:][:, 0:HD])
                elif name == "project_out":
                    stream_pe(pe, f"out{l}", 2, 2, lambda s, k: pair_of(high_mix, xT_r, s, k))
                elif name == "turn_h":
                    turn_pe(pe, lambda s, k: ht[:, s, k * P:(k + 1) * P])
                elif name == "embed":
                    pe.wait_ge(aux, aux_at["ple", l])
                    for c in range(4):
                        for s in range(NT):
                            for k in range(2):
                                mm = pe.matmul(ps[:, 2 * c + s, :], pT[:, k, s * P:(s + 1) * P],
                                               w_ple[:, k, c * CHUNK:(c + 1) * CHUNK], start=(k == 0), stop=(k == 1))
                            mm.then_inc(pe_full, 1)
                elif name == "gate":
                    stream_pe(pe, f"gate{l}", 2, 2, lambda s, k: pair_of(high_mix, xT_r, s, k))
                elif name == "ada":
                    for a in range(ADA_CHUNKS - ADA_LEFT, ADA_CHUNKS):
                        ada_turn(pe, a - 1, 7)
                        ada_pe(pe, a, 6)
                    ada_turn(pe, ADA_CHUNKS - 1, 7)
                elif name == "turn_x":
                    turn_pe(pe, lambda s, k: ztiles(s)[:, k * P:(k + 1) * P])
                elif name == "turn_ctx":
                    turn_pe(pe, lambda s, k: r2[:, s * D + k * P:][:, 0:P])
                elif name in ("head_norm", "experts_of"):
                    spread_gate_pe(pe, name)
                elif name == "gates":
                    pe.wait_ge(aux, aux_at["wgates"])
                    for c, src in enumerate((xT, cT)):
                        for k in range(KT):
                            q = k % 4
                            mm = pe.matmul(ps[32 * q:32 * q + 16, c, 0:TOK], wgates[:, k, :], src[:, k, :],
                                           start=(k < 4), stop=(k >= KT - 4), tile_position=(0, 32 * q))
                        mm.then_inc(pe_full, 1)
                    pe.wait_ge(part_done, DEPTH + 1)
                    for s in range(4):
                        pe.matmul(ps[:, 2 + s, 0:16], part_rows[:, s * P:(s + 1) * P], sel16[:, :],
                                  start=True, stop=True).then_inc(pe_full, 1)
                elif name == "gate_rows":
                    for dk in range(4):
                        for i, s in enumerate((2, 3, 0, 1)):
                            mm = pe.transpose(ps[:, dk, i * P:(i + 1) * P], gpad[:, dk, s, :], ident[:, :])
                        mm.then_inc(pe_full, 1)
                elif name == "gate_back":
                    for d in range(2):
                        for i in range(4):
                            mm = pe.transpose(ps[:, d, i * P:(i + 1) * P], row((7, 13)[d])[:, i * P:(i + 1) * P], ident[:, :])
                        mm.then_inc(pe_full, 1)
                    for d in range(2):
                        for s in range(NT):
                            c0 = (TOK, 0)[d] + s * P
                            mm = pe.transpose(ps[:, 2, (2 * d + s) * P:(2 * d + s + 1) * P],
                                              row((11, 14)[d])[:, c0:c0 + P], ident[:, :])
                    mm.then_inc(pe_full, 1)
                elif name == "kv":
                    stream_pe(pe, "kv", 2, 4, lambda s, k: pair_of(high_x, xT_r, s, k) if s < 2 else pair_of(high_c, cT_r, s - 2, k), tiles=4)
                elif name in ("mvmk", "mqrq", "query"):
                    def key_scores(c):
                        pe.wait_ge(evac[c % 2], EVAC0[name] + 4 * (c // 2) + 4)
                        for s in range(NT):
                            for b in range(4):
                                mm = pe.matmul(ps[:, 4 * (c % 2) + s, b * P:(b + 1) * P], qT[:, 4 * c + b, s * P:(s + 1) * P],
                                               keysT[:, 4 * c + b, :], start=True, stop=True)
                        mm.then_inc(key_full, 1)

                    for i in range(2 if name == "query" else 1):
                        for par in range(2):
                            chunk = 2 * (PAIR0[name] + i) + par
                            pe.wait_ge(evac[par], EVAC0[name] + 4 * i)
                            if name == "query" and i == 1:
                                pe.wait_ge(key_read, par + 1)
                            if name == "mvmk" and par == 1:
                                pe.wait_ge(evac[0], EVAC0[name] + 4)
                            turned = name == "query" or (name == "mvmk") == (par == 1)
                            high_ = high_2 if name == "query" else high_x
                            for k in range(KT):
                                j = k // PIECE_KT
                                if k % PIECE_KT == 0:
                                    pe.wait_ge(piece_low[j], chunk + 1)
                                flags = (k == 0, k == KT - 1)
                                w0 = (k % PIECE_KT) * CHUNK
                                if turned:
                                    for b in range(4):
                                        wb = weights(j, w0 + b * P, P)
                                        mm = product(pe, ps[:, par * 4 + b, 0:TOK], wb, (high_(k), xT_r[:, k, :]), *flags)
                                        if name == "mvmk":
                                            mm = product(pe, ps[:, b, 0:TOK], wb, (high_c(k), cT_r[:, k, :]), *flags)
                                else:
                                    for s in range(4 if name == "mvmk" else 2):
                                        lhs = pair_of(high_, xT_r, s, k) if s < 2 else pair_of(high_c, cT_r, s - 2, k)
                                        mm = product(pe, ps[:, par * 4 + s, :], lhs, weights(j, w0, CHUNK), *flags)
                                if k % PIECE_KT == PIECE_KT - 1:
                                    mm.then_inc(piece_used[j], 1)
                                if name == "query" and k == PIECE_KT - 1 and 2 * i + par >= 1:
                                    if 2 * i + par == 1:
                                        pe.wait_ge(aux, aux_at["keys"])
                                    key_scores(2 * i + par - 1)
                    if name == "query":
                        key_scores(3)
                elif name == "rgmo":
                    stream_pe(pe, "rgmo", 2, 2, lambda s, k: pair_of(high_xm, xT_r, s, k))
                elif name == "turn_r":
                    def src(s, k):
                        if k < 4:
                            return zt[:, s, RQ + k * P:][:, 0:P]
                        return zt[:, s, RK + (k - 4) * P:][:, 0:P] if k < 8 else czt[:, s, RK + (k - 8) * P:][:, 0:P]
                    turn_pe(pe, src, blocks=12)
                elif name == "retention":
                    def att(u):
                        hd, half = u // 2, u % 2
                        r, b = (hd % 2) * R_DK, hd // 2
                        if u >= 2:
                            pe.wait_ge(re_ready, u - 1)
                        keys_ = rT[:, (4 if half else 8) + b, :]
                        for i in range(2):
                            mm = pe.matmul(ps[:, u % 2, i * TOK:(i + 1) * TOK], keys_[r:r + R_DK, i * P:(i + 1) * P],
                                           rT[r:r + R_DK, b, :], start=True, stop=True)
                        mm.then_inc(re_att, 1)

                    def out(u):
                        hd, half = u // 2, u % 2
                        pe.wait_ge(re_ready, u + 1)
                        if half == 0 and hd >= 2:
                            pe.wait_ge(re_done, hd - 1)
                        v = zt if half else czt
                        for s in range(NT):
                            for i in range(2):
                                mm = pe.matmul(ps[:, 2 + 2 * (hd % 2) + s, 0:R_DV],
                                               work[:, 2 * (u % 2) + 1, i * TOK + s * P:i * TOK + (s + 1) * P],
                                               v[:, i, RV + hd * R_DV:RV + (hd + 1) * R_DV],
                                               start=(half == 0 and i == 0), stop=(half == 1 and i == 1))
                        mm.then_inc(re_out, 1)

                    for u in range(2 * R_HEADS + 1):
                        if u < 2 * R_HEADS:
                            att(u)
                        if u >= 1:
                            out(u - 1)
                elif name == "mlstm":
                    def att(v):
                        hd, d = v // 2, v % 2
                        if d == 0:
                            if hd >= 2:
                                pe.wait_ge(ml_ready, 2 * hd - 2)
                            for i in range(4):
                                kT = conv[:, 8 + hd, i * P:(i + 1) * P] if i < 2 else conv[:, hd, (i - 2) * P:(i - 1) * P]
                                pe.matmul(ps[:, 2 * (hd % 2) + i // 2, (i % 2) * TOK:(i % 2 + 1) * TOK], kT, conv[:, 4 + hd, :],
                                          start=True, stop=True)
                        if v >= 2:
                            pe.wait_ge(ml_arg, v - 1)
                        mm = pe.matmul(ps[:, 4 + v % 2, 0:TOK], ones[32 * hd:32 * hd + 1, :], negm[32 * hd:32 * hd + 1, d, :],
                                       start=True, stop=True, tile_position=(32 * hd, 0))
                        mm.then_inc(ml_att, 1)

                    def out(v):
                        hd, d = v // 2, v % 2
                        pe.wait_ge(ml_ready, v + 1)
                        if v >= 1:
                            pe.wait_ge(ml_done, v)
                        w = work[:, 2 * (v % 2):2 * (v % 2) + 2, :].rearrange("p b n -> p (b n)")
                        for s in range(NT):
                            see = [i for i in range(4) if i < 2 or (i - 2 <= s if d == 0 else i - 2 >= s)]
                            for what in range(2):
                                for i in see:
                                    vals = ones[:, 0:1] if what else (czt if i < 2 else zt)[:, i % 2, MV + hd * M_DV:MV + (hd + 1) * M_DV]
                                    dst = ps[:, 6 + s, M_DV:M_DV + 1] if what else ps[:, 6 + s, 0:M_DV]
                                    mm = pe.matmul(dst, w[:, i * TOK + s * P:i * TOK + (s + 1) * P], vals,
                                                   start=(i == see[0]), stop=(i == see[-1]))
                        mm.then_inc(ml_out, 1)

                    for v in range(2 * M_HEADS + 1):
                        if v < 2 * M_HEADS:
                            att(v)
                        if v >= 1:
                            out(v - 1)
                elif name == "turn_y":
                    turn_pe(pe, lambda s, k: zt[:, s, RG + k * P:][:, 0:P])
                elif name == "merge":
                    for n4 in range(4):
                        for which in range(3):
                            c = 3 * n4 + which
                            chunk = 2 * PAIR0["merge"] + c
                            if n4 >= 1 and which == 0:
                                pe.wait_ge(mg_sig, 2 * n4)
                            if n4 >= 1 and which == 2:
                                pe.wait_ge(mg_sum, n4)
                            for k in range(KT):
                                j = k // PIECE_KT
                                if k % PIECE_KT == 0:
                                    pe.wait_ge(piece_low[j], chunk + 1)
                                w = weights(j, (k % PIECE_KT) * CHUNK, CHUNK)
                                for s in range(NT):
                                    if which < 2:
                                        mm = product(pe, ps[:, 2 * which + s, :], pair_of(high_mix, xT_r, s, k), w, k == 0, k == KT - 1)
                                    else:
                                        mm = product(pe, ps[:, 4 + 2 * (k // 8) + s, :], pair_of(high_y, yT_r, s, k), w,
                                                     k % 8 == 0, k % 8 == 7)
                                if k % PIECE_KT == PIECE_KT - 1:
                                    mm.then_inc(piece_used[j], 1)
                elif name == "turn_m":
                    turn_pe(pe, lambda s, k: ztiles(s)[:, k * P:(k + 1) * P])
                elif name == "out2":
                    stream_pe(pe, "out2", 2, 2, lambda s, k: pair_of(high_2, xT_r, s, k))
                elif name == "turn_2":
                    turn_pe(pe, lambda s, k: ztiles(s)[:, k * P:(k + 1) * P])
                elif name == "turn_sel":
                    for m in range(3):
                        for s in range(NT):
                            mm = pe.transpose(ps[:, m, s * P:(s + 1) * P], sel[m][:, s, :], ident[:, :])
                        mm.then_inc(pe_full, 1)
                elif name == "spread":
                    def block_of_tokens(b, first):
                        for i in range(SB):
                            pe.wait_ge(hot_made, b * SB + (i + 1))
                            if i % 8 == 0:
                                pe.wait_ge(hot_second, b * (SB // 8) + (i // 8 + 1))
                            if i % 4 == 0 and not first:
                                pe.wait_ge(sp_read, b * 8 + (i // 4 - 7))
                            mm = pe.matmul(ps[:, i // 4, (i % 4) * P:(i % 4 + 1) * P], hot1[:, i % 8, :], hot2[:, (i // 8) % 2, i % 8, :],
                                           start=True, stop=True)
                            mm.then_inc(hot_used, 1)

                    block_of_tokens(0, True)
                    with pe.Fori(1, TOK // SB) as b:
                        block_of_tokens(b, False)
                elif name == "experts":
                    def down(g, off):
                        c = expert_chunk(g, off, 0)
                        if not (isinstance(g, int) and 2 * g + off == 0):
                            pe.wait_ge(hid_act, g * 2 + off)
                        for k in range(KT):
                            j = k // PIECE_KT
                            if k % PIECE_KT == 0:
                                pe.wait_ge(piece_low[j], count(c, 1, 1))
                            for b in range(4):
                                mm = product(pe, ps[:, b, 0:TOK], weights(j, (k % PIECE_KT) * CHUNK + b * P, P),
                                             (high_2(k), xT_r[:, k, :]), k == 0, k == KT - 1)
                            if k % PIECE_KT == PIECE_KT - 1:
                                mm.then_inc(piece_used[j], 1)

                    def up(g, off):
                        c = expert_chunk(g, off, 1)
                        pe.wait_ge(hid_done, g * 2 + (off + 1))
                        for dc in range(4):
                            pe.wait_ge(piece_low[dc], count(c, 1, 1))
                            if dc >= 2 or not (isinstance(g, int) and 2 * g + off == 0):
                                pe.wait_ge(up_read, g * 8 + (4 * off + dc - 1))
                            for i in range(4):
                                for s in range(NT):
                                    tok = slice(s * P, (s + 1) * P)
                                    mm = product(pe, ps[:, 4 + 2 * (dc % 2) + s, :], (hid_high[:, off % 2, i, tok], hid_low[:, off % 2, i, tok]),
                                                 weights(dc, i * CHUNK, CHUNK), i == 0, i == 3)
                            mm.then_inc(piece_used[dc], 1)

                    down(0, 0)
                    down(0, 1)
                    up(0, 0)
                    down(0, 2)
                    up(0, 1)
                    with pe.Fori(1, GROUPS // 2 - 1) as g:
                        down(g, 1)
                        up(g, 0)
                        down(g, 2)
                        up(g, 1)
                    down(GROUPS // 2 - 1, 1)
                    up(GROUPS // 2 - 1, 0)
                    up(GROUPS // 2 - 1, 1)
                if (name, l) in ADA_OF and not name.startswith("attend"):
                    a, (b, b2) = ADA_OF[name, l], ada_bank(name)
                    if a >= 1:
                        ada_turn(pe, a - 1, b2)
                    ada_pe(pe, a, b)
                end(pe, "pe")

        @block.scalar
        def _(sc):
            for n, (name, l) in enumerate(STAGES):
                begin(sc, n)
                f0 = full[n]
                if name == "norm":
                    if l == 0:
                        sc.wait_ge(consts, 32)
                    rms_act(sc, rms_k[n], [(ht[:, s, :], D, z[:, 2 * D + s * D:][:, 0:D]) for s in range(NT)], NT)
                elif name == "turn_in":
                    turn_evac(sc, "act", f0, lambda k: xT[:, k, :], scale=lambda k: col(C_NORM + l * KT + k))
                elif name in SPLITS:
                    for x, x_r, high_ in SPLITS[name]:
                        for k in range(KT):
                            sc.copy(high_(k), x[:, k, :]).then_inc(x_high, 1)
                    if name == "split_in":
                        sc.wait_ge(pe_full, f0 + 1)
                        for q in range(4):
                            c = sc.copy(part_rows[32 * q:32 * q + IDX_HEADS, 0:TOK], ps[32 * q:32 * q + IDX_HEADS, 5, 0:TOK])
                        c.then_inc(part_done, 1)
                elif name == "gates":
                    for c in range(2):
                        sc.wait_ge(pe_full, f0 + c + 1)
                        for q in range(4):
                            m = sc.copy(part_rows[32 * q:32 * q + 16, c * TOK:(c + 1) * TOK], ps[32 * q:32 * q + 16, c, 0:TOK])
                    m.then_inc(part_done, 1)
                elif name == "project":
                    if l == 0:
                        sc.activation(trig[:, 1, :, :], zs[:, 128:192].rearrange("p (t n) -> p t n", t=NT), ACT.Sin)
                        sc.activation(trig[:, 0, :, :], zs[:, 192:256].rearrange("p (t n) -> p t n", t=NT), ACT.Sin)
                        sc.activation(st[:, 64:68], st[:, 68:72], ACT.Exp)
                        sc.activation(cols[:, C_SILU:C_SILU + 2 * KT], cols[:, C_SILU:C_SILU + 2 * KT], ACT.Silu)
                    stream_split(sc, split_act, f"in{l}", 7, lambda i, par:
                                 sc.copy(zt[:, 0, bass.ds(i * 1024 + par * CHUNK, CHUNK)], ps[:, par * 2, :]).then_inc(evac[par], 1), ends=True)
                elif name == "prep_a":
                    junk = [act[:, 0:A_Q], act[:, A_Q:2 * A_Q], act[:, 1024:1024 + A_KV], act[:, 1536:1536 + A_KV]]
                    rms_act(sc, rms_k[n], [(zt[:, s, CQ0:CQ0 + A_Q], A_Q, junk[s]) for s in range(NT)] +
                            [(zt[:, s, CKV0:CKV0 + A_KV], A_KV, junk[2 + s]) for s in range(NT)], 4)
                    for g0, w in zip(MIX0, MIXW):
                        sc.activation(zt[:, :, g0:g0 + w], zt[:, :, g0:g0 + w], ACT.Silu)
                elif name == "turn_a":
                    turn_evac(sc, "act", f0, turn_a_dst, blocks=6,
                              scale=lambda k: col(C_QN + l * 3 + k if k < 3 else C_KVN + l * 2 + k - 3))
                elif name == "heads_a":
                    for j in (3, 4, 5):
                        sc.wait_ge(pe_full, f0 + j + 1)
                        sc.copy(knT[:, 2 * j - 6:2 * j - 4, :], ps[:, j, :].rearrange("p (h n) -> p h n", h=2))
                    sc.wait_ge(pe_full, f0 + 8)
                    sc.copy(qr[:, 1, :], ps[:, 7, 0:384])
                elif name == "values_a":
                    for j in range(2):
                        sc.wait_ge(pe_full, f0 + 2 * j + 2)
                        sc.copy(va[:, 1, j * 384:(j + 1) * 384], ps[:, 2 * j + 1, 0:384])
                        sc.copy(va[:, 0, j * 384:(j + 1) * 384], ps[:, 2 * j, 0:384])
                elif name == "turn_ar":
                    turn_evac(sc, "act", f0, lambda k: qrT[:, k, :], blocks=3)
                elif name in ("attend_a", "attend_b", "attend_c"):
                    attend_act(sc, name[-1].upper(), l)
                elif name in ("turn_b", "turn_c"):
                    turn_evac(sc, "act", f0, turn_ab_dst, blocks=10)
                elif name == "turn_idx":
                    turn_evac(sc, "act", f0, lambda k: act[:, 2560 + k * TOK:][:, 0:TOK], blocks=5)
                elif name == "index":
                    for c in range(2):
                        sc.wait_ge(pe_full, f0 + c + 1)
                        sc.activation(rel[:, c:8:2, 0:P], ps[:, c, :].rearrange("p (h n) -> p h n", h=4), ACT.Relu)\
                          .then_inc(rel_done, 1)
                    for c in range(2):
                        for j in range(2):
                            b = 2 + 2 * c + j
                            sc.wait_ge(pe_full, f0 + b + 1)
                            sc.activation(rel[:, 4 * j + c:4 * j + c + 3:2, P:], ps[:, b, :].rearrange("p (h n) -> p h n", h=2), ACT.Relu)\
                              .then_inc(rel_done, 1)
                elif name == "norm_c":
                    rms_act(sc, rms_k[n], None, NT * C_HEADS, have_sums=True)
                elif name == "turn_mix":
                    turn_evac(sc, "act", f0, lambda k: xT[:, k, :])
                elif name == "turn_h":
                    turn_evac(sc, "act", f0, lambda k: xT[:, k, :])
                elif name == "embed":
                    for c in range(4):
                        sc.wait_ge(pe_full, f0 + 2 * c + 1)
                        sc.copy(z[:, c * CHUNK:(c + 1) * CHUNK], ps[:, 2 * c, :])
                elif name == "project_out":
                    stream_split(sc, split_act, f"out{l}", 2, ends=True)
                elif name == "gate":
                    def sigmoids(i, par):
                        c = 2 * i + par
                        if c >= 2:
                            sc.wait_ge(gate_used, l * 4 + c - 1)
                        for s in range(NT):
                            sc.activation(r2[:, (par * 2 + s) * 512:][:, 0:512], ps[:, par * 2 + s, :], ACT.Sigmoid).then_inc(evac[par], 1)
                    stream_split(sc, split_act, f"gate{l}", 2, sigmoids, looped=False, ends=True)
                elif name == "final1":
                    rms_act(sc, rms_k[n], [(ht[:, s, :], D, z[:, 2 * D + s * D:][:, 0:D]) for s in range(NT)], NT)
                elif name == "ada":
                    for a in range(ADA_CHUNKS - ADA_LEFT, ADA_CHUNKS):
                        ada_act(sc, a, 6)
                elif name == "norm_x":
                    sc.wait_ge(consts_p, 16 * 3)
                    rms_act(sc, rms_k[n], [(ht[:, s, :], D, z[:, 2 * D + s * D:][:, 0:D]) for s in range(NT)] +
                            [(r2[:, s * D:(s + 1) * D], D, z[:, 4 * D + s * D:][:, 0:D]) for s in range(NT)], 4)
                elif name == "turn_x":
                    turn_evac(sc, "act", f0, lambda k: xT[:, k, :], scale=lambda k: modc[:, 0, k:k + 1],
                              bias=lambda k: adac[:, k, 0:1])
                elif name == "turn_ctx":
                    turn_evac(sc, "act", f0, lambda k: cT[:, k, :], scale=lambda k: modc[:, 1, k:k + 1],
                              bias=lambda k: adac[:, k, 1:2])
                elif name == "gates_exp":
                    chain(sc, "act", sc.activation(z[:, 2304:2352], z[:, 2304:2352], ACT.Exp, scale=-1.0))
                    sc.activation(z[:, 2304:2352], z[:, 2304:2352], ACT.Ln, bias=1.0)
                elif name == "gate_clamp":
                    sc.activation(row(11)[:, TOK:], row(11)[:, TOK:], ACT.Exp)
                    sc.activation(row(14)[:, 0:TOK], row(12)[:, 2 * TOK - 1:TOK - 1:-1], ACT.Exp)
                elif name == "kv":
                    def out_kv(i, par):
                        for s in (0, 2):
                            sc.copy((zt if s < 2 else czt)[:, 0, (2 * i + par) * CHUNK:][:, 0:CHUNK], ps[:, par * 4 + s, :]).then_inc(evac[par], 1)
                    stream_split(sc, split_act, "kv", 2, out_kv, looped=False)
                elif name == "mvmk":
                    def out_m(i, par):
                        if par == 0:
                            for s in (0, 2):
                                sc.copy((zt if s < 2 else czt)[:, 0, 2048:2560], ps[:, s, :]).then_inc(evac[0], 1)
                        else:
                            for b in (0, 2):
                                sc.copy(raw_x[:, b, :], ps[:, 4 + b, 0:TOK])
                                sc.copy(raw_c[:, b, :], ps[:, b, 0:TOK]).then_inc(evac[1], 1)
                    stream_split(sc, split_act, "mvmk", 1, out_m, looped=False)
                elif name == "mqrq":
                    def out_q(i, par):
                        if par == 0:
                            for b in (0, 2):
                                sc.copy(raw_x[:, 4 + b, :], ps[:, b, 0:TOK]).then_inc(evac[0], 1)
                        else:
                            for c in range(2):
                                sc.copy(zt[:, 0, RQ + c * 256:][:, 0:256], ps[:, 4, c * 256:(c + 1) * 256]).then_inc(evac[1], 1)
                    for k in range(13, 16):
                        sc.copy(high_xm(k), high_x(k))
                    stream_split(sc, split_act, "mqrq", 1, out_q, looped=False)
                elif name == "rgmo":
                    def out_g(i, par):
                        c0 = RG + (2 * i + par) * CHUNK
                        sc.activation(zt[:, 0, c0:c0 + CHUNK], ps[:, par * 2, :], ACT.Silu if i == 0 else ACT.Sigmoid).then_inc(evac[par], 1)
                    stream_split(sc, split_act, "rgmo", 2, out_g, looped=False)
                elif name == "conv":
                    for f, c0 in ((ACT.Silu, RG), (ACT.Sigmoid, MO)):
                        sc.activation(zt[:, 1, c0:c0 + 1024], zt[:, 1, c0:c0 + 1024], f)
                elif name == "conv_silu":
                    sc.activation(act[:, 4096:7168], act[:, 4096:7168], ACT.Silu)
                elif name == "turn_r":
                    turn_evac(sc, "act", f0, lambda k: rT[:, k, :], blocks=12)
                elif name == "retention":
                    sc.wait_ge(aux, aux_at["dist"])
                    for u in range(2 * R_HEADS):
                        hd, half = u // 2, u % 2
                        if u >= 2:
                            sc.wait_ge(re_out, u - 1)
                        for d in range(2):
                            last = sc.activation(work[:, 2 * (u % 2) + d, :].rearrange("p (i n) -> p i n", i=2), dist[:, d, 2 * half:2 * half + 2, :],
                                                 ACT.Exp, scale=st[:, 112 + 8 * d + hd:113 + 8 * d + hd])
                        last.then_inc(re_exp, 1)
                elif name == "mlstm":
                    for v in range(2 * M_HEADS):
                        sc.wait_ge(ml_arg, v + 1)
                        w = work[:, 2 * (v % 2):2 * (v % 2) + 2, :]
                        sc.activation(w, w, ACT.Exp).then_inc(ml_exp, 1)
                elif name == "experts_of":
                    spread_gate_act(sc, f0)
                elif name == "head_norm":
                    spread_gate_act(sc, f0)
                    rms_act(sc, rms_k[n], None, 24, have_sums=True)
                elif name == "turn_y":
                    turn_evac(sc, "act", f0, lambda k: yT[:, k, :])
                elif name == "merge":
                    for n4 in range(4):
                        for which in range(3):
                            c = 2 * PAIR0["merge"] + 3 * n4 + which
                            split_act(sc, (0, c, ADA_CHUNKS), (3,))
                            split_act(sc, (0, c + 1, ADA_CHUNKS), range(3))
                            if which == 0 and n4 >= 1:
                                sc.wait_ge(mg_sum, n4)
                            if which < 2:
                                sc.wait_ge(piece_used[3], c + ADA_CHUNKS + 1)
                                for s in range(NT):
                                    a = sc.activation(r2[:, 2048 + (2 * which + s) * 512:][:, 0:512], ps[:, 2 * which + s, :], ACT.Sigmoid)
                                a.then_inc(mg_sig, 1)
                elif name == "turn_m":
                    turn_evac(sc, "act", f0, lambda k: xT[:, k, :])
                elif name == "norm_2":
                    rms_act(sc, rms_k[n], [(ht[:, s, :], D, z[:, 2 * D + s * D:][:, 0:D]) for s in range(NT)], NT)
                elif name == "turn_2":
                    turn_evac(sc, "act", f0, lambda k: xT[:, k, :], scale=lambda k: modc[:, 2, k:k + 1],
                              bias=lambda k: adac[:, SH2 + k, 0:1])
                elif name == "out2":
                    stream_split(sc, split_act, "out2", 2)
                elif name == "query":
                    def out_query(i, par):
                        for b in (0, 2):
                            sc.copy(qT[:, (2 * i + par) * 4 + b, :], ps[:, par * 4 + b, 0:TOK]).then_inc(evac[par], 1)
                    stream_split(sc, split_act, "query", 2, out_query, looped=False)
                elif name == "soft":
                    for s in range(NT):
                        sc.activation(sel[2][:, s, :], sel[2][:, s, :], ACT.Exp)
                elif name == "spread":
                    def two_blocks(bb, first):
                        for half in range(2):
                            if not first:
                                sc.wait_ge(sp_stored[half], bb * 16)
                            for i in range(SB // 4):
                                sc.wait_ge(hot_used, bb * 64 + (half * SB + 4 * i + 4))
                                sc.copy(stage[:, half, :, 4 * i:4 * i + 4].rearrange("p i n -> p n i"),
                                        ps[:, i, :].rearrange("p (n i) -> p n i", n=4)).then_inc(sp_read, 1)
                            sc.wait_ge(sp_read, bb * (2 * SB // 4) + (half + 1) * (SB // 4))
                            sc.dma_start(GT[bass.ds(bb * 2 + half, 1)].rearrange("b p n i -> p (b n i)"),
                                         stage[:, half].rearrange("p n i -> p (n i)")).then_inc(sp_stored[half], 16)

                    two_blocks(0, True)
                    with sc.Fori(1, TOK // (2 * SB)) as bb:
                        two_blocks(bb, False)
                elif name == "experts":
                    def next_down(g, off):
                        split_act(sc, expert_chunk(g, off - 1, 1), range(3))
                        gelu(g, off)
                        split_act(sc, expert_chunk(g, off - 1, 1), (3,))

                    def gelu(g, off):
                        sc.wait_ge(piece_used[3], place(expert_chunk(g, off, 0), 1, 1))
                        if not (isinstance(g, int) and 2 * g + off < 2):
                            sc.wait_ge(piece_used[3], place(expert_chunk(g, off - 2, 1), 1, 1))
                        sc.activation(hid[:, off % 2], ps[:, 0:4, 0:TOK], ACT.Gelu).then_inc(hid_act, 1)

                    split_act(sc, expert_chunk(0, 0, 0), (3,))
                    split_act(sc, expert_chunk(0, 1, 0), range(3))
                    gelu(0, 0)
                    split_act(sc, expert_chunk(0, 1, 0), (3,))
                    next_down(0, 1)
                    split_act(sc, expert_chunk(0, 2, 0), range(4))
                    next_down(0, 2)
                    split_act(sc, expert_chunk(1, 1, 0), range(4))
                    with sc.Fori(1, GROUPS // 2 - 1) as g:
                        next_down(g, 1)
                        split_act(sc, expert_chunk(g, 2, 0), range(4))
                        next_down(g, 2)
                        split_act(sc, expert_chunk(g, 3, 0), range(4))
                    next_down(GROUPS // 2 - 1, 1)
                    split_act(sc, expert_chunk(GROUPS // 2 - 1, 1, 1), range(4))
                elif name == "final2":
                    for s in range(NT):
                        sc.wait_ge(h_sum, s + 1)
                        last = sc.activation(z[:, 2 * D + s * D:][:, 0:D], ht[:, s, :], ACT.Square, scale=float(D) ** -0.5,
                                             accum_out=rs[:, s:s + 1])
                    last.then_inc(rms_sums, 1)
                    rms_act(sc, rms_k[n], None, NT, have_sums=True)
                if (name, l) in ADA_OF:
                    ada_act(sc, ADA_OF[name, l], ada_bank(name)[0])
                after = PRE_SPLIT.get((name, l))
                if after:
                    split_act(sc, (0, 2 * PAIR0[after], ADA_BEFORE[after]), range(3))
                end(sc, "act")

        @block.vector
        def _(dve):
            def top16(values_, vals, idx, rows):
                for r in range(2):
                    for x in rows:
                        a = dve.max(vals(x)[:, 8 * r:8 * r + 8], values_(x))
                    chain(dve, "dve", a)
                    for x in rows:
                        a = dve.max_index(idx(x)[:, 8 * r:8 * r + 8], vals(x)[:, 8 * r:8 * r + 8], values_(x))
                    chain(dve, "dve", a)
                    if r == 0:
                        for x in rows:
                            a = dve.match_replace(values_(x), vals(x)[:, 0:8], values_(x), -3e38)
                        chain(dve, "dve", a)
            for n, (name, l) in enumerate(STAGES):
                begin(dve, n)
                f0 = full[n]
                if name == "setup":
                    chain(dve, "dve", dve.memset(mask[:, :], 0.0))
                    dve.memset(mask[0:64, 64:128], NEG)
                    dve.memset(mask[0:64, 128 + 192:], NEG)
                elif name == "norm":
                    rms_dve(dve, rms_k[n], NT, sums=rms_s[n])
                    for s in range(NT):
                        dve.tensor_scalar(ztiles(s), ht[:, s, :], rs[:, 64 + s:65 + s], None, ALU.mult)
                elif name == "turn_in":
                    turn_evac(dve, "dve", f0, lambda k: xT[:, k, :], scale=lambda k: col(C_NORM + l * KT + k))
                elif name in SPLITS:
                    if name == "split_in":
                        dve.wait_ge(pe_full, f0 + 1)
                    made_ = high0[n]
                    for x, x_r, high_ in SPLITS[name]:
                        for k in range(KT):
                            made_ += 1
                            dve.wait_ge(x_high, made_)
                            dve.tensor_tensor(x_r[:, k, :], x[:, k, :], high_(k), ALU.subtract)
                    if name == "split_in":
                        for s in range(NT):
                            dve.wait_ge(pe_full, f0 + s + 2)
                            dve.tensor_copy(zt[:, s, WI0:WI0 + IDX_HEADS], ps[:, 6 + s, 0:IDX_HEADS])
                elif name == "join":
                    for k in range(KT):
                        dve.tensor_tensor(xT[:, k, :], xT_r[:, k, :], high_xm(k), ALU.add)
                elif name == "project":
                    stream_split(dve, split_dve, f"in{l}", 7, lambda i, par:
                                 dve.tensor_copy(zt[:, 1, bass.ds(i * 1024 + par * CHUNK, CHUNK)], ps[:, par * 2 + 1, :]).then_inc(evac[par], 1), ends=True)
                elif name == "prep_a":
                    kr = zt[:, :, KR0:KR0 + A_ROPE].unsqueeze(2)
                    kd1 = kd[:, :, 0:64].unsqueeze(2)
                    rope(dve, kr[:, :, :, 0:32], kr[:, :, :, 32:64], 1, 32, lambda i, w: r2[:, i * 384:][:, 0:w],
                         kd1[:, :, :, 0:32], kd1[:, :, :, 32:64])
                    dve.tensor_copy(kd[:, :, 64:128], kd[:, :, 0:64])
                    rms_dve(dve, rms_k[n], 4, sums=rms_s[n])
                    for s in range(NT):
                        dve.tensor_scalar(zt[:, s, CQ0:CQ0 + A_Q], zt[:, s, CQ0:CQ0 + A_Q], rs[:, 64 + s:65 + s], None, ALU.mult)
                        dve.tensor_scalar(zt[:, s, CKV0:CKV0 + A_KV], zt[:, s, CKV0:CKV0 + A_KV], rs[:, 66 + s:67 + s], None, ALU.mult)
                elif name == "turn_a":
                    for j in (0, 2):
                        dve.wait_ge(pe_full, f0 + j + 1)
                        for k in (2 * j, 2 * j + 1):
                            src = ps[:, j, (k % 2) * TOK:(k % 2 + 1) * TOK]
                            if k == 5:
                                dve.tensor_copy(kpeT, src)
                            else:
                                dve.tensor_scalar(turn_a_dst(k), src, col(C_QN + l * 3 + k if k < 3 else C_KVN + l * 2 + k - 3),
                                                  None, ALU.mult)
                elif name == "heads_a":
                    for j in range(3):
                        dve.wait_ge(pe_full, f0 + j + 1)
                        dve.tensor_copy(qnT[:, 2 * j:2 * j + 2, :], ps[:, j, :].rearrange("p (h n) -> p h n", h=2))
                    dve.wait_ge(pe_full, f0 + 7)
                    dve.tensor_copy(qr[:, 0, :], ps[:, 6, 0:384])
                elif name == "values_a":
                    q = qr.rearrange("p t (h d) -> p t h d", h=A_HEADS)
                    rope(dve, q[:, :, :, 0:32], q[:, :, :, 32:64], A_HEADS, 32,
                         lambda i, w: (act[:, 3072 + i * 384:] if i < 2 else r2[:, 4096 + (i - 2) * 384:])[:, 0:w])
                elif name == "turn_ar":
                    turn_evac(dve, "dve", f0, lambda k: qrT[:, k, :], blocks=3)
                elif name in ("attend_a", "attend_b", "attend_c"):
                    attend_dve(dve, name[-1].upper(), l)
                elif name == "prep_b":
                    def tmp(i, w):
                        return r2[:, i * 160:][:, 0:w]
                    for c0 in (QB0, KB0):
                        rope(dve, heads_of(c0, B_HEADS, HD, 0, 16), heads_of(c0, B_HEADS, HD, 16, 32), B_HEADS, 16, tmp)
                    rope(dve, heads_of(QI0, IDX_HEADS, IDX_DIM, 0, 8), heads_of(QI0, IDX_HEADS, IDX_DIM, 8, 16), IDX_HEADS, 8, tmp)
                    rope(dve, heads_of(KI0, 1, IDX_DIM, 0, 8), heads_of(KI0, 1, IDX_DIM, 8, 16), 1, 8, tmp)
                    dve.tensor_copy(kid[:, :, 0:64], zt[:, :, KI0:KI0 + IDX_DIM])
                    dve.tensor_copy(kid[:, :, 64:128], zt[:, :, KI0:KI0 + IDX_DIM])
                elif name in ("turn_b", "turn_c"):
                    turn_evac(dve, "dve", f0, turn_ab_dst, blocks=10)
                elif name == "turn_idx":
                    turn_evac(dve, "dve", f0, lambda k: act[:, 2560 + k * TOK:][:, 0:TOK], blocks=5)
                elif name == "index":
                    dve.wait_ge(rel_done, l * 6 + 6)
                    for hd in range(IDX_HEADS):
                        for s in range(NT):
                            nk, m0 = keys(s)
                            wi = zt[:, s, WI0 + hd:WI0 + hd + 1]
                            o = score[:, m0:m0 + nk]
                            if hd == 0:
                                a = dve.tensor_scalar(o, rel[:, hd, m0:m0 + nk], wi, None, ALU.mult)
                            else:
                                a = dve.scalar_tensor_tensor(o, rel[:, hd, m0:m0 + nk], wi, o, ALU.mult, ALU.add)
                        chain(dve, "dve", a)
                elif name == "select":
                    TAKEN = -3e38
                    chain(dve, "dve", dve.tensor_tensor(kept, score, mask[:, :], ALU.add))
                    for r in range(N_SEL // 8):
                        for s in range(NT):
                            nk, m0 = keys(s)
                            a = dve.max(st[:, 90 + 8 * s:98 + 8 * s], kept[:, m0:m0 + nk])
                        chain(dve, "dve", a)
                        for s in range(NT):
                            nk, m0 = keys(s)
                            a = dve.match_replace(kept[:, m0:m0 + nk], st[:, 90 + 8 * s:98 + 8 * s], kept[:, m0:m0 + nk], TAKEN)
                        chain(dve, "dve", a)
                    chain(dve, "dve", dve.tensor_scalar(kept, kept, -2e38, NEG, ALU.is_gt, ALU.mult))
                    dve.tensor_tensor(score, kept, mask[:, :], ALU.add)
                elif name == "prep_c":
                    for c0 in (QC0, KC0):
                        rope(dve, heads_of(c0, 2 * C_HEADS, C_QK, 0, 8), heads_of(c0, 2 * C_HEADS, C_QK, 8, 16), 2 * C_HEADS, 8,
                             lambda i, w: r2[:, 4096 + i * 160:][:, 0:w])
                elif name == "norm_c":
                    for s in range(NT):
                        a = dve.tensor_tensor(norm_c_sq[:, s], norm_c_in[:, s], norm_c_in[:, s], ALU.mult)
                    chain(dve, "dve", a)
                    chain(dve, "dve", dve.tensor_reduce(rs[:, 0:10], r2[:, 0:1280].rearrange("p (h d) -> p h d", d=HD), AX_X, ALU.add))
                    chain(dve, "dve", dve.tensor_scalar(rs[:, 0:10], rs[:, 0:10], 1.0 / HD, None, ALU.mult))
                    rms_dve(dve, rms_k[n], 10)
                    for s in range(NT):
                        for hd in range(C_HEADS):
                            g0 = GC0 + hd * HD
                            a = dve.scalar_tensor_tensor(norm_c_sq[:, s, hd], norm_c_in[:, s, hd], rs[:, 64 + s * 5 + hd:65 + s * 5 + hd],
                                                         bc[:, B_SUB + l * HD:][:, 0:HD], ALU.mult, ALU.mult)
                        chain(dve, "dve", a)
                        dve.tensor_tensor(zt[:, s, GC0:GC0 + 640], r2[:, s * 640:(s + 1) * 640], zt[:, s, GC0:GC0 + 640], ALU.mult)
                elif name in ("turn_mix", "turn_h"):
                    turn_evac(dve, "dve", f0, lambda k: xT[:, k, :])
                elif name == "project_out":
                    def add_out(i, par):
                        for s in range(NT):
                            hc = ht[:, s, bass.ds(i * 1024 + par * CHUNK, CHUNK)]
                            dve.tensor_tensor(hc, ps[:, par * 2 + s, :], hc, ALU.add).then_inc(evac[par], 1)
                    stream_split(dve, split_dve, f"out{l}", 2, add_out, ends=True)
                elif name == "embed":
                    for c in range(4):
                        dve.wait_ge(pe_full, f0 + 2 * c + 2)
                        dve.tensor_copy(z[:, D + c * CHUNK:][:, 0:CHUNK], ps[:, 2 * c + 1, :])
                elif name == "gate":
                    e0 = EVAC0[f"gate{l}"]
                    def apply(i, par):
                        c = 2 * i + par
                        dve.wait_ge(evac[par], e0 + 2 * i + 2)
                        for s in range(NT):
                            g = r2[:, (par * 2 + s) * 512:][:, 0:512]
                            a = dve.tensor_tensor(g, g, ztiles(s)[:, c * CHUNK:(c + 1) * CHUNK], ALU.mult)
                        chain(dve, "dve", a)
                        for s in range(NT):
                            g = r2[:, (par * 2 + s) * 512:][:, 0:512]
                            hc = ht[:, s, c * CHUNK:(c + 1) * CHUNK]
                            a = dve.tensor_tensor(hc, hc, g, ALU.add)
                        a.then_inc(gate_used, 1)
                    stream_split(dve, split_dve, f"gate{l}", 2, apply, looped=False, ends=True)
                elif name == "final1":
                    rms_dve(dve, rms_k[n], NT, sums=rms_s[n])
                    dve.wait_ge(aux, aux_at["final"])
                    for s in range(NT):
                        dve.scalar_tensor_tensor(ht[:, s, :], ht[:, s, :], rs[:, 64 + s:65 + s], act[:, W0:W0 + D], ALU.mult, ALU.mult)
                elif name == "ada":
                    for a in range(ADA_CHUNKS - ADA_LEFT - 1, ADA_CHUNKS):
                        ada_dve(dve, a, 7)
                elif name == "mod_cols":
                    dve.wait_ge(consts_p, 16 * 3)
                    chain(dve, "dve", dve.tensor_tensor(adac[:, :, :], adac[:, :, :], b_ada.unsqueeze(2).to_broadcast([P, 6 * KT, 2]), ALU.add))
                    for m, (g0, sec, r) in enumerate(((C_N1, SC1, 0), (C_N1, SC1, 1), (C_N2, SC2, 0))):
                        chain(dve, "dve", dve.tensor_scalar(modc[:, m, :], adac[:, sec:sec + KT, r], 1.0, None, ALU.add))
                        dve.tensor_tensor(modc[:, m, :], modc[:, m, :], cols[:, g0:g0 + KT], ALU.mult)
                elif name == "norm_x":
                    dve.wait_ge(consts_p, 16 * 3)
                    rms_dve(dve, rms_k[n], 4, sums=rms_s[n])
                    for s in range(NT):
                        dve.tensor_scalar(ztiles(s), ht[:, s, :], rs[:, 64 + s:65 + s], None, ALU.mult)
                        dve.tensor_scalar(r2[:, s * D:(s + 1) * D], r2[:, s * D:(s + 1) * D], rs[:, 66 + s:67 + s], None, ALU.mult)
                elif name == "turn_x":
                    turn_evac(dve, "dve", f0, lambda k: xT[:, k, :], scale=lambda k: modc[:, 0, k:k + 1],
                              bias=lambda k: adac[:, k, 0:1])
                elif name == "turn_ctx":
                    turn_evac(dve, "dve", f0, lambda k: cT[:, k, :], scale=lambda k: modc[:, 1, k:k + 1],
                              bias=lambda k: adac[:, k, 1:2])
                elif name == "gates":
                    chain(dve, "dve", dve.memset(z[:, 0:2048], 0.0))
                    bias = bc[:, B_MGB:B_MGB + 16].rearrange("p (d h) -> p d h", h=M_HEADS)
                    for s in range(4):
                        dve.wait_ge(pe_full, f0 + s + 3)
                        a = dve.tensor_tensor(gpad[:, :, s, 0:P:32], ps[:, 2 + s, 0:16].rearrange("p (d h) -> p d h", h=M_HEADS), bias, ALU.add)
                    chain(dve, "dve", a)
                    for d in range(2):
                        dve.scalar_tensor_tensor(z[:, 2304 + 16 * d:2320 + 16 * d].rearrange("p (s h) -> p s h", s=4),
                                                 gpad[:, 2 * d + 1, :, 0:P:32], -1.0, gpad[:, 2 * d + 1, :, 0:P:32], ALU.mult, ALU.max)
                    rd = bc[:, B_RDEC:B_RDEC + 16]
                    dve.scalar_tensor_tensor(z[:, 2336:2352], rd, -1.0, rd, ALU.mult, ALU.max)
                elif name == "gates_log":
                    for d in range(2):
                        f = gpad[:, 2 * d + 1, :, 0:P:32]
                        dve.scalar_tensor_tensor(f, f, 0.0, z[:, 2304 + 16 * d:2320 + 16 * d].rearrange("p (s h) -> p s h", s=4),
                                                 ALU.min, ALU.subtract)
                    rd = bc[:, B_RDEC:B_RDEC + 16]
                    chain(dve, "dve", dve.scalar_tensor_tensor(st[:, 112:128], rd, 0.0, z[:, 2336:2352], ALU.min, ALU.subtract))
                    dve.tensor_scalar(st[:, 112:128], st[:, 112:128], -1e-20, None, ALU.min)
                elif name == "gate_rows":
                    F, I, B, X, M, EN = (0, 1), (2, 3), (5, 6), (7, 8), (9, 10), (11, 12)
                    for dk in range(4):
                        d, kind = dk // 2, dk % 2
                        dst = row((I, F)[kind][d])
                        dve.wait_ge(pe_full, f0 + dk + 1)
                        if d == 0:
                            dve.tensor_copy(dst, ps[:, dk, :])
                        else:
                            dve.tensor_copy(dst[:, 0:TOK], ps[:, dk, TOK - 1::-1])
                            dve.tensor_copy(dst[:, TOK:], ps[:, dk, 2 * TOK - 1:TOK - 1:-1])
                    chain(dve, "dve", dve.memset(row(4), 0.0))
                    for d in range(2):
                        chain(dve, "dve", dve.tensor_tensor_scan(row(B[d]), row(F[d]), row(4), 0.0, ALU.add, ALU.add))
                    for d in range(2):
                        a = dve.tensor_tensor(row(X[d]), row(I[d]), row(B[d]), ALU.subtract)
                    chain(dve, "dve", a)
                    for d in range(2):
                        chain(dve, "dve", dve.tensor_tensor_scan(row(M[d]), row(X[d]), row(X[d]), 0.0, ALU.max, ALU.max))
                    for d in range(2):
                        chain(dve, "dve", dve.tensor_tensor(row(EN[d])[:, TOK:], row(B[d])[:, TOK:], row(M[d])[:, TOK:], ALU.add))
                        dve.tensor_scalar(row(EN[d])[:, TOK:], row(EN[d])[:, TOK:], -1.0, 88.0, ALU.mult, ALU.min)
                    dve.tensor_scalar(negm[:, 0, :], row(M[0])[:, TOK:], -1.0, None, ALU.mult)
                    dve.tensor_scalar(negm[:, 1, :], row(M[1])[:, 2 * TOK - 1:TOK - 1:-1], -1.0, None, ALU.mult)
                    dve.tensor_copy(row(13)[:, 0:TOK], row(X[1])[:, TOK - 1::-1])
                    dve.tensor_copy(row(13)[:, TOK:], row(X[1])[:, 2 * TOK - 1:TOK - 1:-1])
                elif name == "gate_back":
                    for b in range(3):
                        dve.wait_ge(pe_full, f0 + b + 1)
                        dve.tensor_copy(mcols[:, 4 * b:4 * b + 4, :], ps[:, b, :].rearrange("p (i n) -> p i n", i=4)[:, :, 0:P:32])
                elif name == "kv":
                    def out_kv(i, par):
                        for s in (1, 3):
                            dve.tensor_copy((zt if s < 2 else czt)[:, 1, (2 * i + par) * CHUNK:][:, 0:CHUNK], ps[:, par * 4 + s, :])\
                               .then_inc(evac[par], 1)
                    stream_split(dve, split_dve, "kv", 2, out_kv, looped=False)
                elif name == "mvmk":
                    def out_m(i, par):
                        if par == 0:
                            for s in (1, 3):
                                dve.tensor_copy((zt if s < 2 else czt)[:, 1, 2048:2560], ps[:, s, :]).then_inc(evac[0], 1)
                        else:
                            for b in (1, 3):
                                dve.tensor_copy(raw_x[:, b, :], ps[:, 4 + b, 0:TOK])
                                dve.tensor_copy(raw_c[:, b, :], ps[:, b, 0:TOK]).then_inc(evac[1], 1)
                    stream_split(dve, split_dve, "mvmk", 1, out_m, looped=False)
                elif name == "mqrq":
                    def out_q(i, par):
                        if par == 0:
                            for b in (1, 3):
                                dve.tensor_copy(raw_x[:, 4 + b, :], ps[:, b, 0:TOK]).then_inc(evac[0], 1)
                        else:
                            for c in range(2):
                                dve.tensor_copy(zt[:, 1, RQ + c * 256:][:, 0:256], ps[:, 5, c * 256:(c + 1) * 256]).then_inc(evac[1], 1)
                    stream_split(dve, split_dve, "mqrq", 1, out_q, looped=False)
                elif name == "rgmo":
                    def out_g(i, par):
                        c0 = RG + (2 * i + par) * CHUNK
                        dve.tensor_copy(zt[:, 1, c0:c0 + CHUNK], ps[:, par * 2 + 1, :]).then_inc(evac[par], 1)
                    stream_split(dve, split_dve, "rgmo", 2, out_g, looped=False)
                elif name == "conv":
                    def tap(i, ch):
                        return cols[:, C_CONV + i * 8 + ch:C_CONV + i * 8 + ch + 1]
                    def parts(b):
                        return (raw_x[:, b, :], b + 4 if b < 4 else b - 4) if b < 8 else (raw_c[:, b - 8, :], b - 4)
                    for step in range(3):
                        for b in range(12):
                            x, ch = parts(b)
                            o = conv[:, b, :]
                            if step == 0:
                                a = dve.tensor_scalar(o, x, tap(1, ch), None, ALU.mult)
                            elif step == 1:
                                a = dve.scalar_tensor_tensor(o[:, 1:], x[:, 0:TOK - 1], tap(0, ch), o[:, 1:], ALU.mult, ALU.add)
                            else:
                                a = dve.scalar_tensor_tensor(o[:, 0:TOK - 1], x[:, 1:], tap(2, ch), o[:, 0:TOK - 1], ALU.mult, ALU.add)
                        chain(dve, "dve", a)
                    dve.wait_ge(consts_p, 16 * 3)
                    def tmp2(i, w):
                        return act[:, 8192 + i * 512:][:, 0:w]
                    for c0 in (RQ, RK):
                        rope(dve, heads_of(c0, R_HEADS, R_DK, 0, 32), heads_of(c0, R_HEADS, R_DK, 32, 64), R_HEADS, 32, tmp2)
                elif name == "turn_r":
                    turn_evac(dve, "dve", f0, lambda k: rT[:, k, :], blocks=12)
                elif name == "retention":
                    def ready(u):
                        dve.wait_ge(re_exp, u + 1)
                        e, w = work[:, 2 * (u % 2), :], work[:, 2 * (u % 2) + 1, :]
                        chain(dve, "dve", dve.tensor_tensor(e, e, w, ALU.add))
                        dve.wait_ge(re_att, u + 1)
                        dve.scalar_tensor_tensor(w, ps[:, u % 2, :], R_DK ** -0.5, e, ALU.mult, ALU.mult).then_inc(re_ready, 1)

                    def done(hd):
                        dve.wait_ge(re_out, 2 * hd + 2)
                        for s in range(NT):
                            a = dve.tensor_copy(zt[:, s, RV + hd * R_DV:RV + (hd + 1) * R_DV], ps[:, 2 + 2 * (hd % 2) + s, 0:R_DV])
                        a.then_inc(re_done, 1)

                    for u in range(2 * R_HEADS):
                        ready(u)
                        if u >= 2 and u % 2 == 0:
                            done(u // 2 - 1)
                    done(R_HEADS - 1)
                elif name == "mlstm":
                    def arg(v):
                        hd, d = v // 2, v % 2
                        dve.wait_ge(ml_att, v + 1)
                        if v >= 2:
                            dve.wait_ge(ml_out, v - 1)
                        w = work[:, 2 * (v % 2):2 * (v % 2) + 2, :].rearrange("p b n -> p (b n)")
                        for i in range(4):
                            a = dve.tensor_scalar(w[:, i * TOK:(i + 1) * TOK], ps[:, 4 + v % 2, 0:TOK], mcols[:, 4 * d + i, hd:hd + 1], 0.0,
                                                  ALU.add, ALU.min)
                        a.then_inc(ml_arg, 1)

                    def ready(v):
                        hd, d = v // 2, v % 2
                        dve.wait_ge(ml_exp, v + 1)
                        lat = work[:, 2 * (v % 2) + 1, :]
                        chain(dve, "dve", dve.scalar_tensor_tensor(lat, dist[:, d, 2:4, :].rearrange("p i n -> p (i n)"), 1e29, lat,
                                                                   ALU.is_lt, ALU.mult))
                        for half in range(2):
                            w = work[:, 2 * (v % 2) + half, :]
                            a = dve.scalar_tensor_tensor(w, ps[:, 2 * (hd % 2) + half, :], M_DK ** -0.5, w, ALU.mult, ALU.mult)
                        a.then_inc(ml_ready, 1)

                    def done(v):
                        hd, d = v // 2, v % 2
                        dve.wait_ge(ml_out, v + 1)
                        y0 = (RK if hd < 2 else RQ) + (hd % 2) * M_DV
                        den = ps[:, 6:8, M_DV]
                        clamp = mcols[:, 8 + 2 * d:10 + 2 * d, hd]
                        a, b = st[:, 80:82], st[:, 82:84]
                        chain(dve, "dve", dve.tensor_copy(b, den))
                        chain(dve, "dve", dve.scalar_tensor_tensor(a, b, -1.0, b, ALU.mult, ALU.max))
                        chain(dve, "dve", dve.tensor_tensor(a, a, clamp, ALU.max))
                        chain(dve, "dve", dve.reciprocal(a, a))
                        for s in range(NT):
                            y = zt[:, s, y0:y0 + M_DV]
                            if d == 0:
                                m = dve.tensor_scalar(y, ps[:, 6 + s, 0:M_DV], a[:, s:s + 1], None, ALU.mult)
                            else:
                                m = dve.scalar_tensor_tensor(y, ps[:, 6 + s, 0:M_DV], a[:, s:s + 1], y, ALU.mult, ALU.add)
                        m.then_inc(ml_done, 1)

                    for v in range(2 * M_HEADS + 2):
                        if 1 <= v <= 2 * M_HEADS:
                            ready(v - 1)
                        if v >= 2:
                            done(v - 2)
                        if v < 2 * M_HEADS:
                            arg(v)
                elif name == "head_norm":
                    spread_gate_dve(dve, name)
                    yr = zt[:, :, RV:RV + 1024].rearrange("p t (h d) -> p t h d", h=R_HEADS)
                    ym = [zt[:, :, c0:c0 + 512].rearrange("p t (h d) -> p t h d", h=2) for c0 in (RK, RQ)]
                    groups = [(yr, R_HEADS, R_DV, 0)] + [(y, 2, M_DV, 16 + 4 * i) for i, y in enumerate(ym)]
                    def stat(tile_, c0, heads):
                        return tile_[:, c0:c0 + NT * heads].rearrange("p (t h) -> p t h", t=NT)
                    for y, heads, dv, c0 in groups:
                        a = dve.tensor_reduce(stat(st, c0, heads), y, AX_X, ALU.add)
                    chain(dve, "dve", a)
                    dve.tensor_scalar(st[:, 0:16], st[:, 0:16], 1.0 / R_DV, None, ALU.mult)
                    chain(dve, "dve", dve.tensor_scalar(st[:, 16:24], st[:, 16:24], 1.0 / M_DV, None, ALU.mult))
                    for y, heads, dv, c0 in groups:
                        a = dve.tensor_tensor(y, y, stat(st, c0, heads).unsqueeze(3).to_broadcast([P, NT, heads, dv]), ALU.subtract)
                    chain(dve, "dve", a)
                    sq = [act[:, o:o + NT * heads * dv].rearrange("p (t h d) -> p t h d", t=NT, h=heads)
                          for o, (y, heads, dv, c0) in zip((4096, 6144, 7168), groups)]
                    for q, (y, heads, dv, c0) in zip(sq, groups):
                        a = dve.tensor_tensor(q, y, y, ALU.mult)
                    chain(dve, "dve", a)
                    for q, (y, heads, dv, c0) in zip(sq, groups):
                        a = dve.tensor_reduce(stat(rs, c0, heads), q, AX_X, ALU.add)
                    chain(dve, "dve", a)
                    dve.tensor_scalar(rs[:, 0:16], rs[:, 0:16], 1.0 / R_DV, None, ALU.mult)
                    chain(dve, "dve", dve.tensor_scalar(rs[:, 16:24], rs[:, 16:24], 1.0 / M_DV, None, ALU.mult))
                    rms_dve(dve, rms_k[n], 24)
                    for y, heads, dv, c0 in groups:
                        a = dve.tensor_tensor(y, y, stat(rs, 64 + c0, heads).unsqueeze(3).to_broadcast([P, NT, heads, dv]), ALU.mult)
                    chain(dve, "dve", a)
                    for s in range(NT):
                        dve.tensor_tensor(zt[:, s, RG:RG + 1024], zt[:, s, RG:RG + 1024], zt[:, s, RV:RV + 1024], ALU.mult)
                        for i, c0 in enumerate((RK, RQ)):
                            m0 = MO + i * 512
                            dve.tensor_tensor(zt[:, s, m0:m0 + 512], zt[:, s, m0:m0 + 512], zt[:, s, c0:c0 + 512], ALU.mult)
                elif name == "turn_y":
                    turn_evac(dve, "dve", f0, lambda k: yT[:, k, :])
                elif name == "merge":
                    for n4 in range(4):
                        for which in range(3):
                            c = 2 * PAIR0["merge"] + 3 * n4 + which
                            split_dve(dve, (0, c, ADA_CHUNKS), (3,))
                            split_dve(dve, (0, c + 1, ADA_CHUNKS), range(3))
                            if which == 2:
                                dve.wait_ge(mg_sig, 2 * n4 + 2)
                                dve.wait_ge(piece_used[3], c + ADA_CHUNKS + 1)
                                g = [r2[:, 2048 + i * 512:2560 + i * 512] for i in range(4)]
                                for i in range(4):
                                    a = dve.tensor_tensor(g[i], g[i], ps[:, 4 + i, :], ALU.mult)
                                chain(dve, "dve", a)
                                for s in range(NT):
                                    a = dve.tensor_tensor(ztiles(s)[:, n4 * CHUNK:(n4 + 1) * CHUNK], g[s], g[2 + s], ALU.add)
                                a.then_inc(mg_sum, 1)
                elif name == "turn_m":
                    turn_evac(dve, "dve", f0, lambda k: xT[:, k, :])
                elif name == "out2":
                    def add_gated(i, par):
                        c = 2 * i + par
                        for s in range(NT):
                            a = dve.tensor_tensor(ztiles(s)[:, c * CHUNK:(c + 1) * CHUNK], ps[:, par * 2 + s, :], gt[:, c * CHUNK:(c + 1) * CHUNK], ALU.mult)
                            a.then_inc(evac[par], 1)
                        dve.wait_ge(evac[par], EVAC0["out2"] + 2 * i + 2)
                        for s in range(NT):
                            hc = ht[:, s, c * CHUNK:(c + 1) * CHUNK]
                            dve.tensor_tensor(hc, hc, ztiles(s)[:, c * CHUNK:(c + 1) * CHUNK], ALU.add)
                    stream_split(dve, split_dve, "out2", 2, add_gated, looped=False)
                elif name == "norm_2":
                    rms_dve(dve, rms_k[n], NT, sums=rms_s[n])
                    for s in range(NT):
                        dve.tensor_scalar(ztiles(s), ht[:, s, :], rs[:, 64 + s:65 + s], None, ALU.mult)
                elif name == "turn_2":
                    turn_evac(dve, "dve", f0, lambda k: xT[:, k, :], scale=lambda k: modc[:, 2, k:k + 1],
                              bias=lambda k: adac[:, SH2 + k, 0:1])
                elif name == "query":
                    def out_query(i, par):
                        for b in (1, 3):
                            dve.tensor_copy(qT[:, (2 * i + par) * 4 + b, :], ps[:, par * 4 + b, 0:TOK]).then_inc(evac[par], 1)

                    def read_scores(c):
                        dve.wait_ge(key_full, c + 1)
                        for s in range(NT):
                            m = dve.tensor_copy(S[:, s, 4 * c:4 * c + 4, :], ps[:, 4 * (c % 2) + s, :].rearrange("p (b n) -> p b n", b=4))
                        m.then_inc(key_read, 1)

                    def top_of(c, s):
                        dve.wait_ge(key_read, c + 1)
                        top16(lambda x: S[:, x[0], x[1], :], lambda x: sv[:, x[0], x[1], :], lambda x: si[:, x[0], x[1], :],
                              [(s, b) for b in range(4 * c, 4 * c + 4)])

                    for c in range(4):
                        this, after = (0, 2 * PAIR0["query"] + c, ADA_CHUNKS), (0, 2 * PAIR0["query"] + c + 1, ADA_CHUNKS)
                        split_dve(dve, this, (3,))
                        if c >= 1:
                            read_scores(c - 1)
                            top_of(c - 1, 0)
                        split_dve(dve, after, range(2))
                        if c >= 1:
                            top_of(c - 1, 1)
                        split_dve(dve, after, (2,))
                        dve.wait_ge(piece_used[3], place(this, 1, 1))
                        out_query(c // 2, c % 2)
                    read_scores(3)
                    top_of(3, 0)
                    top_of(3, 1)
                elif name == "top_keys":
                    dve.tensor_copy(z[:, 5120:5632], z[:, 4608:5120].bitcast(U32))
                    svp = z[:, 4096:4608].rearrange("p (s h f n) -> p s h f n", s=NT, h=P_HEADS, f=2)
                    for s in range(NT):
                        a = dve.tensor_tensor(cand[:, s].rearrange("p h (i j) -> p h i j", i=16),
                                              svp[:, s, :, 0, :].unsqueeze(3).to_broadcast([P, P_HEADS, 16, 16]),
                                              svp[:, s, :, 1, :].unsqueeze(2).to_broadcast([P, P_HEADS, 16, 16]), ALU.add)
                    chain(dve, "dve", a)
                    rows = [(s, b) for s in range(NT) for b in range(P_HEADS)]
                    top16(lambda x: cand[:, x[0], x[1], :], lambda x: bs[:, x[0], x[1], :], lambda x: bjv[:, x[0], x[1], :], rows)
                    for s in range(NT):
                        dve.tensor_tensor(sel[2][:, s, :].rearrange("p (h n) -> p h n", n=16), bs[:, s], bs[:, s, :, 0:1].to_broadcast([P, P_HEADS, 16]),
                                          ALU.subtract)
                elif name == "experts_of":
                    spread_gate_dve(dve, name)
                    for s in range(NT):
                        a = dve.tensor_reduce(st[:, 8 * s:8 * s + 8], sel[2][:, s, :].rearrange("p (h n) -> p h n", n=16), AX_X, ALU.add)
                    chain(dve, "dve", a)
                    chain(dve, "dve", dve.reciprocal(st[:, 0:16], st[:, 0:16]))
                    for s in range(NT):
                        g = sel[2][:, s, :].rearrange("p (h n) -> p h n", n=16)
                        dve.tensor_tensor(g, g, st[:, 8 * s:8 * s + 8].unsqueeze(2).to_broadcast([P, P_HEADS, 16]), ALU.mult)
                    dve.tensor_scalar(j12[0], bj, 4, None, ALU.logical_shift_right)
                    chain(dve, "dve", dve.tensor_scalar(j12[1], bj, 15, None, ALU.bitwise_and))
                    for i in range(2):
                        a = dve.tensor_copy(z[:, 10752 + i * 256:11008 + i * 256], j12[i])
                    chain(dve, "dve", a)
                    sifp = z[:, 5120:5632].rearrange("p (s h f n) -> p s h f n", s=NT, h=P_HEADS, f=2)
                    pos16 = iota[:, 0:16].unsqueeze(1).to_broadcast([P, P, 16])
                    for s in range(NT):
                        for f in range(2):
                            chain(dve, "dve", dve.tensor_tensor(hot, j12f[f][:, s, :].unsqueeze(2).to_broadcast([P, P, 16]), pos16, ALU.is_equal))
                            h4 = hot.rearrange("p (h k) j -> p h k j", h=P_HEADS)
                            chain(dve, "dve", dve.tensor_tensor(h4, h4, sifp[:, s, :, f, :].unsqueeze(2).to_broadcast([P, P_HEADS, 16, 16]), ALU.mult))
                            chain(dve, "dve", dve.tensor_reduce(sel[f][:, s, :], hot, AX_X, ALU.add))
                elif name == "turn_sel":
                    for m in range(3):
                        dve.wait_ge(pe_full, f0 + m + 1)
                        dve.tensor_copy(selT[:, m, :], ps[:, m, 0:TOK])
                elif name == "spread":
                    def block_of_tokens(b, first):
                        for i in range(SB):
                            if i % 8 == 0:
                                if i >= 8 or not first:
                                    dve.wait_ge(hot_used, b * SB + (i - 8))
                                half = (i // 8) % 2
                                dve.tensor_tensor(hot2[:, half], iota[:, :].unsqueeze(1).to_broadcast([P, 8, P]),
                                                  selT[:, 1, bass.ds(b * SB + i, 8)].unsqueeze(2).to_broadcast([P, 8, P]),
                                                  ALU.is_equal).then_inc(hot_second, 1)
                            if i >= 8 or not first:
                                dve.wait_ge(hot_used, b * SB + (i - 7))
                            dve.tensor_scalar(hot1[:, i % 8, :], iota[:, :], selT[:, 0, bass.ds(b * SB + i, 1)],
                                              selT[:, 2, bass.ds(b * SB + i, 1)], ALU.is_equal, ALU.mult).then_inc(hot_made, 1)

                    block_of_tokens(0, True)
                    with dve.Fori(1, TOK // SB) as b:
                        block_of_tokens(b, False)
                elif name == "experts":
                    dve.memset(z[:, 0:4096], 0.0).then_inc(yacc_zero, 1)
                    dve.wait_ge(yacc_zero, 1)

                    def gates(g, off):
                        b = off % 2
                        dve.wait_ge(slab_full[b], g * 16 + (16 * (off // 2) + 16))
                        dve.wait_ge(hid_act, g * 2 + (off + 1))
                        hb = hid[:, b].rearrange("p i (b n) -> p i b n", n=SB)
                        dve.tensor_tensor(hb, hb, slab[:, b].rearrange("p b i n -> p i b n"), ALU.mult).then_inc(hid_step, 1)
                        dve.wait_ge(hid_step, g * 4 + (2 * off + 1))
                        dve.tensor_copy(hid_high[:, b], hid[:, b]).then_inc(hid_step, 1)
                        dve.wait_ge(hid_step, g * 4 + (2 * off + 2))
                        dve.tensor_tensor(hid_low[:, b], hid[:, b], hid_high[:, b], ALU.subtract).then_inc(hid_done, 1)

                    def next_down(g, off):
                        split_dve(dve, expert_chunk(g, off - 1, 1), range(3))
                        gates(g, off)
                        split_dve(dve, expert_chunk(g, off - 1, 1), (3,))

                    def this_up(g, off, nxt):
                        c = expert_chunk(g, off, 1)
                        for dc in range(4):
                            dve.wait_ge(piece_used[dc], place(c, 1, 1))
                            for s in range(NT):
                                y = yacc[:, s, dc * CHUNK:(dc + 1) * CHUNK]
                                a = dve.tensor_tensor(y, y, ps[:, 4 + 2 * (dc % 2) + s, :], ALU.add)
                            a.then_inc(up_read, 1)
                            if nxt is not None and dc >= 1:
                                split_dve(dve, nxt, (dc - 1,))
                        if nxt is not None:
                            split_dve(dve, nxt, (3,))

                    split_dve(dve, expert_chunk(0, 0, 0), (3,))
                    split_dve(dve, expert_chunk(0, 1, 0), range(3))
                    gates(0, 0)
                    split_dve(dve, expert_chunk(0, 1, 0), (3,))
                    next_down(0, 1)
                    this_up(0, 0, expert_chunk(0, 2, 0))
                    next_down(0, 2)
                    this_up(0, 1, expert_chunk(1, 1, 0))
                    last = GROUPS // 2 - 1
                    with dve.Fori(1, last) as g:
                        next_down(g, 1)
                        this_up(g, 0, expert_chunk(g, 2, 0))
                        next_down(g, 2)
                        this_up(g, 1, expert_chunk(g, 3, 0))
                    next_down(last, 1)
                    this_up(last, 0, expert_chunk(last, 1, 1))
                    this_up(last, 1, None)
                elif name == "final2":
                    dve.wait_ge(aux, aux_at["final2"])
                    for s in range(NT):
                        a = dve.tensor_tensor(yacc[:, s, :], yacc[:, s, :], gt, ALU.mult)
                    chain(dve, "dve", a)
                    for s in range(NT):
                        dve.tensor_tensor(ht[:, s, :], ht[:, s, :], yacc[:, s, :], ALU.add).then_inc(h_sum, 1)
                    rms_dve(dve, rms_k[n], NT, sums=rms_s[n])
                    for s in range(NT):
                        dve.scalar_tensor_tensor(ht[:, s, :], ht[:, s, :], rs[:, 64 + s:65 + s], act[:, 4096:4096 + D], ALU.mult, ALU.mult)\
                           .then_inc(out_ready, 1)
                if (name, l) == ("norm", 0):
                    dve.tensor_reduce(sel16[:, :], ident[:, :].rearrange("p (q s) -> p s q", q=4)[:, 0:16, :], AX_X, ALU.add)
                if name in ("turn_in", "turn_ctx"):
                    dve.memset(part_rows, 0.0)
                if (name, l) == ("turn_in", 0):
                    dve.wait_ge(small, 16 * 5)
                    pos, inv = st[:, 80:82], zs[:, 0:32]
                    chain(dve, "dve", dve.tensor_copy(pos, sti[:, 0:NT]))
                    for s in range(NT):
                        a = dve.tensor_scalar(zs[:, 32 + s * 32:64 + s * 32], inv, pos[:, s:s + 1], None, ALU.mult)
                    chain(dve, "dve", a)
                    ang, turns, r = zs[:, 32:96], zs[:, 96:160], zs[:, 128:192]
                    turns = zs[:, 256:320]
                    chain(dve, "dve", dve.tensor_scalar(turns, ang, float(np.float32(1 / TWO_PI)), 12582912.0, ALU.mult, ALU.add))
                    chain(dve, "dve", dve.tensor_scalar(turns, turns, 12582912.0, None, ALU.subtract))
                    c1 = 6.28125
                    c2 = float(np.float32(np.round((TWO_PI - c1) * 2 ** 20) / 2 ** 20))
                    c3 = float(np.float32(TWO_PI - c1 - c2))
                    prev = ang
                    for cc in (c1, c2, c3):
                        chain(dve, "dve", dve.scalar_tensor_tensor(r, turns, -cc, prev, ALU.mult, ALU.add))
                        prev = r
                    pi = float(np.nextafter(np.float32(np.pi), np.float32(0)))
                    chain(dve, "dve", dve.tensor_scalar(r, r, pi, -pi, ALU.min, ALU.max))
                    c = zs[:, 192:256]
                    chain(dve, "dve", dve.scalar_tensor_tensor(c, r, -1.0, r, ALU.mult, ALU.max))
                    dve.tensor_scalar(c, c, -1.0, float(np.float32(np.pi / 2)), ALU.mult, ALU.add)
                    lam = zs[:, 512:1024].rearrange("p (k l n) -> p k l n", k=4, l=DEPTH)
                    for ly in range(DEPTH):
                        for pr in range(2):
                            k = 2 * ly + pr
                            dve.tensor_tensor_reduce(zs[:, 1024 + k * 64:][:, 0:64], lam[:, 2 * pr, ly, :], lam[:, 2 * pr + 1, ly, :],
                                                     1.0, 0.0, ALU.mult, ALU.add, st[:, 68 + k:69 + k])
                elif (name, l) == ("split_in", 0):
                    dve.memset(mod_rows, 0.0)
                elif (name, l) == ("prep_a", 0):
                    e = st[:, 64:68].rearrange("p (l k) -> p l k", k=2)
                    chain(dve, "dve", dve.tensor_tensor(st[:, 60:62], e[:, :, 1], e[:, :, 0], ALU.subtract))
                    for ly in range(DEPTH):
                        init = 0.8 - 0.6 * float(np.exp(-0.3 * ly))
                        dve.tensor_scalar(st[:, 60 + ly:61 + ly], st[:, 60 + ly:61 + ly], -init, None, ALU.add)
                        dve.tensor_scalar(bc[:, B_SUB + ly * HD:][:, 0:HD], bc[:, B_SUB + ly * HD:][:, 0:HD], 1.0 - init, None, ALU.mult)
                if ADA_OF.get((name, l), 0) >= 1:
                    ada_dve(dve, ADA_OF[name, l] - 1, ada_bank(name)[1])
                after = PRE_SPLIT.get((name, l))
                if after:
                    split_dve(dve, (0, 2 * PAIR0[after], ADA_BEFORE[after]), range(3))
                end(dve, "dve")


def pack_chunks(w):
    n = w.shape[1] // CHUNK
    return w.reshape(4, PIECE_KT, P, n, CHUNK).transpose(3, 0, 2, 1, 4).reshape(n, 4, P, PIECE)


def lay_out(i):
    f32 = np.float32
    w0 = KI0 + IDX_DIM
    order = np.concatenate([np.arange(w0), np.arange(w0 + IDX_HEADS, ZW), np.arange(w0, w0 + IDX_HEADS)])
    parts, ada = [], pack_chunks(i["w_ada_2"][0])

    def ada_before(name):
        return [ada[a:a + 1] for a in range(ADA_CHUNKS) if ADA_NEXT[a] == name]

    for l in range(DEPTH):
        for name, w in ((f"in{l}", i["w_in"][l][:, order[:WI0]]), (f"out{l}", i["w_o"][l]), (f"gate{l}", i["w_pg"][l])):
            parts += ada_before(name) + [pack_chunks(w)]
    parts += ada_before("kv")
    w2 = i["w_in_2"][0]
    rq, rk, rv, rg = w2[:, 0:512], w2[:, 512:1024], w2[:, 1024:2048], w2[:, 2048:3072]
    mq, mk, mv, mo = w2[:, 3072:3584], w2[:, 3584:4096], w2[:, 4096:5120], w2[:, 5120:6144]
    wg, gr, gm = w2[:, 6144:6160], w2[:, 6160:6160 + D], w2[:, 6160 + D:6160 + 2 * D]
    for w in (rk, rv, mv, mk, mq, rq, rg, mo):
        parts.append(pack_chunks(w))
    outs = np.concatenate([i["w_ret_out_2"][0], i["w_mlstm_out_2"][0]])
    merge = np.stack([pack_chunks(w) for w in (gr, gm, outs)], axis=1)
    parts += [merge.reshape(-1, 4, P, PIECE), pack_chunks(i["w_out_2"][0]), pack_chunks(i["peer_query_2"][0])]
    down = i["peer_down_2"][0].reshape(P_KEYS, GROUPS, 4, 4, PIECE_KT, P).transpose(1, 3, 5, 4, 2, 0)
    up = i["peer_up_2"][0].reshape(P_KEYS, GROUPS, 4, 4, CHUNK).transpose(1, 3, 0, 2, 4).reshape(GROUPS, 4, P, PIECE)
    experts = np.empty((GROUPS, 2, 4, P, PIECE), f32)
    experts[:, 0] = down.reshape(GROUPS, 4, P, PIECE)
    experts[:, 1] = up
    parts += [experts[0:1, 0], np.stack([experts[1:, 0], experts[:-1, 1]], axis=1).reshape(-1, 4, P, PIECE), experts[-1:, 1]]
    stream = np.concatenate(parts)

    def columns(v):
        return v.reshape(-1, P).T

    cols = np.concatenate([columns(i["norm_g"]), columns(i["q_norm_g"]), columns(i["kv_norm_g"]), columns(i["norm1_g_2"]),
                           columns(i["norm2_g_2"]), columns(i["m_conv_2"][0]),
                           np.stack([columns(i["c_2"][0]), columns(i["c_ctx_2"])], axis=2).reshape(P, 2 * KT)], axis=1)
    bc = np.concatenate([i["subln_g"].reshape(-1), i["m_gate_bias_2"][0].reshape(-1), i["ret_decay_2"][0].reshape(-1)])
    tail = i["w_in"][:, :, w0:w0 + IDX_HEADS].reshape(DEPTH, KT, P, IDX_HEADS).transpose(2, 0, 1, 3).reshape(P, -1)
    wg = wg.reshape(KT, P, 16).transpose(1, 0, 2).reshape(P, -1)
    nope = [np.arange(h * (HD + A_ROPE), h * (HD + A_ROPE) + HD) for h in range(A_HEADS)]
    rot = [np.arange(h * (HD + A_ROPE) + HD, (h + 1) * (HD + A_ROPE)) for h in range(A_HEADS)]
    key = [np.arange(h * 2 * HD, h * 2 * HD + HD) for h in range(A_HEADS)]
    val = [np.arange(h * 2 * HD + HD, (h + 1) * 2 * HD) for h in range(A_HEADS)]
    inv_freq = (1.0 / (f32(500000.0) ** (np.arange(32, dtype=f32) * f32(2.0 / 64)))).astype(f32)
    freq = (f32(10000.0) ** (-np.arange(16, dtype=f32) / f32(16))).astype(f32)
    tok = np.arange(TOK)
    ang = np.concatenate([(tok // 64)[:, None].astype(f32) * freq, (tok % 64)[:, None].astype(f32) * freq], axis=1)
    trig2 = np.stack([np.cos(ang), np.sin(ang)]).reshape(2, NT, P, 32).transpose(2, 0, 1, 3).astype(f32)
    s, c = tok[:, None], tok[None, :]
    far = 1e30
    dist = np.stack([np.concatenate([TOK + c - s, np.where(c >= s, c - s, far)]),
                     np.concatenate([TOK - c + s, np.where(s >= c, s - c, far)])])
    dist = dist.reshape(2, 4, P, TOK).transpose(2, 0, 1, 3).reshape(P, -1).astype(f32)
    return dict(
        x=i["x"][0], positions=i["positions"][0].reshape(NT, P).T, cols=cols, bc=bc,
        wtail=tail, inv_freq=inv_freq,
        lam=np.concatenate([i[k].reshape(-1) for k in ("lam_q1", "lam_k1", "lam_q2", "lam_k2")]),
        w_uq=i["w_uq"][:, :, np.concatenate(nope + rot)], w_ukv=i["w_ukv"][:, :, np.concatenate(key + val)],
        w_ple=i["w_ple"], pT=i["p"][:, 0].transpose(0, 2, 1), final_g=i["final_g"], trig2=trig2,
        ctx=i["ctx_2"][0], wgates=wg.reshape(P, KT, 16), dist=dist, b_ada=columns(i["b_ada_2"][0]),
        keysT=i["peer_keys_2"][0].reshape(16, P_KEYS, P).transpose(2, 0, 1).reshape(P, -1), final_g2=i["final_g_2"],
        stream=stream)


def kernel(**inputs):
    import concourse.bacc as bacc
    from concourse.bass_utils import run_bass_kernel_spmd

    laid = {k: np.ascontiguousarray(v) for k, v in lay_out({k: np.asarray(v) for k, v in inputs.items()}).items()}
    nc = bacc.Bacc("TRN2", target_bir_lowering=False, num_devices=1)
    arrays, t = {}, {}
    for name, a in laid.items():
        arrays[f"in_{name}_dram"] = a
        t[name] = nc.dram_tensor(f"in_{name}_dram", a.shape, mybir.dt.from_np(a.dtype), kind="ExternalInput").ap()
    t["out"] = nc.dram_tensor("out_0_dram", (TOK, D), F32, kind="ExternalOutput").ap()
    build_program(nc, t)
    r = run_bass_kernel_spmd(nc, [arrays], core_ids=[0])
    return r.results[0]["out_0_dram"].reshape(1, TOK, D)
```
